# Optimizing a Trainium2 kernel written in Bass

```python
import math
import jax, jax.numpy as jnp
from jax import lax
import numpy as np

D_MODEL = 1024
BATCH = 1
SEQ = 256
DEPTH = 2
DEC_BATCH = 8
DEC_SEQ = 4
PAST_LEN = 2048
PAGE_SIZE = 128

D_MIX = D_MODEL
W_A = D_MIX // 4
NH_A = 4
HD_A = W_A // NH_A
CONV_A = 4
LRU_C = 8.0
W_B = D_MIX // 4
CONV_B = 31
W_C = D_MIX // 2
NH_C = 8
HD_C = W_C // NH_C
RET_CHUNK = 128
ROPE_BASE = 10000.0
N_GROUPS = 4
EXPERTS_PER_GROUP = 8
N_EXPERTS = N_GROUPS * EXPERTS_PER_GROUP
TOP_K = 2
D_EXPERT = D_MODEL // 4
D_IN = 2 * W_A + 2 * W_B + 4 * W_C
EPS = 1e-6

kernel_name = "hymba_style_lru_conv_retention_hmoe_step"

def rmsnorm(x, g):
    xf = x.astype(jnp.float32)
    y = xf * lax.rsqrt(jnp.mean(xf * xf, axis=-1, keepdims=True) + EPS)
    return (y * g.astype(jnp.float32)).astype(x.dtype)

def layernorm_f32(x, g, b):
    mu = jnp.mean(x, axis=-1, keepdims=True)
    xc = x - mu
    var = jnp.mean(xc * xc, axis=-1, keepdims=True)
    return xc * lax.rsqrt(var + EPS) * g.astype(jnp.float32) + b.astype(jnp.float32)

def causal_dwconv(x, buf, w, b):
    xp = jnp.concatenate([buf.astype(x.dtype), x], axis=1)
    y = lax.conv_general_dilated(xp, w[:, None, :].astype(x.dtype), window_strides=(1,), padding='VALID',
                                 dimension_numbers=('NWC', 'WIO', 'NWC'), feature_group_count=x.shape[-1])
    return y + b.astype(x.dtype), xp[:, -(w.shape[0] - 1):]

def rglru(xc, h0, wa, ba, wx, bx, lam):
    B, T, W = xc.shape
    xf = xc.astype(jnp.float32)
    xh = xf.reshape(B, T, NH_A, HD_A)
    r = jax.nn.sigmoid(jnp.einsum('bthi,hij->bthj', xh, wa.astype(jnp.float32)).reshape(B, T, W) + ba.astype(jnp.float32))
    i = jax.nn.sigmoid(jnp.einsum('bthi,hij->bthj', xh, wx.astype(jnp.float32)).reshape(B, T, W) + bx.astype(jnp.float32))
    log_a = -LRU_C * r * jax.nn.softplus(-lam.astype(jnp.float32))
    a = jnp.exp(log_a)
    bterm = jnp.sqrt(-jnp.expm1(2.0 * log_a)) * (i * xf)
    bterm = bterm.at[:, 0].add(a[:, 0] * h0.astype(jnp.float32))

    def combine(c1, c2):
        a1, b1 = c1
        a2, b2 = c2
        return a1 * a2, a2 * b1 + b2

    _, h = lax.associative_scan(combine, (a, bterm), axis=1)
    return h, h[:, -1]

def rope(x, pos):
    half = x.shape[-1] // 2
    inv = ROPE_BASE ** (-jnp.arange(half, dtype=jnp.float32) / half)
    ang = pos.astype(jnp.float32)[:, None] * inv[None, :]
    cos = jnp.cos(ang)[None, :, None, :]
    sin = jnp.sin(ang)[None, :, None, :]
    x1, x2 = x[..., :half], x[..., half:]
    return jnp.concatenate([x1 * cos - x2 * sin, x1 * sin + x2 * cos], axis=-1)

def retention(q, k, v, S0, chunk):
    B, T, H, D = q.shape
    N = T // chunk
    log_g = jnp.log1p(-jnp.exp2(-5.0 - jnp.arange(H, dtype=jnp.float32)))
    idx = jnp.arange(chunk, dtype=jnp.float32)
    diff = idx[:, None] - idx[None, :]
    causal = diff >= 0
    dmat = jnp.where(causal[None], jnp.exp(jnp.where(causal, diff, 0.0)[None] * log_g[:, None, None]), 0.0)
    xi = jnp.exp((idx + 1.0)[None, :] * log_g[:, None])
    zeta = jnp.exp((chunk - 1.0 - idx)[None, :] * log_g[:, None])
    g_chunk = jnp.exp(chunk * log_g)

    def to_chunks(t):
        return t.reshape(B, N, chunk, H, D).transpose(1, 0, 3, 2, 4)

    def step(S, qkv):
        qc, kc, vc = qkv
        inner = jnp.einsum('bhid,bhjd->bhij', qc, kc) * dmat
        o = jnp.einsum('bhij,bhjd->bhid', inner, vc) + jnp.einsum('bhid,bhde->bhie', qc, S) * xi[None, :, :, None]
        S_new = g_chunk[None, :, None, None] * S + jnp.einsum('bhjd,bhje->bhde', kc * zeta[None, :, :, None], vc)
        return S_new, o

    S_last, o = lax.scan(step, S0.astype(jnp.float32), (to_chunks(q), to_chunks(k), to_chunks(v)))
    o = o.transpose(1, 0, 3, 2, 4).reshape(B, T, H, D)
    return o, S_last

def hier_moe(x, wg, bg, we, be, w1, w3, w2):
    B, T, D = x.shape
    xt = x.reshape(B * T, D)
    xf = xt.astype(jnp.float32)
    pg = jax.nn.softmax(xf @ wg.astype(jnp.float32) + bg.astype(jnp.float32), axis=-1)
    g_sel = jnp.argmax(pg, axis=-1)
    p_top = jnp.take_along_axis(pg, g_sel[:, None], axis=-1)
    le = (xf @ we.astype(jnp.float32) + be.astype(jnp.float32)).reshape(-1, N_GROUPS, EXPERTS_PER_GROUP)
    le_sel = jnp.take_along_axis(le, g_sel[:, None, None], axis=1)[:, 0]
    top_v, top_i = lax.top_k(le_sel, TOP_K)
    pe = jax.nn.softmax(top_v, axis=-1)
    eid = g_sel[:, None] * EXPERTS_PER_GROUP + top_i
    gates = jnp.sum(jax.nn.one_hot(eid, N_EXPERTS, dtype=jnp.float32) * (p_top * pe)[..., None], axis=1)

    def expert(acc, params):
        w1e, w3e, w2e, ge = params
        h = jax.nn.silu(xt @ w1e) * (xt @ w3e)
        return acc + ge[:, None] * (h @ w2e).astype(jnp.float32), None

    y, _ = lax.scan(expert, jnp.zeros((B * T, D), jnp.float32), (w1, w3, w2, gates.T))
    return y.astype(x.dtype).reshape(B, T, D)

def setup_inputs(seed: int = 0) -> dict:
    key = jax.random.key(seed)
    ks = jax.random.split(key, 40)
    nrm = lambda k, shape, s: jax.random.normal(k, shape, jnp.float32) * s
    a0 = jax.random.uniform(ks[14], (DEPTH, W_A), jnp.float32, 0.9, 0.999)
    return {
        "x_prompt": nrm(ks[0], (BATCH, SEQ, D_MODEL), 1.0),
        "x_sample": nrm(ks[1], (DEC_BATCH, DEC_SEQ, D_MODEL), 1.0),
        "state_lru_h": nrm(ks[2], (DEPTH, DEC_BATCH, W_A), 0.5),
        "state_lru_conv": nrm(ks[3], (DEPTH, DEC_BATCH, CONV_A - 1, W_A), 1.0),
        "state_conv": nrm(ks[4], (DEPTH, DEC_BATCH, CONV_B - 1, W_B), 0.5),
        "state_ret": nrm(ks[5], (DEPTH, DEC_BATCH, NH_C, HD_C, HD_C), 2.0),
        "norm_mix_g": 1.0 + nrm(ks[6], (DEPTH, D_MODEL), 0.01),
        "norm_ffn_g": 1.0 + nrm(ks[7], (DEPTH, D_MODEL), 0.01),
        "final_norm_g": 1.0 + nrm(ks[8], (D_MODEL,), 0.01),
        "w_in": nrm(ks[9], (DEPTH, D_MODEL, D_IN), D_MODEL ** -0.5),
        "lru_conv_w": nrm(ks[10], (DEPTH, CONV_A, W_A), CONV_A ** -0.5),
        "lru_conv_b": nrm(ks[11], (DEPTH, W_A), 0.02),
        "lru_wa": nrm(ks[12], (DEPTH, NH_A, HD_A, HD_A), HD_A ** -0.5),
        "lru_ba": nrm(ks[13], (DEPTH, W_A), 0.1),
        "lru_wx": nrm(ks[15], (DEPTH, NH_A, HD_A, HD_A), HD_A ** -0.5),
        "lru_bx": nrm(ks[16], (DEPTH, W_A), 0.1),
        "lru_lambda": jnp.log(a0) - jnp.log1p(-a0),
        "cm_dw_w": nrm(ks[17], (DEPTH, CONV_B, W_B), CONV_B ** -0.5),
        "cm_dw_b": nrm(ks[18], (DEPTH, W_B), 0.02),
        "cm_ln_g": 1.0 + nrm(ks[19], (DEPTH, W_B), 0.01),
        "cm_ln_b": nrm(ks[20], (DEPTH, W_B), 0.02),
        "ret_norm_g": 1.0 + nrm(ks[21], (DEPTH, W_C), 0.01),
        "w_out": nrm(ks[22], (DEPTH, D_MIX, D_MODEL), D_MIX ** -0.5),
        "moe_w_group": nrm(ks[23], (DEPTH, D_MODEL, N_GROUPS), D_MODEL ** -0.5),
        "moe_b_group": nrm(ks[24], (DEPTH, N_GROUPS), 0.01),
        "moe_w_expert": nrm(ks[25], (DEPTH, D_MODEL, N_EXPERTS), D_MODEL ** -0.5),
        "moe_b_expert": nrm(ks[26], (DEPTH, N_EXPERTS), 0.01),
        "moe_w1": nrm(ks[27], (DEPTH, N_EXPERTS, D_MODEL, D_EXPERT), D_MODEL ** -0.5),
        "moe_w3": nrm(ks[28], (DEPTH, N_EXPERTS, D_MODEL, D_EXPERT), D_MODEL ** -0.5),
        "moe_w2": nrm(ks[29], (DEPTH, N_EXPERTS, D_EXPERT, D_MODEL), D_EXPERT ** -0.5),
    }

def reference(x_prompt, x_sample, state_lru_h, state_lru_conv, state_conv, state_ret,
              norm_mix_g, norm_ffn_g, final_norm_g, w_in, lru_conv_w, lru_conv_b,
              lru_wa, lru_ba, lru_wx, lru_bx, lru_lambda, cm_dw_w, cm_dw_b, cm_ln_g, cm_ln_b,
              ret_norm_g, w_out, moe_w_group, moe_b_group, moe_w_expert, moe_b_expert,
              moe_w1, moe_w3, moe_w2):
    splits = [W_A, 2 * W_A, 2 * W_A + 2 * W_B, 2 * W_A + 2 * W_B + W_C,
              2 * W_A + 2 * W_B + 2 * W_C, 2 * W_A + 2 * W_B + 3 * W_C]

    def layer(x, h0, buf_a, buf_b, S0, pos, l):
        Bn, T, _ = x.shape
        u = rmsnorm(x, norm_mix_g[l])
        proj = u @ w_in[l]
        a_gate, a_x, b_in, c_q, c_k, c_v, c_g = jnp.split(proj, splits, axis=-1)
        xa, nbuf_a = causal_dwconv(a_x, buf_a, lru_conv_w[l], lru_conv_b[l])
        ha, h_last = rglru(xa, h0, lru_wa[l], lru_ba[l], lru_wx[l], lru_bx[l], lru_lambda[l])
        out_a = jax.nn.gelu(a_gate.astype(jnp.float32)) * ha
        glu = b_in[..., :W_B] * jax.nn.sigmoid(b_in[..., W_B:])
        cb, nbuf_b = causal_dwconv(glu, buf_b, cm_dw_w[l], cm_dw_b[l])
        out_b = jax.nn.silu(layernorm_f32(cb.astype(jnp.float32), cm_ln_g[l], cm_ln_b[l]))
        q = rope(c_q.reshape(Bn, T, NH_C, HD_C).astype(jnp.float32), pos)
        k = rope(c_k.reshape(Bn, T, NH_C, HD_C).astype(jnp.float32), pos) * (HD_C ** -0.5)
        v = c_v.reshape(Bn, T, NH_C, HD_C).astype(jnp.float32)
        o, S_last = retention(q, k, v, S0, math.gcd(T, RET_CHUNK))
        mu = jnp.mean(o, axis=-1, keepdims=True)
        oc = o - mu
        o = oc * lax.rsqrt(jnp.mean(oc * oc, axis=-1, keepdims=True) + EPS)
        o = o.reshape(Bn, T, W_C) * ret_norm_g[l].astype(jnp.float32)
        out_c = jax.nn.silu(c_g.astype(jnp.float32)) * o
        mix = jnp.concatenate([out_a, out_b, out_c], axis=-1).astype(x.dtype) @ w_out[l]
        x = x + mix
        x = x + hier_moe(rmsnorm(x, norm_ffn_g[l]), moe_w_group[l], moe_b_group[l], moe_w_expert[l],
                         moe_b_expert[l], moe_w1[l], moe_w3[l], moe_w2[l])
        return x, h_last, nbuf_a, nbuf_b, S_last

    Bp, Tp, _ = x_prompt.shape
    Bs, Ts, _ = x_sample.shape
    pos_p = jnp.arange(Tp, dtype=jnp.int32)
    pos_s = PAST_LEN + jnp.arange(Ts, dtype=jnp.int32)
    xp, xs = x_prompt, x_sample
    p_h, p_ca, p_cb, p_S = [], [], [], []
    s_h, s_ca, s_cb, s_S = [], [], [], []
    for l in range(DEPTH):
        xp, h, ca, cb, S = layer(xp, jnp.zeros((Bp, W_A), jnp.float32),
                                 jnp.zeros((Bp, CONV_A - 1, W_A), xp.dtype),
                                 jnp.zeros((Bp, CONV_B - 1, W_B), xp.dtype),
                                 jnp.zeros((Bp, NH_C, HD_C, HD_C), jnp.float32), pos_p, l)
        p_h.append(h); p_ca.append(ca); p_cb.append(cb); p_S.append(S)
        xs, h, ca, cb, S = layer(xs, state_lru_h[l], state_lru_conv[l], state_conv[l], state_ret[l], pos_s, l)
        s_h.append(h); s_ca.append(ca); s_cb.append(cb); s_S.append(S)
    y_prompt = rmsnorm(xp, final_norm_g)
    y_sample = rmsnorm(xs, final_norm_g)
    return (y_prompt, y_sample,
            jnp.stack(p_h), jnp.stack(p_ca), jnp.stack(p_cb), jnp.stack(p_S),
            jnp.stack(s_h), jnp.stack(s_ca), jnp.stack(s_cb), jnp.stack(s_S))


_drawn_inputs = setup_inputs


def setup_inputs(seed=0):
    import zlib

    import numpy as np

    out = dict(_drawn_inputs(seed))
    spreads = {}
    factors = {'final_norm_g': 200.0,
     'cm_ln_g': 49.094,
     'ret_norm_g': 41.504,
     'cm_ln_b': 23.281,
     'moe_b_group': 35.09,
     'moe_b_expert': 21.832,
     'norm_ffn_g': 7.857,
     'lru_ba': 2.811}
    for name, (base, spread) in spreads.items():
        noise = np.random.default_rng([zlib.crc32(name.encode()), seed]).standard_normal(out[name].shape)
        drawn = base * np.exp(spread * noise) if base else spread * noise
        out[name] = __import__('jax').numpy.asarray(drawn.astype(out[name].dtype))
    for name, factor in factors.items():
        out[name] = (out[name] * factor).astype(out[name].dtype)
    return out
```

```python
from contextlib import ExitStack

import numpy as np

import concourse.bass as bass
from concourse import mybir

F32 = mybir.dt.float32
BF16 = mybir.dt.bfloat16
U32 = mybir.dt.uint32
I32 = mybir.dt.int32
ALU = mybir.AluOpType
ACT = mybir.ActivationFunctionType
AX = mybir.AxisListType.X

DEPTH, D, SEQ, NB, DT = 2, 1024, 256, 8, 4
NT = SEQ + NB * DT
TILES = [(0, 128), (128, 128), (256, 32)]
KT = D // 128
W_A = W_B = 256
CONV_A, CONV_B = 4, 31
NH, HD = 8, 64
NG, EPG = 4, 8
NE = NG * EPG
FE = 256
EPS = 1e-6
PAST = 2048
SLOTS = 64
OVER = 8
NBLK = NE + OVER
NSLOT = NBLK * SLOTS
EMPTY = 1.0e6
BIG = 1.0e30
LA, LS = 3 + SEQ, 3 + DT
LB, LT = 30 + SEQ, 30 + DT
SCAN = SEQ + NB * (DT + 1)

PARAMS = [("cw", CONV_A * 2), ("cb", 2), ("ba", 2), ("bx", 2), ("lam", 2), ("dw", CONV_B * 2),
          ("db", 2), ("lg", 2), ("lb", 2), ("rg", 4)]
PCOL, _n = {}, 0
for _name, _k in PARAMS:
    PCOL[_name] = _n
    _n += _k
NPRM = _n

CONSTS = [("ident", 128), ("upper", 128), ("dmat", 1024), ("dmats", 256), ("xi", 8), ("zeta", 8),
          ("zetas", 8), ("gch", 4), ("gst", 4), ("cmask", 16), ("vmask", 8), ("cos", 96),
          ("sin", 96), ("iota", 32), ("e64", 32), ("ovc", 32),
          ("thr", 4), ("iotaj", 8), ("desc", 4), ("vals", 12), ("half", 1)]
CCOL, _n = {}, 0
for _name, _k in CONSTS:
    CCOL[_name] = (_n, _k)
    _n += _k
NCONST = _n


def constants():
    c = np.zeros((128, NCONST), np.float32)

    def put(name, a, rows=128):
        o, k = CCOL[name]
        c[:rows, o:o + k] = np.asarray(a, np.float64).reshape(rows, k).astype(np.float32)

    p = np.arange(128)
    g = 1.0 - 2.0 ** (-5.0 - np.arange(NH))
    heads = np.arange(NH).reshape(4, 2).T
    scale = HD ** -0.5
    put("ident", np.eye(128))
    put("upper", p[:, None] < p[None, :])
    diff = p[None, :] - p[:, None]
    put("dmat", scale * np.where(diff[:, None, None, :] >= 0,
                         g[heads][None, :, :, None] ** np.maximum(diff, 0)[:, None, None, :], 0.0))
    s = np.arange(32)
    ds = s[None, :] - s[:, None]
    same = (s[None, :] // DT == s[:, None] // DT) & (ds >= 0)
    put("dmats", scale * np.where(same[:, None, None, :],
                          g[heads][None, :, :, None] ** np.maximum(ds, 0)[:, None, None, :], 0.0), 32)
    put("xi", g[None, :] ** (p[:, None] + 1))
    put("zeta", scale * g[None, :] ** (127 - p[:, None]))
    put("zetas", scale * g[None, :] ** (DT - 1 - s[:, None] % DT), 32)
    par, m4 = (p // 64)[:, None], np.arange(4)[None, :]
    put("gch", g[2 * m4 + par] ** 128)
    put("gst", g[2 * m4 + par] ** DT)
    m, tok = p // 32, p % 32
    cm = np.zeros((128, 2, NB))
    for q in range(2):
        cm[p, q, tok // DT] = g[2 * m + q] ** (tok % DT + 1)
    put("cmask", cm)
    put("vmask", s[:, None] // DT == np.arange(NB)[None, :], 32)
    half = HD // 2
    inv = (np.float32(10000.0) ** (-np.arange(half, dtype=np.float32) / np.float32(half))).astype(np.float32)
    pos = np.zeros((128, 3), np.float32)
    pos[:, 0], pos[:, 1] = p, p + 128
    pos[:32, 2] = PAST + s % DT
    ang = (pos[:, :, None] * inv[None, None, :]).astype(np.float32).astype(np.float64)
    put("cos", np.cos(ang))
    put("sin", np.sin(ang))
    e = np.arange(NE)
    put("iota", np.tile(e, (128, 1)))
    put("e64", np.tile(SLOTS * e, (128, 1)))
    put("ovc", np.tile(SLOTS * (NE - 1 - e), (128, 1)))
    put("thr", np.tile(SLOTS * (1 + np.arange(4)), (128, 1)))
    put("iotaj", np.tile(np.arange(OVER), (128, 1)))
    put("desc", np.tile(NG - np.arange(NG), (128, 1)))
    vals = np.zeros((128, 3, 2, 2))
    tokid = p[:, None] + 128 * np.arange(3)[None, :]
    for k in range(2):
        vals[:, :, k, 0] = tokid
        vals[:, :, k, 1] = 2 * tokid + k
    put("vals", vals)
    put("half", p // 64)
    return c


def bank_plan():
    jobs = [("sa", 7), ("sc", 6)]
    norm = [("t0a", 0), ("t0b", 1), ("t1a", 2), ("t1b", 3), ("t2a", 0)]
    jobs += [("n1" + n, b) for n, b in norm]
    jobs += [(f"b{c}", 4 + c % 4) for c in range(8)]
    jobs += [("q0", 0), ("k0", 1), ("q1", 2), ("k1", 3), ("qk2", 4)]
    jobs += [("gr0", 7), ("tq0", 5), ("gi0", 7), ("tk0", 6), ("v0", 0), ("gr1", 7), ("tq1", 5),
             ("gi1", 7), ("tk1", 6), ("g0", 1), ("tq2", 5), ("tk2", 6), ("v1", 2), ("g1", 3), ("vg2", 4)]
    jobs += [("st", 7), ("lnm", 5), ("in0e", 0), ("in0o", 1), ("in1e", 2), ("in1o", 3), ("S0", 7),
             ("lnv", 6), ("o0", 4), ("ht", 5), ("x1e", 0), ("x1o", 1), ("o1", 2), ("S1", 7),
             ("inse", 5), ("inso", 6), ("xse", 5), ("xso", 6), ("os", 3),
             ("su0", 0), ("su1", 1), ("su2", 2), ("su3", 4), ("to0", 7), ("to1", 5), ("to2", 6)]
    jobs += [(f"w{q}{t}", (2 * q + t) % 8) for q in range(4) for t in range(2)] + [("w2", 0)]
    jobs += [("n2" + n, b) for n, b in norm]
    jobs += [("lgT", 4), ("lg", 5), ("cum", 6), ("tabg", 4), ("tabs", 5)]
    return jobs


GROUPS = NE // 4
BANK, PER_BANK = {}, [0] * 8
for _name, _b in bank_plan():
    assert _name not in BANK
    BANK[_name] = (_b, PER_BANK[_b])
    PER_BANK[_b] += 1
EXPERT_BASE = list(PER_BANK)
EXPERT_TURN = [2] * 8
PER_BANK = [n + GROUPS * k for n, k in zip(PER_BANK, EXPERT_TURN)]

OUTS = [(SEQ, D), (NB * DT, D), (DEPTH, 1, W_A), (DEPTH, 1, CONV_A - 1, W_A), (DEPTH, 1, CONV_B - 1, W_B),
        (DEPTH, 1, NH, HD, HD), (DEPTH, NB, W_A), (DEPTH, NB, CONV_A - 1, W_A),
        (DEPTH, NB, CONV_B - 1, W_B), (DEPTH, NB, NH, HD, HD)]


class Own:

    def __init__(self, eng, sem):
        self.eng, self.sem, self.n = eng, sem, 0

    def __call__(self, ins):
        ins.then_inc(self.sem, 1)
        self.n += 1
        return self.n

    def wait(self, n=None):
        self.eng.wait_ge(self.sem, self.n if n is None else n)


def build(nc, ins, outs):
    (x_prompt, x_sample, st_lru_h, st_lru_conv, st_conv, st_ret, g_mix, g_ffn, g_fin, w_in, p_cw, p_cb,
     w_a, p_ba, w_x, p_bx, p_lam, p_dw, p_db, p_lg, p_lb, p_rg, w_out, w_grp, b_grp, w_exp, b_exp,
     w1, w3, w2, cst) = ins
    (y_prompt, y_sample, o_lru_h, o_lru_conv, o_conv, o_ret, s_lru_h, s_lru_conv, s_conv, s_ret) = outs
    params = [(p_cw, "cw"), (p_cb, "cb"), (p_ba, "ba"), (p_bx, "bx"), (p_lam, "lam"), (p_dw, "dw"),
              (p_db, "db"), (p_lg, "lg"), (p_lb, "lb"), (p_rg, "rg")]

    xn_dram = nc.dram_tensor("xn_scratch", (NT, D), F32, kind="Internal").ap()
    y_dram = nc.dram_tensor("y_scratch", (NT * 4, D // 2), F32, kind="Internal").ap()
    tab_dram = [nc.dram_tensor(f"slot_table{l}", (NSLOT, 2), F32, kind="Internal").ap() for l in range(DEPTH)]

    with ExitStack() as ctx:
        def sb(name, shape, dt=F32):
            return ctx.enter_context(nc.sbuf_tensor(name, shape, dt))

        def sem(name):
            return ctx.enter_context(nc.semaphore(name))

        ring = sb("ring", [128, 12, 2048])
        x = sb("x", [128, 3, D])
        uT = sb("uT", [128, KT * NT])
        mixT = sb("mixT", [128, KT, NT])
        rows = sb("rows", [128, 2, D])
        arena = sb("arena", [128, 4096])
        const = sb("const", [128, NCONST])
        qT = sb("qT", [128, 4, NT])
        kT = sb("kT", [128, 4, NT])
        kr = sb("kr", [128, 3, 512])
        v = sb("v", [128, 3, 512])
        sg = sb("sg", [128, 3, 512])
        axp = sb("axp", [128, 2, LA])
        axs = sb("axs", [128, 2, NB, LS])
        glp = sb("glp", [128, 2, LB])
        gls = sb("gls", [128, 2, NB, LT])
        cb = sb("cb", [128, 2 * NT])
        xc = sb("xc", [128, 2 * NT])
        rs = sb("rs", [128, NT])
        tt = sb("tt", [128, 2, 512])
        S1 = sb("S1", [128, 4, HD])
        bd = sb("bd", [128, 2, 2, 128])
        prm = sb("prm", [128, DEPTH, NPRM])
        wr = sb("wr", [128, KT, NG + NE])
        gmx = sb("gmx", [128, DEPTH, KT])
        gff = sb("gff", [128, DEPTH, KT])
        lbias = sb("lbias", [NG + NE, DEPTH])
        ones = sb("ones", [128, 128])
        onesb = sb("onesb", [128, 128], BF16)
        upb = sb("upb", [128, 128], BF16)
        ssq = sb("ssq", [128, 3])
        rms = sb("rms", [128, 3])
        rec = sb("rec", [128, 3])
        eps = sb("eps", [128, 1])
        st_mu = sb("st_mu", [128, NH])
        st_va = sb("st_va", [128, NH])
        hst = sb("hst", [128, 2, 9])
        osumb = sb("osumb", [128, 3, NE], BF16)

        psum = ctx.enter_context(nc.psum_tensor("psum", [128, 8, 512], F32))

        uTk = uT[:, :].rearrange("p (k t) -> p k t", k=KT)
        w_out3 = uT[:, 0:2048].rearrange("p (k c) -> p k c", k=KT)

        def C(name, n=128):
            o, k = CCOL[name]
            return const[0:n, o:o + k]

        def P_(l, name, i):
            return prm[:, l, PCOL[name] + i:PCOL[name] + i + 1]

        AG, XA = arena[:, 0:576], arena[:, 576:1152]
        RG, RI = arena[:, 1152:1728], arena[:, 1744:2320]
        IG = arena[:, 2320:2896]
        HS = arena[:, 1152:1744].rearrange("p (c n) -> p c n", c=2)
        As = arena[:, 2896:3488].rearrange("p (c n) -> p c n", c=2)
        Bs = arena[:, 3488:4080].rearrange("p (c n) -> p c n", c=2)
        S0 = arena[:, 0:2048].rearrange("p (m b e) -> p m b e", m=4, b=NB)
        xsT = arena[:, 0:2048].rearrange("p (i k s) -> p i k s", i=2, k=KT)
        hsb = arena[:, 2048:2560].rearrange("p (i n) -> p i n", i=2)
        hT = arena[:, 2560:2816].rearrange("p (i f s) -> p i f s", i=2, f=2)
        th = arena[:, 2816:2944].rearrange("p (f s) -> p f s", f=2)
        tm = arena[:, 2944:3072].rearrange("p (f s) -> p f s", f=2)
        ysb = arena[:, 3072:4096].rearrange("p (i n) -> p i n", i=2)
        ybuf = [rows[:, :, :], arena[:, 0:2048].rearrange("p (k d) -> p k d", k=2)]
        P = rows[:, :, :].rearrange("p c (q m i) -> p c q m i", q=2, m=4)
        Vx = rows[0:32, :, :].rearrange("p i (q b e) -> p i q b e", q=2, b=NB)
        ttf = tt[:, :, :].rearrange("p a n -> p (a n)")
        krf, vf, sgf = (a[:, :, :].rearrange("p a n -> p (a n)") for a in (kr, v, sg))
        onehot = krf[:, 0:192].rearrange("p (t k e) -> p t k e", t=3, k=2)
        rtmp = krf[:, 192:384].rearrange("p (t k e) -> p t k e", t=3, k=2)
        bsum = krf[:, 384:480].rearrange("p (t e) -> p t e", t=3)
        ge = krf[:, 480:576].rearrange("p (t e) -> p t e", t=3)
        ovcmp = krf[:, 576:832]
        lgT = krf[0:NG + NE, 832:832 + NT]
        masked = krf[:, 1152:1248].rearrange("p (t e) -> p t e", t=3)
        used = 0

        def cut(shape, dt=F32):
            nonlocal used
            n = int(np.prod(shape))
            a = sgf[:, used:used + n]
            used += n
            if dt != F32:
                a = a.bitcast(dt)
            return a.rearrange("p (a b) -> p a b", a=shape[0]) if len(shape) == 2 else a

        lg, r_oh, r_ex = cut((3, NG + NE)), cut((3, NG)), cut((3, NG))
        r_gm, r_pt, r_e2 = cut((3,)), cut((3,)), cut((3,))
        r_top, r_idx, r_if = cut((3, 8)), cut((3, 8), U32), cut((3, 2))
        gate, slot, slotu = cut((3, 2)), cut((3, 2)), cut((3, 2), U32)
        gidx, sidx, ogidx = cut((NBLK // 2,), U32), cut((NBLK,), U32), cut((OVER,), U32)
        ovi, ovg, ovs = cut((16,), I32), cut((1,), U32), cut((1,), U32)
        ov = cut((4, NE))
        ps_ = rs[:, 0:256].rearrange("p (q m i) -> p q m i", q=2, m=4)
        osm = arena[:, 2048:2176].rearrange("p (q e) -> p q e", q=2)
        ho = arena[0:9, 2176:2432].rearrange("p (c n) -> p c n", c=2)
        so = gls[0:64, :, :, :].rearrange("p c b t -> p (c b t)")[:, 0:512].rearrange("p (c n) -> p c n", c=4)
        stg = S1[:, :, :]
        tabg = vf[0:NBLK // 2, 0:256].rearrange("p (s c) -> p s c", c=2)
        tabs = vf[0:NBLK, 256:512].rearrange("p (s c) -> p s c", c=2)
        empty = vf[:, 512:552]
        gfin = ring[:, 0, 0:D]
        prow = [ring[0:NPRM, 10, 0:128], ring[0:NPRM, 10, 128:256]]
        sp_t = ring[:, 11, 0:16]

        def pr(a):
            return a.rearrange("p (c t) -> p c t", c=2)[:, :, 0:SEQ]

        def sa(a):
            return a.rearrange("p (c t) -> p c t", c=2)[:, :, SEQ:NT].rearrange("p c (b t) -> p c b t", b=NB)

        def spr(a):
            return a[:, :, 0:SEQ]

        def ssa(a):
            return a[:, :, SEQ:SCAN].rearrange("p c (b t) -> p c b t", b=NB)

        def bc(a, shape):
            return a.to_broadcast(shape)

        bank_full = [sem(f"bank_full{b}") for b in range(8)]
        bank_free = [sem(f"bank_free{b}") for b in range(8)]
        granule_in = [sem(f"granule_in{g}") for g in range(12)]
        wout3_in = sem("wout3_in")
        const_in, x_in, param_in, state_in, s0_in = (sem(f"{n}_in") for n in ("const", "x", "param", "state", "s0"))
        bd_in, wr_in, g_in, gfin_in, y_in0, y_in1 = (sem(f"{n}_in") for n in ("bd", "wr", "g", "gfin", "y0", "y1"))
        rms_ready, rows_ready = sem("rms_ready"), sem("rows_ready")
        xn_out = [sem(f"xn_out{t}") for t in range(3)]
        setup_done, prm_ready, u_lam, xa_ready, la_ready, tau_ready = (
            sem(n) for n in ("setup_done", "prm_ready", "u_lam", "xa_ready", "la_ready", "tau_ready"))
        gelu_arg, gelu_ready, glu_ready, conv_ready, ln_arg, ln_sq = (
            sem(n) for n in ("gelu_arg", "gelu_ready", "glu_ready", "conv_ready", "ln_arg", "ln_sq"))
        ixa_ready, sqrt_tau, ln_tanh, mixb_done, mixa_done = (
            sem(n) for n in ("ixa_ready", "sqrt_tau", "ln_tanh", "mixb_done", "mixa_done"))
        qr_ready, kr_ready, kz_ready, sg_tanh, sg_ready, stage_ready, h_ready, so_ready, ho_ready = (
            sem(n) for n in ("qr_ready", "kr_ready", "kz_ready", "sg_tanh", "sg_ready", "stage_ready",
                             "h_ready", "so_ready", "ho_ready"))
        var_ready, gstd_ready, oc_ready, vx_ready, os_norm, os_packed = (
            sem(n) for n in ("var_ready", "gstd_ready", "oc_ready", "vx_ready", "os_norm", "os_packed"))
        ret_out, st_out, conv_out = (sem(n) for n in ("ret_out", "st_out", "conv_out"))
        lg_arg, lg_exp, osum_ready, slot_ready, tab_init, tab_put, tab_in, idx_ready = (
            sem(n) for n in ("lg_arg", "lg_exp", "osum_ready", "slot_ready", "tab_init", "tab_put",
                             "tab_in", "idx_ready"))
        e2_arg, e2_ready = sem("e2_arg"), sem("e2_ready")
        gath = [sem(f"gathered{i}") for i in range(2)]
        y_put = [sem(f"y_put{i}") for i in range(2)]
        th_ready, tm_ready, moe_done = sem("th_ready"), sem("tm_ready"), sem("moe_done")
        all_put, bd_zero = sem("all_put"), sem("bd_zero")
        y_out, past_out = sem("y_out"), sem("past_out")
        O = [{n: sem(f"ov{l}_{n}") for n in ("w", "idx", "gath", "xT", "xTe", "h", "he", "hT", "th", "tm", "hTe",
                                             "y", "ye", "put", "done", "seen")} for l in range(DEPTH)]
        own_dve, own_act, own_pool = sem("own_dve"), sem("own_act"), sem("own_pool")

        def bank(name):
            return psum[:, BANK[name][0], :]

        def full(eng, l, name):
            b, n = BANK[name]
            eng.wait_ge(bank_full[b], l * PER_BANK[b] + n + 1)

        def freed(eng, l, name):
            b, n = BANK[name]
            eng.wait_ge(bank_free[b], l * PER_BANK[b] + n + 1)

        def free(i, name):
            i.then_inc(bank_free[BANK[name][0]], 1)

        def done(i, name):
            i.then_inc(bank_full[BANK[name][0]], 1)

        def expert_job(kind, u, it, l):
            b, n = {"x0": (0, 2 * it + u), "x1": (1, 2 * it + u), "h": (2 + u % 2, 2 * it + u // 2),
                    "hT": (4 + u % 2, 2 * it + u // 2), "y": (6 + u % 2, 2 * it + u // 2)}[kind]
            return b, l * PER_BANK[b] + EXPERT_BASE[b] + n

        def xfull(eng, kind, u, it, l):
            b, n = expert_job(kind, u, it, l)
            eng.wait_ge(bank_full[b], n + 1)

        def xfreed(eng, kind, u, it, l):
            b, n = expert_job(kind, u, it, l)
            eng.wait_ge(bank_free[b], n + 1)

        def granule(eng, l, g, use):
            per = 1 + (g >= 9) + GROUPS
            k = {"in": 0, "out": 1}[use] if isinstance(use, str) else 1 + (g >= 9) + use[0]
            eng.wait_ge(granule_in[g], 16 * (l * per + k + 1))

        block = ctx.enter_context(nc.Block())

        @block.sync
        def _(sp):
            sp.dma_start(const[:, :], cst).then_inc(const_in, 16)
            sp.dma_start(x[:, 0:2, :], x_prompt[0].rearrange("(t p) d -> p t d", p=128)).then_inc(x_in, 16)
            sp.dma_start(x[0:32, 2, :], x_sample.rearrange("b t d -> (b t) d")).then_inc(x_in, 16)

            def expert(l, it, u):
                e = 4 * it + u
                sp.dma_start(ring[:, 3 * u, :], w1[l, e].rearrange("(p k) f -> p (k f)", p=128)).then_inc(granule_in[3 * u], 16)
                sp.dma_start(ring[:, 3 * u + 1, :], w3[l, e].rearrange("(p k) f -> p (k f)", p=128)).then_inc(granule_in[3 * u + 1], 16)

            def expert2(l, it, u):
                e = 4 * it + u
                sp.dma_start(ring[:, 3 * u + 2, :].rearrange("p (f d) -> p f d", f=2),
                             w2[l, e].rearrange("(f p) d -> p f d", p=128)).then_inc(granule_in[3 * u + 2], 16)

            for l in range(DEPTH):
                for g in range(12):
                    if l:
                        xfull(sp, "y" if g % 3 == 2 else "h", g // 3, GROUPS - 1, l - 1)
                    elif g == 10:
                        sp.wait_ge(prm_ready, 2)
                    sp.dma_start(ring[:, g, :].rearrange("p (k c) -> p k c", k=KT),
                                 w_in[l].rearrange("(p k) c -> p k c", k=KT)[:, :, 256 * g:256 * g + 256]).then_inc(granule_in[g], 16)
                full(sp, l, "b5")
                expert(l, 0, 0)
                expert2(l, 0, 0)
                full(sp, l, "qk2")
                expert(l, 0, 1)
                full(sp, l, "qk2")
                expert2(l, 0, 1)
                sp.dma_start(ring[:, 6, :], w1[l, 2].rearrange("(p k) f -> p (k f)", p=128)).then_inc(granule_in[6], 16)
                sp.dma_start(ring[:, 7, :], w3[l, 2].rearrange("(p k) f -> p (k f)", p=128)).then_inc(granule_in[7], 16)
                full(sp, l, "vg2")
                for q in range(4):
                    dst = ring[:, 9 + q, :].rearrange("p (k c) -> p k c", k=KT) if q < 3 else w_out3
                    sp.dma_start(dst, w_out[l].rearrange("(k p) c -> p k c", p=128)[:, :, 256 * q:256 * q + 256]).then_inc(
                        granule_in[9 + q] if q < 3 else wout3_in, 16)
                expert2(l, 0, 2)
                full(sp, l, "w2")
                expert(l, 0, 3)
                expert2(l, 0, 3)
                for it in range(1, GROUPS):
                    for u in range(4):
                        xfull(sp, "h", u, it - 1, l)
                        expert(l, it, u)
                        xfull(sp, "y", u, it - 1, l)
                        expert2(l, it, u)
                sp.wait_ge(idx_ready, l + 1)
                n = sp.value_load(ovi[0:1, 8:9], min_val=0, max_val=OVER)
                xfull(sp, "y", 0, GROUPS - 1, l)
                with sp.If(n > 0):
                    with sp.Fori(0, n) as j:
                        e = sp.value_load(ovi[0:1, bass.ds(j, 1)], min_val=0, max_val=NE - 1)
                        sp.dma_start(ring[:, 0, :], w1[l, bass.ds(e, 1)].rearrange("o (p k) f -> p (o k f)", p=128)).then_inc(O[l]["w"], 16)
                        sp.dma_start(ring[:, 1, :], w3[l, bass.ds(e, 1)].rearrange("o (p k) f -> p (o k f)", p=128)).then_inc(O[l]["w"], 16)
                        sp.dma_start(ring[:, 2, :].rearrange("p (f d) -> p f d", f=2),
                                     w2[l, bass.ds(e, 1)].rearrange("o (f p) d -> p (o f) d", p=128)).then_inc(O[l]["w"], 16)
                        sp.wait_ge(O[l]["done"], j + 1)
                        sp.sem_inc(O[l]["seen"], 1)
                with sp.Else():
                    sp.nop()
            xfull(sp, "h", 0, GROUPS - 1, DEPTH - 1)
            sp.dma_start(gfin, g_fin.partition_broadcast(128)).then_inc(gfin_in, 16)
            for t, (o, n) in enumerate(TILES):
                sp.wait_ge(rows_ready, 6 * DEPTH + t + 1)
                dst = y_prompt[0, o:o + n] if t < 2 else y_sample.rearrange("b t d -> (b t) d")
                sp.dma_start(dst, x[0:n, t, :]).then_inc(y_out, 16)
            sp.wait_ge(y_out, 48)

        @block.tensor
        def _(pe):
            def start(l, name):
                b, n = BANK[name]
                if l * PER_BANK[b] + n:
                    pe.wait_ge(bank_free[b], l * PER_BANK[b] + n)
                return bank(name)

            ident = C("ident")
            pe.wait_ge(const_in, 16)

            def transpose(out, in_, n):
                return pe.transpose(out, in_, ident[0:n, 0:n])

            def norm(l, s):
                for t, (o, n) in enumerate(TILES):
                    pe.wait_ge(rows_ready, 6 * l + 3 * s + t + 1)
                    if l == 0 and s == 0 and t == 1:
                        pe.wait_ge(prm_ready, 1)
                    r = rows[0:n, t % 2, :].rearrange("p (m k) -> p m k", k=KT)
                    halves = (("a", 0, 4), ("b", 4, 8)) if t < 2 else (("a", 0, 8),)
                    for h, k0, k1 in halves:
                        name = f"n{s + 1}t{t}{h}"
                        b = start(l, name)[:, 0:(k1 - k0) * n].rearrange("p (k t) -> p k t", t=n)
                        for k in range(k0, k1):
                            i = transpose(b[:, k - k0, :], r[:, :, k], n)
                        done(i, name)

            for l in range(DEPTH):
                pe.wait_ge(state_in, 64 * (l + 1))
                b = start(l, "sa")
                for c in range(2):
                    i = transpose(b[:, 32 * c:32 * c + 32], cb[0:32, 128 * c:128 * c + 128], 32)
                done(i, "sa")
                b = start(l, "sc")
                for c in range(2):
                    for h in range(2):
                        i = transpose(b[:, 240 * c + 120 * h:240 * c + 120 * h + 120], xc[0:120, 256 * h + 128 * c:256 * h + 128 * c + 128], 120)
                done(i, "sc")
                if l == 0:
                    pe.wait_ge(param_in, 16 * len(params) * DEPTH)
                    for m in range(DEPTH):
                        i = transpose(psum[:, 2, 128 * m:128 * m + NPRM], prow[m], NPRM)
                    i.then_inc(u_lam, 1)
                norm(l, 0)

                freed(pe, l, "n1t2a")
                for c in range(8):
                    granule(pe, l, c // 2, "in")
                    b = start(l, f"b{c}")[:, 0:NT]
                    w = ring[:, c // 2, :].rearrange("p (k c) -> p k c", k=KT)
                    for k in range(KT):
                        i = pe.matmul(b, w[:, k, 128 * (c % 2):128 * (c % 2) + 128], uTk[:, k, :], start=k == 0, stop=k == KT - 1)
                    done(i, f"b{c}")

                def project(name, g, t):
                    for h in range(2):
                        granule(pe, l, g + h, "in")
                    b = start(l, name)
                    w = ring[:, g:g + 2, :].rearrange("p g (k c) -> p g k c", k=KT)
                    for k in range(KT):
                        i = pe.matmul(b, uTk[:, k, 128 * t:128 * t + 128], w[:, :, k, :], start=k == 0, stop=k == KT - 1)
                    done(i, name)

                def project_samples(name, g):
                    b = start(l, name)
                    for k in range(KT):
                        for h in range(2):
                            w = ring[:, g + 2 * h:g + 2 * h + 2, :].rearrange("p g (k c) -> p g k c", k=KT)
                            i = pe.matmul(b[32 * h:32 * h + 32, :], uTk[:, k, SEQ:NT], w[:, :, k, :], start=k == 0, stop=k == KT - 1,
                                          skip_group_check=True)
                    done(i, name)

                def gates(name, which, c):
                    if name == "gr0":
                        pe.wait_ge(bd_in, 16 * 8 * (l + 1))
                        pe.wait_ge(xa_ready, l + 1)
                    b = start(l, name)
                    done(pe.matmul(b[:, 0:NT], bd[:, which, c, :], XA[:, NT * c:NT * c + NT], start=True, stop=True), name)

                def turn(name, t):
                    o, n = TILES[t]
                    src, s, k = (tt[:, 0, :], qr_ready, 3 * l + t + 1) if name[1] == "q" else (kr[:, t, :], kr_ready, 3 * l + t + 1)
                    pe.wait_ge(s, k)
                    b = start(l, name)[:, 0:4 * n].rearrange("p (m t) -> p m t", m=4)
                    for m in range(4):
                        i = transpose(b[:, m, :], src[0:n, 128 * m:128 * m + 128], n)
                    done(i, name)

                project("q0", 4, 0)
                turn_order = [("k0", 6, 0), ("q1", 4, 1), ("k1", 6, 1)]
                for name, g, t in turn_order:
                    project(name, g, t)
                project_samples("qk2", 4)
                gates("gr0", 0, 0)
                turn("tq0", 0)
                gates("gi0", 1, 0)
                turn("tk0", 0)
                project("v0", 8, 0)
                gates("gr1", 0, 1)
                turn("tq1", 1)
                gates("gi1", 1, 1)
                turn("tk1", 1)
                project("g0", 10, 0)
                turn("tq2", 2)
                turn("tk2", 2)
                project("v1", 8, 1)
                project("g1", 10, 1)
                project_samples("vg2", 8)

                pe.wait_ge(stage_ready, l + 1)
                b = start(l, "st")
                for c in range(4):
                    i = transpose(b[0:64, 128 * c:128 * c + 128], stg[:, c, :], 128)
                done(i, "st")
                pe.wait_ge(conv_ready, l + 1)
                b = start(l, "lnm")
                for c in range(2):
                    i = pe.matmul(b[:, 0:NT], ones[:, :], cb[:, NT * c:NT * c + NT], start=c == 0, stop=c == 1)
                done(i, "lnm")

                def inner(c):
                    o, n = TILES[c]
                    freed(pe, l, f"tk{c}")
                    nm = [f"in{c}e", f"in{c}o"] if c < 2 else ["inse", "inso"]
                    b = [start(l, z)[0:n, 0:4 * n].rearrange("p (m t) -> p m t", m=4) for z in nm]
                    for m in range(4):
                        for q in range(2):
                            h = slice(64 * q, 64 * q + 64)
                            i = pe.matmul(b[q][:, m, :], kT[h, m, o:o + n], qT[h, m, o:o + n], start=True, stop=True)
                            if m == 3:
                                done(i, nm[q])

                def state(c):
                    pe.wait_ge(kz_ready, 3 * l + c + 1)
                    b = start(l, f"S{c}")[:, 0:256].rearrange("p (m e) -> p m e", m=4)
                    for m in range(4):
                        for q in range(2):
                            h = 64 * (2 * m + q)
                            i = pe.matmul(b[64 * q:64 * q + 64, m, :], kr[:, c, h:h + 64], v[:, c, h:h + 64], start=True, stop=True,
                                          skip_group_check=True)
                    done(i, f"S{c}")

                def inside(c):
                    freed(pe, l, f"in{c}e")
                    freed(pe, l, f"in{c}o")
                    b = start(l, f"o{c}")
                    for m in range(4):
                        for q in range(2):
                            h = 64 * (2 * m + q)
                            i = pe.matmul(b[:, h:h + 64], P[:, c, q, m, :], v[:, c, h:h + 64], start=True, stop=True)
                    done(i, f"o{c}")

                inner(0)
                inner(1)
                freed(pe, l, "v1")
                state(0)
                pe.wait_ge(ln_sq, l + 1)
                b = start(l, "lnv")
                for c in range(2):
                    i = pe.matmul(b[:, 0:NT], ones[:, :], cb[:, NT * c:NT * c + NT], start=c == 0, stop=c == 1)
                done(i, "lnv")
                inside(0)
                pe.wait_ge(h_ready, l + 1)
                b = start(l, "ht")
                for c in range(2):
                    i = transpose(b[0:9, 128 * c:128 * c + 128], hst[:, c, :], 128)
                done(i, "ht")
                freed(pe, l, "S0")
                b = [start(l, z)[:, 0:256].rearrange("p (m e) -> p m e", m=4) for z in ("x1e", "x1o")]
                for m in range(4):
                    for q in range(2):
                        h = slice(64 * q, 64 * q + 64)
                        i = pe.matmul(b[q][:, m, :], qT[h, m, 128:256], S1[h, m, :], start=True, stop=True)
                        if m == 3:
                            done(i, ("x1e", "x1o")[q])
                inside(1)
                state(1)
                inner(2)
                pe.wait_ge(s0_in, 128 * (l + 1))
                b = [start(l, z) for z in ("xse", "xso")]
                for m in range(4):
                    for q in range(2):
                        h = slice(64 * q, 64 * q + 64)
                        i = pe.matmul(b[q][32 * m:32 * m + 32, :], qT[h, m, SEQ:NT], S0[h, m, :, :], start=True, stop=True,
                                      skip_group_check=True)
                        if m == 3:
                            done(i, ("xse", "xso")[q])
                freed(pe, l, "inse")
                freed(pe, l, "inso")
                freed(pe, l, "vg2")
                b = start(l, "os")[:, 0:128].rearrange("p (q e) -> p q e", q=2)
                for m in range(4):
                    for q in range(2):
                        h = 64 * (2 * m + q)
                        i = pe.matmul(b[32 * m:32 * m + 32, q, :], ps_[0:32, q, m, :], v[0:32, 2, h:h + 64], start=True, stop=True,
                                      skip_group_check=True)
                done(i, "os")
                pe.wait_ge(kz_ready, 3 * l + 3)
                for m in range(4):
                    pe.wait_ge(vx_ready, 4 * l + m + 1)
                    b = start(l, f"su{m}")
                    for q in range(2):
                        h = 64 * (2 * m + q)
                        i = pe.matmul(b[64 * q:64 * q + 64, :], kr[0:32, 2, h:h + 64], Vx[:, m % 2, q, :, :], start=True, stop=True,
                                      skip_group_check=True)
                    done(i, f"su{m}")
                for t, (o, n) in enumerate(TILES):
                    pe.wait_ge(oc_ready, 3 * l + t + 1)
                    b = start(l, f"to{t}")[:, 0:4 * n].rearrange("p (m t) -> p m t", m=4)
                    for m in range(4):
                        i = transpose(b[:, m, :], sg[0:n, t, 128 * m:128 * m + 128], n)
                    done(i, f"to{t}")

                pe.wait_ge(mixa_done, l + 1)
                pe.wait_ge(mixb_done, l + 1)
                freed(pe, l, "to2")
                quarter = [ring[:, 9 + q, :].rearrange("p (k c) -> p k c", k=KT) for q in range(3)] + [w_out3]
                for q in range(4):
                    if q < 3:
                        granule(pe, l, 9 + q, "out")
                    else:
                        pe.wait_ge(wout3_in, 16 * (l + 1))
                    for t in range(2):
                        b = start(l, f"w{q}{t}")[:, 0:256]
                        for k in range(KT):
                            i = pe.matmul(b, mixT[:, k, 128 * t:128 * t + 128], quarter[q][:, k, :], start=k == 0, stop=k == KT - 1)
                        done(i, f"w{q}{t}")
                b = start(l, "w2")
                for k in range(KT):
                    for q in range(4):
                        i = pe.matmul(b[32 * q:32 * q + 32, 0:256], mixT[:, k, SEQ:NT], quarter[q][:, k, :], start=k == 0,
                                      stop=k == KT - 1, skip_group_check=True)
                done(i, "w2")

                norm(l, 1)
                freed(pe, l, "n2t2a")
                pe.wait_ge(wr_in, 32 * (l + 1))
                b = start(l, "lgT")
                for k in range(KT):
                    i = pe.matmul(b[0:NG + NE, 0:NT], wr[:, k, :], uTk[:, k, :], start=k == 0, stop=k == KT - 1)
                done(i, "lgT")
                freed(pe, l, "lgT")
                b = start(l, "lg")[:, 0:3 * (NG + NE)].rearrange("p (t e) -> p t e", t=3)
                for t, (o, n) in enumerate(TILES):
                    i = transpose(b[0:n, t, :], lgT[:, o:o + n], NG + NE)
                done(i, "lg")
                pe.wait_ge(osum_ready, l + 1)
                b = start(l, "cum")[:, 0:128].rearrange("p (t e) -> p t e", t=4)
                for t in range(4):
                    for s in range(min(t, 2) + 1):
                        n = TILES[s][1]
                        i = pe.matmul(b[:, t, :], (upb if s == t else onesb)[0:n, :], osumb[0:n, s, :], start=s == 0,
                                      stop=s == min(t, 2))
                done(i, "cum")
                pe.wait_ge(tab_in, 48 * (l + 1))
                b = start(l, "tabg")
                i = transpose(b[:, 0:NBLK // 2], tabg[:, :, 0], NBLK // 2)
                done(i, "tabg")
                b = start(l, "tabs")
                transpose(b[:, 0:NBLK], tabs[:, :, 1], NBLK)
                i = transpose(b[:, 64:64 + NBLK], tabs[:, :, 0], NBLK)
                done(i, "tabs")

                def begin(kind, u, it):
                    b, n = expert_job(kind, u, it, l)
                    pe.wait_ge(bank_free[b], n)
                    return psum[:, b, :]

                def finish(i, kind, u):
                    i.then_inc(bank_full[{"x0": 0, "x1": 1}.get(kind, {"h": 2, "hT": 4, "y": 6}.get(kind, 0) + u % 2)], 1)

                def tokens(g2, it):
                    par = g2 % 2
                    pe.wait_ge(gath[par], 16 * (l * GROUPS + it + g2 // 2 + 1))
                    for kind, k0 in (("x0", 0), ("x1", 4)):
                        b = begin(kind, g2, it).rearrange("p (k s) -> p k s", k=4)
                        r = rows[:, par, :].rearrange("p (m k) -> p m k", k=KT)
                        for k in range(4):
                            i = transpose(b[:, k, :], r[:, :, k0 + k], 128)
                        finish(i, kind, g2)

                def up(u, it):
                    granule(pe, l, 3 * u, (it,))
                    granule(pe, l, 3 * u + 1, (it,))
                    if u % 2 == 0:
                        xfreed(pe, "x1", u // 2, it, l)
                    b = begin("h", u, it)
                    w = [ring[:, 3 * u + j, :].rearrange("p (k f) -> p k f", k=KT) for j in range(2)]
                    s = slice(SLOTS * (u % 2), SLOTS * (u % 2) + SLOTS)
                    for k in range(KT):
                        for j in range(2):
                            i = pe.matmul(b[64 * j:64 * j + 64, 0:FE], xsT[:, u // 2, k, s], w[j][:, k, :], start=k == 0,
                                          stop=k == KT - 1, skip_group_check=True)
                    finish(i, "h", u)

                def turn_h(u, it):
                    xfreed(pe, "h", u, it, l)
                    b = begin("hT", u, it)
                    for f in range(2):
                        i = transpose(b[:, 128 * f:128 * f + 128], hsb[:, u % 2, 128 * f:128 * f + 128], 128)
                    finish(i, "hT", u)

                def down(u, it):
                    granule(pe, l, 3 * u + 2, (it,))
                    xfreed(pe, "hT", u, it, l)
                    b = begin("y", u, it)
                    w = ring[:, 3 * u + 2, :].rearrange("p (f d) -> p f d", f=2)
                    for f in range(2):
                        for j in range(2):
                            i = pe.matmul(b[64 * j:64 * j + 64, :], hT[:, u % 2, f, :], w[:, f, 512 * j:512 * j + 512], start=f == 0,
                                          stop=f == 1, skip_group_check=True)
                    finish(i, "y", u)

                def experts4(it, first=False, last=False):
                    for u in range(4):
                        up(u, it)
                        if u:
                            down(u - 1, it)
                        elif not first:
                            down(3, it - 1)
                        if u == 1 or (u == 3 and not last):
                            tokens((u + 1) // 2, it)
                        turn_h(u, it)

                tokens(0, 0)
                experts4(0, first=True)
                with pe.Fori(1, GROUPS - 1) as it:
                    experts4(it)
                experts4(GROUPS - 1, last=True)
                down(3, GROUPS - 1)

                o = O[l]
                pe.wait_ge(idx_ready, l + 1)
                n = pe.value_load(ovi[0:1, 8:9], min_val=0, max_val=OVER)
                for kind, u in (("x0", 1), ("x1", 1), ("h", 2), ("hT", 2), ("y", 2)):
                    xfreed(pe, kind, u, GROUPS - 1, l)
                xfreed(pe, "y", 3, GROUPS - 1, l)
                with pe.If(n > 0):
                    with pe.Fori(0, n) as j:
                        pe.wait_ge(o["gath"], 16 * j + 16)
                        pe.sem_inc(o["seen"], 1)
                        r = rows[0:SLOTS, 0, :].rearrange("p (m k) -> p m k", k=KT)
                        for k in range(KT):
                            i = transpose(psum[:, 0, SLOTS * k:SLOTS * k + SLOTS], r[:, :, k], SLOTS)
                        i.then_inc(o["xT"], 1)
                        pe.wait_ge(o["xTe"], j + 1)
                        pe.wait_ge(o["w"], 48 * j + 48)
                        for k in range(KT):
                            for q in range(2):
                                w = ring[:, q, :].rearrange("p (k f) -> p k f", k=KT)
                                i = pe.matmul(psum[64 * q:64 * q + 64, 2, 0:FE], xsT[:, 0, k, 0:SLOTS], w[:, k, :], start=k == 0,
                                              stop=k == KT - 1, skip_group_check=True)
                        i.then_inc(o["h"], 1)
                        pe.wait_ge(o["he"], j + 1)
                        for f in range(2):
                            i = transpose(psum[:, 4, 128 * f:128 * f + 128], hsb[:, 0, 128 * f:128 * f + 128], 128)
                        i.then_inc(o["hT"], 1)
                        pe.wait_ge(o["hTe"], j + 1)
                        w = ring[:, 2, :].rearrange("p (f d) -> p f d", f=2)
                        for f in range(2):
                            for q in range(2):
                                i = pe.matmul(psum[64 * q:64 * q + 64, 6, :], hT[:, 0, f, :], w[:, f, 512 * q:512 * q + 512],
                                              start=f == 0, stop=f == 1, skip_group_check=True)
                        i.then_inc(o["y"], 1)
                        pe.wait_ge(o["done"], j + 1)
                with pe.Else():
                    pe.nop()

        @block.vector
        def _(dve):
            own = Own(dve, own_dve)

            def do(i):
                own(i)
                own.wait()

            T = dve.tensor_tensor
            S = dve.tensor_scalar
            STT = dve.scalar_tensor_tensor

            own(dve.memset(eps[:, :], EPS))
            own(dve.memset(ones[:, :], 1.0 / W_B))
            own(dve.memset(onesb[:, :], 1.0))
            own(dve.memset(ssq[:, :], 1.0))
            own(dve.memset(axp[:, :, 0:3], 0.0))
            own(dve.memset(glp[:, :, 0:30], 0.0))
            own.wait()
            dve.wait_ge(const_in, 16)
            dve.tensor_copy(upb[:, :], C("upper")).then_inc(setup_done, 1)

            dve.wait_ge(u_lam, 1)
            do(dve.tensor_copy(prm[:, :, :], psum[:, 2, 0:256].rearrange("p (l n) -> p l n", l=2)[:, :, 0:NPRM]))
            own(S(prm[:, :, PCOL["ba"]:PCOL["ba"] + 4], prm[:, :, PCOL["ba"]:PCOL["ba"] + 4], 0.5, None, ALU.mult))
            own(S(prm[:, :, PCOL["lg"]:PCOL["lg"] + 8], prm[:, :, PCOL["lg"]:PCOL["lg"] + 8], 0.5, None, ALU.mult))
            lam = prm[:, :, PCOL["lam"]:PCOL["lam"] + 2]
            z, az, u, w = (sp_t[:, 4 * i:4 * i + 4].rearrange("p (l c) -> p l c", l=2) for i in range(4))
            do(S(z, lam, -1.0, None, ALU.mult))
            T(az, lam, z, ALU.max).then_inc(prm_ready, 1)
            dve.wait_ge(u_lam, 2)
            do(S(w, u, 1.0, None, ALU.add))
            S(lam, w, -1.0, None, ALU.add).then_inc(la_ready, 1)
            dve.wait_ge(u_lam, 3)
            dve.wait_ge(la_ready, 1)
            do(T(az, az, u, ALU.mult))
            do(S(w, lam, 0.0, None, ALU.is_equal))
            do(T(u, u, w, ALU.mult))
            do(S(lam, lam, 1.0e-30, None, ALU.max))
            do(dve.reciprocal(w, lam))
            do(T(az, az, w, ALU.mult))
            do(T(az, az, u, ALU.add))
            do(S(z, z, 0.0, None, ALU.max))
            do(T(az, az, z, ALU.add))
            S(lam, az, -2.0, None, ALU.mult).then_inc(prm_ready, 1)
            dve.wait_ge(prm_ready, 2)

            def norm(l, s):
                g = (gmx, gff)[s]
                dve.wait_ge(rms_ready, 2 * l + s + 1)
                do(dve.reciprocal(rec[:, :], rms[:, :]))
                if l == 0 and s == 0:
                    dve.wait_ge(g_in, 16 * 4)

                def scaled(t):
                    n = TILES[t][1]
                    S(rows[0:n, t % 2, :], x[0:n, t, :], rec[0:n, t:t + 1], None, ALU.mult).then_inc(rows_ready, 1)

                def turned(t, h, k0, k1):
                    o, n = TILES[t]
                    name = f"n{s + 1}t{t}{h}"
                    full(dve, l, name)
                    free(T(uTk[:, k0:k1, o:o + n], bank(name)[:, 0:(k1 - k0) * n].rearrange("p (k t) -> p k t", t=n),
                           bc(g[:, l, k0:k1].unsqueeze(2), [128, k1 - k0, n]), ALU.mult), name)

                scaled(0)
                scaled(1)
                if s:
                    full(dve, l, "w2")
                turned(0, "a", 0, 4)
                turned(0, "b", 4, 8)
                if s:
                    dve.wait_ge(xn_out[0], 16 * (l + 1))
                scaled(2)
                turned(1, "a", 0, 4)
                turned(1, "b", 4, 8)
                turned(2, "a", 0, 8)

            for l in range(DEPTH):
                full(dve, l, "sc")
                if l:
                    dve.wait_ge(conv_out, 16 * 11 * l)
                free(dve.tensor_copy(gls[:, :, :, 0:30], bank("sc")[:, 0:480].rearrange("p (c b k) -> p c b k", c=2, b=NB)), "sc")
                full(dve, l, "sa")
                sa_b = bank("sa")[:, 0:64].rearrange("p (c n) -> p c n", c=2)
                own(dve.tensor_copy(axs[:, :, :, 0:3], sa_b[:, :, 0:24].rearrange("p c (b k) -> p c b k", b=NB)))
                own(dve.memset(ssa(As)[:, :, :, 0], 0.0))
                free(dve.tensor_copy(ssa(Bs)[:, :, :, 0], sa_b[:, :, 24:32]), "sa")
                norm(l, 0)

                freed(dve, l, "b3")
                last = [None] * 4
                for k in range(CONV_A):
                    for c in range(2):
                        w = P_(l, "cw", 2 * k + c)
                        for i, (src, dst) in enumerate((
                                (axp[:, c, k:k + SEQ], pr(XA)[:, c, :]),
                                (axs[:, c, :, k:k + DT], sa(XA)[:, c, :, :]))):
                            if k == 0:
                                ins_ = S(dst, src, w, P_(l, "cb", c), ALU.mult, ALU.add)
                            else:
                                own.wait(last[2 * c + i])
                                ins_ = STT(dst, src, w, dst, ALU.mult, ALU.add)
                            if k < CONV_A - 1:
                                last[2 * c + i] = own(ins_)
                            elif (c, i) == (1, 1):
                                ins_.then_inc(xa_ready, 1)
                            else:
                                own(ins_)

                freed(dve, l, "b7")
                STT(glp[:, :, 30:LB], pr(xc[:, :]), 1.0, pr(cb[:, :]), ALU.add, ALU.mult).then_inc(glu_ready, 1)
                dve.wait_ge(glu_ready, 2 * l + 1)
                for c in range(2):
                    i = STT(gls[:, c, :, 30:LT], sa(xc[:, :])[:, c], 1.0, sa(cb[:, :])[:, c], ALU.add, ALU.mult)
                    if c:
                        i.then_inc(glu_ready, 1)
                    else:
                        own(i)
                dve.wait_ge(glu_ready, 2 * l + 2)

                chain = [None, None]

                def taps(k0, k1):
                    for k in range(k0, k1):
                        for c in range(2):
                            w = P_(l, "dw", 2 * k + c)
                            dst = pr(cb[:, :])[:, c, :]
                            if k == 0:
                                chain[c] = own(S(dst, glp[:, c, k:k + SEQ], w, P_(l, "db", c), ALU.mult, ALU.add))
                            else:
                                own.wait(chain[c])
                                chain[c] = own(STT(dst, glp[:, c, k:k + SEQ], w, dst, ALU.mult, ALU.add))

                def taps_samples(c):
                    pw = ttf[:, 0:NB * DT * CONV_B].rearrange("p (b t k) -> p b t k", b=NB, t=DT)
                    a = PCOL["dw"] + c
                    w = prm[:, l, a:a + 2 * CONV_B - 1:2]
                    for t in range(DT):
                        own(T(pw[:, :, t, :], gls[:, c, :, t:t + CONV_B], bc(w.unsqueeze(1), [128, NB, CONV_B]), ALU.mult))
                    own.wait()
                    do(dve.tensor_reduce(sa(cb[:, :])[:, c], pw, AX, ALU.add))
                    own(S(sa(cb[:, :])[:, c], sa(cb[:, :])[:, c], P_(l, "db", c), None, ALU.add))

                taps_samples(0)
                taps_samples(1)
                own.wait()

                def rotate(name, t, out, lo, cos, sin, n, last_sem):
                    b = bank(name)[lo:lo + n, :].rearrange("p (h s i) -> p h s i", h=NH, s=2)
                    c3 = C(cos, n)[:, 32 * t:32 * t + 32].unsqueeze(1)
                    s3 = C(sin, n)[:, 32 * t:32 * t + 32].unsqueeze(1)
                    o4 = out.rearrange("p (h s i) -> p h s i", h=NH, s=2)
                    x4 = tt[0:n, 1, :].rearrange("p (h s i) -> p h s i", h=NH, s=2)
                    full(dve, l, name)
                    own(T(o4, b, bc(c3.unsqueeze(1), [n, NH, 2, 32]), ALU.mult))
                    own(T(x4[:, :, 0, :], b[:, :, 1, :], bc(s3, [n, NH, 32]), ALU.mult))
                    i = T(x4[:, :, 1, :], b[:, :, 0, :], bc(s3, [n, NH, 32]), ALU.mult)
                    if name != "qk2" or lo:
                        free(i, name)
                        freed(dve, l, name)
                    else:
                        own(i)
                    own.wait()
                    own(T(o4[:, :, 0, :], o4[:, :, 0, :], x4[:, :, 0, :], ALU.subtract))
                    T(o4[:, :, 1, :], o4[:, :, 1, :], x4[:, :, 1, :], ALU.add).then_inc(last_sem, 1)
                    own.wait()

                def rotate_q(t, name="", lo=0):
                    if t:
                        full(dve, l, f"tq{t - 1}")
                    rotate(name or f"q{t}", t, tt[0:TILES[t][1], 0, :], lo, "cos", "sin", TILES[t][1], qr_ready)
                    dve.wait_ge(qr_ready, 3 * l + t + 1)

                def rotate_k(t, name="", lo=0):
                    rotate(name or f"k{t}", t, kr[0:TILES[t][1], t, :], lo, "cos", "sin", TILES[t][1], kr_ready)
                    dve.wait_ge(kr_ready, 3 * l + t + 1)

                def decay_keys(t):
                    n = TILES[t][1]
                    full(dve, l, f"tk{t}")
                    k3 = kr[0:n, t, :].rearrange("p (h e) -> p h e", h=NH)
                    T(k3, k3, bc(C("zeta" if t < 2 else "zetas", n).unsqueeze(2), [n, NH, HD]), ALU.mult).then_inc(kz_ready, 1)

                def gate_v(t):
                    n = TILES[t][1]
                    name = f"g{t}" if t < 2 else "vg2"
                    lo = 0 if t < 2 else 32
                    dve.wait_ge(sg_tanh, 3 * l + t + 1)
                    free(STT(sg[0:n, t, :], sg[0:n, t, :], 1.0, bank(name)[lo:lo + n, :], ALU.add, ALU.mult), name)

                rotate_q(0)
                rotate_k(0)
                taps(0, 6)
                rotate_q(1)
                rotate_k(1)
                freed(dve, l, "gr0")
                own(S(RG[:, 0:NT], RG[:, 0:NT], 1.0, P_(l, "lam", 0), ALU.add, ALU.mult))
                rotate_q(2, "qk2", 0)
                rotate_k(2, "qk2", 32)
                freed(dve, l, "gi1")
                S(RG[:, NT:], RG[:, NT:], 1.0, P_(l, "lam", 1), ALU.add, ALU.mult).then_inc(la_ready, 1)
                STT(IG, IG, 1.0, XA, ALU.add, ALU.mult).then_inc(ixa_ready, 1)
                taps(6, 12)
                dve.wait_ge(tau_ready, l + 1)
                do(S(RI, RG, -1.0, 1.0, ALU.mult, ALU.add))
                do(dve.reciprocal(RI, RI))
                dve.wait_ge(ixa_ready, l + 1)
                do(T(IG, IG, RI, ALU.mult))
                own(STT(spr(As), pr(RG), 1.0, pr(RI), ALU.add, ALU.mult))
                for c in range(2):
                    own(STT(ssa(As)[:, c, :, 1:5], sa(RG)[:, c], 1.0, sa(RI)[:, c], ALU.add, ALU.mult))
                gate_v(0)
                dve.wait_ge(sqrt_tau, l + 1)
                own(T(spr(Bs), pr(IG), pr(XA), ALU.mult))
                for c in range(2):
                    own(T(ssa(Bs)[:, c, :, 1:5], sa(IG)[:, c], sa(XA)[:, c], ALU.mult))
                own.wait()
                for c in range(2):
                    own(dve.tensor_tensor_scan(HS[:, c, :], As[:, c, :], Bs[:, c, :], 0.0, ALU.mult, ALU.add))
                dve.wait_ge(gelu_ready, l + 1)
                m0 = mixT[:, 0:2, :].rearrange("p c t -> p (c t)")
                do(STT(m0, m0, 1.0, AG, ALU.add, ALU.mult))
                own(STT(spr(mixT[:, 0:2, :]), spr(mixT[:, 0:2, :]), 0.5, spr(HS), ALU.mult, ALU.mult))
                for c in range(2):
                    ms = mixT[:, c, SEQ:NT].rearrange("p (b t) -> p b t", b=NB)
                    own(STT(ms, ms, 0.5, ssa(HS)[:, c, :, 1:5], ALU.mult, ALU.mult))
                own(dve.tensor_copy(hst[:, :, 0:1], HS[:, :, SEQ - 1:SEQ]))
                own.wait()
                dve.tensor_copy(hst[:, :, 1:9], ssa(HS)[:, :, :, 4]).then_inc(h_ready, 1)
                dve.wait_ge(h_ready, l + 1)
                own.wait()
                dve.sem_inc(mixa_done, 1)
                taps(12, 22)
                decay_keys(0)
                decay_keys(1)
                gate_v(1)
                taps(22, CONV_B)
                own.wait()
                dve.sem_inc(conv_ready, 1)
                decay_keys(2)
                gate_v(2)

                def mask_scores(c):
                    for q in range(2):
                        name = f"in{c if c < 2 else 's'}{'eo'[q]}"
                        full(dve, l, name)
                        if c < 2:
                            i = T(P[:, c, q].rearrange("p m i -> p (m i)"), bank(name), C("dmat")[:, 512 * q:512 * q + 512], ALU.mult)
                        else:
                            i = T(ps_[0:32, q].rearrange("p m i -> p (m i)"), bank(name)[0:32, 0:128],
                                  C("dmats", 32)[:, 128 * q:128 * q + 128], ALU.mult)
                        free(i, name)

                mask_scores(0)
                mask_scores(1)

                full(dve, l, "lnm")
                for c in range(2):
                    i = T(xc[:, NT * c:NT * c + NT], cb[:, NT * c:NT * c + NT], bank("lnm")[:, 0:NT], ALU.subtract)
                    free(i, "lnm") if c else own(i)
                full(dve, l, "S0")
                if l:
                    dve.wait_ge(ret_out, 32 * l)
                free(dve.tensor_copy(S1[:, :, :], bank("S0")[:, 0:256].rearrange("p (m e) -> p m e", m=4)), "S0")

                def group_norm(src, n, H, t):
                    mu, va = st_mu[0:n, 0:H], st_va[0:n, 0:H]
                    sq = tt[0:n, 1, 0:H * HD].rearrange("p (h e) -> p h e", h=H)
                    do(dve.tensor_reduce(mu, src, AX, ALU.add))
                    do(S(mu, mu, 1.0 / HD, None, ALU.mult))
                    do(T(src, src, bc(mu.unsqueeze(2), [n, H, HD]), ALU.subtract))
                    do(T(sq, src, src, ALU.mult))
                    dve.tensor_reduce(va, sq, AX, ALU.add).then_inc(var_ready, 1)
                    dve.wait_ge(gstd_ready, 3 * l + t + 1)
                    do(dve.reciprocal(va, va))
                    do(T(src, src, bc(va.unsqueeze(2), [n, H, HD]), ALU.mult))

                def gated(t, src):
                    n = TILES[t][1]
                    freed(dve, l, f"g{t}" if t < 2 else "vg2")
                    T(sg[0:n, t, :], sg[0:n, t, :], src, ALU.mult).then_inc(oc_ready, 1)
                    dve.wait_ge(oc_ready, 3 * l + t + 1)

                full(dve, l, "tq2")
                full(dve, l, "o0")
                free(dve.tensor_copy(tt[:, 0, :], bank("o0")), "o0")
                freed(dve, l, "o0")
                group_norm(tt[:, 0, :].rearrange("p (h e) -> p h e", h=NH), 128, NH, 0)
                gated(0, tt[:, 0, :])

                freed(dve, l, "lnv")
                do(dve.reciprocal(rs[:, :], rs[:, :]))
                do(T(xc[:, :].rearrange("p (c t) -> p c t", c=2), xc[:, :].rearrange("p (c t) -> p c t", c=2),
                     bc(rs[:, :].unsqueeze(1), [128, 2, NT]), ALU.mult))
                for c in range(2):
                    S(xc[:, NT * c:NT * c + NT], xc[:, NT * c:NT * c + NT], P_(l, "lg", c), P_(l, "lb", c), ALU.mult, ALU.add).then_inc(ln_arg, 1)

                t3 = tt[:, 0, :].rearrange("p (m q e) -> p m q e", m=4, q=2)
                for q in range(2):
                    name = ("x1e", "x1o")[q]
                    full(dve, l, name)
                    xi = C("xi").rearrange("p (m q) -> p m q", q=2)[:, :, q]
                    free(T(t3[:, :, q, :], bank(name)[:, 0:256].rearrange("p (m e) -> p m e", m=4),
                           bc(xi.unsqueeze(2), [128, 4, HD]), ALU.mult), name)
                    freed(dve, l, name)
                full(dve, l, "o1")
                free(T(tt[:, 0, :], tt[:, 0, :], bank("o1"), ALU.add), "o1")
                freed(dve, l, "o1")
                group_norm(tt[:, 0, :].rearrange("p (h e) -> p h e", h=NH), 128, NH, 1)
                gated(1, tt[:, 0, :])
                mask_scores(2)
                freed(dve, l, "S0")
                full(dve, l, "x1o")
                do(T(S1[:, :, :], S1[:, :, :], bc(C("gch").unsqueeze(2), [128, 4, HD]), ALU.mult))
                full(dve, l, "S1")
                free(T(S1[:, :, :], S1[:, :, :], bank("S1")[:, 0:256].rearrange("p (m e) -> p m e", m=4), ALU.add), "S1")

                dve.wait_ge(ln_tanh, l + 1)
                STT(mixT[:, 2:4, :].rearrange("p c t -> p (c t)"), cb[:, :], 1.0, xc[:, :], ALU.add, ALU.mult).then_inc(mixb_done, 1)

                for q in range(2):
                    name = ("xse", "xso")[q]
                    full(dve, l, name)
                    free(T(tt[:, q, :].rearrange("p (b e) -> p b e", b=NB), bank(name).rearrange("p (b e) -> p b e", b=NB),
                           bc(C("cmask")[:, 8 * q:8 * q + 8].unsqueeze(2), [128, NB, HD]), ALU.mult), name)
                    freed(dve, l, name)
                for q in range(2):
                    own(dve.tensor_reduce(osm[:, q, :], tt[:, q, :].rearrange("p (b e) -> p e b", b=NB), AX, ALU.add))
                own.wait()
                full(dve, l, "os")
                free(T(osm[:, :, :], osm[:, :, :], bank("os")[:, 0:128].rearrange("p (q e) -> p q e", q=2), ALU.add), "os")
                freed(dve, l, "os")
                group_norm(osm[:, :, :], 128, 2, 2)
                dve.sem_inc(os_norm, 1)
                for m in range(4):
                    name = f"su{m}"
                    full(dve, l, name)
                    s = S0[:, m, :, :].rearrange("p b e -> p (b e)")
                    free(STT(s, s, C("gst")[:, m:m + 1], bank(name), ALU.mult, ALU.add), name)
                dve.wait_ge(os_packed, l + 1)
                gated(2, tt[0:32, 0, :])
                for t, (o, n) in enumerate(TILES):
                    name = f"to{t}"
                    full(dve, l, name)
                    free(T(mixT[:, 4:8, o:o + n], bank(name)[:, 0:4 * n].rearrange("p (m t) -> p m t", m=4),
                           bc(prm[:, l, PCOL["rg"]:PCOL["rg"] + 4].unsqueeze(2), [128, 4, n]), ALU.mult), name)

                for q in range(4):
                    for t in range(2):
                        name = f"w{q}{t}"
                        full(dve, l, name)
                        s = x[:, t, 256 * q:256 * q + 256]
                        free(T(s, s, bank(name)[:, 0:256], ALU.add), name)
                full(dve, l, "w2")
                for q in range(4):
                    s = x[0:32, 2, 256 * q:256 * q + 256]
                    i = T(s, s, bank("w2")[32 * q:32 * q + 32, 0:256], ALU.add)
                    free(i, "w2") if q == 3 else own(i)

                norm(l, 1)

                full(dve, l, "lg")
                do(dve.memset(lg[:, 2, :], 0.0))
                lgb = bank("lg")[:, 0:3 * (NG + NE)].rearrange("p (t e) -> p t e", t=3)
                own(dve.tensor_copy(lg[:, 0:2, :], lgb[:, 0:2, :]))
                free(dve.tensor_copy(lg[0:32, 2, :], lgb[0:32, 2, :]), "lg")
                freed(dve, l, "lg")
                own.wait()
                G = lg[:, :, 0:NG]
                do(dve.tensor_reduce(r_gm[:, :], G, AX, ALU.max))
                gm3 = bc(r_gm[:, :].unsqueeze(2), [128, 3, NG])
                T(r_ex[:, :, :], G, gm3, ALU.subtract).then_inc(lg_arg, 1)
                do(T(r_oh[:, :, :], G, gm3, ALU.is_equal))
                do(T(r_oh[:, :, :], r_oh[:, :, :], bc(C("desc").unsqueeze(1), [128, 3, NG]), ALU.mult))
                do(dve.tensor_reduce(r_gm[:, :], r_oh[:, :, :], AX, ALU.max))
                do(T(r_oh[:, :, :], r_oh[:, :, :], gm3, ALU.is_equal))
                E3 = lg[:, :, NG:].rearrange("p t (g e) -> p t g e", g=NG)
                M3 = masked.rearrange("p t (g e) -> p t g e", g=NG)
                for t in range(3):
                    own(T(M3[:, t], E3[:, t], bc(r_oh[:, t, :].unsqueeze(2), [128, NG, EPG]), ALU.mult))
                own.wait()
                do(S(r_oh[:, :, :], r_oh[:, :, :], -1.0, BIG, ALU.add, ALU.mult))
                for t in range(3):
                    own(T(M3[:, t], M3[:, t], bc(r_oh[:, t, :].unsqueeze(2), [128, NG, EPG]), ALU.add))
                own.wait()
                for t in range(3):
                    own(dve.max(r_top[:, t, :], masked[:, t, :]))
                own.wait()
                T(r_e2[:, :], r_top[:, :, 1], r_top[:, :, 0], ALU.subtract).then_inc(e2_arg, 1)
                for t in range(3):
                    own(dve.max_index(r_idx[:, t, :], r_top[:, t, :], masked[:, t, :]))
                own.wait()
                do(dve.tensor_copy(r_if[:, :, :], r_idx[:, :, 0:2]))
                for k in range(2):
                    own(T(onehot[:, :, k, :], bc(C("iota").unsqueeze(1), [128, 3, NE]), bc(r_if[:, :, k].unsqueeze(2), [128, 3, NE]), ALU.is_equal))
                own.wait()
                T(osumb[:, :, :], onehot[:, :, 0, :], onehot[:, :, 1, :], ALU.add).then_inc(osum_ready, 1)
                dve.wait_ge(lg_exp, l + 1)
                do(dve.tensor_reduce(r_pt[:, :], r_ex[:, :, :], AX, ALU.add))
                do(dve.reciprocal(r_pt[:, :], r_pt[:, :]))
                dve.wait_ge(e2_ready, l + 1)
                do(S(r_gm[:, :], r_e2[:, :], 1.0, None, ALU.add))
                do(dve.reciprocal(r_gm[:, :], r_gm[:, :]))
                do(T(gate[:, :, 0], r_gm[:, :], r_pt[:, :], ALU.mult))
                own(T(gate[:, :, 1], gate[:, :, 0], r_e2[:, :], ALU.mult))
                full(dve, l, "cum")
                cum = bank("cum")[:, 0:128].rearrange("p (t e) -> p t e", t=4)
                cmp_ = ovcmp[:, 0:128].rearrange("p (e j) -> p e j", j=4)
                own(dve.memset(ov[:, 3, :], 0.0))
                do(T(cmp_, bc(cum[:, 3, :].unsqueeze(2), [128, NE, 4]), bc(C("thr").unsqueeze(1), [128, NE, 4]), ALU.is_gt))
                do(dve.tensor_reduce(ov[:, 0, :], cmp_, AX, ALU.add))
                do(dve.tensor_tensor_scan(ov[:, 1, :], ov[:, 0, :], ov[:, 3, :], 0.0, ALU.add, ALU.add))
                do(T(ov[:, 2, :], ov[:, 1, :], ov[:, 0, :], ALU.subtract))
                do(STT(ov[:, 2, :], ov[:, 2, :], float(SLOTS), C("ovc"), ALU.mult, ALU.add))
                do(S(ge, cum[:, 0:3, :], float(SLOTS), None, ALU.is_ge))
                do(T(ge, ge, bc(ov[:, 2:3, :], [128, 3, NE]), ALU.mult))
                free(T(bsum, cum[:, 0:3, :], bc(C("e64").unsqueeze(1), [128, 3, NE]), ALU.add), "cum")
                freed(dve, l, "cum")
                do(T(bsum, bsum, ge, ALU.add))
                for k in range(2):
                    own(T(rtmp[:, :, k, :], onehot[:, :, k, :], bsum, ALU.mult))
                own.wait()
                do(dve.tensor_reduce(slot[:, :, :], rtmp, AX, ALU.add))
                dve.tensor_copy(slotu[:, :, :], slot[:, :, :]).then_inc(slot_ready, 1)
                cmp8 = ovcmp.rearrange("p (j e) -> p j e", j=OVER)
                do(T(cmp8, bc(ov[:, 1:2, :], [128, OVER, NE]), bc(C("iotaj").unsqueeze(2), [128, OVER, NE]), ALU.is_le))
                do(dve.tensor_reduce(ov[:, 0, 0:OVER], cmp8, AX, ALU.add))
                own(S(ovi[:, 0:OVER], ov[:, 0, 0:OVER], float(NE - 1), None, ALU.min))
                own(dve.tensor_copy(ovi[:, 8:9], ov[:, 1, NE - 1:NE]))
                full(dve, l, "tabg")
                free(dve.tensor_copy(gidx[:, :], bank("tabg")[:, 0:NBLK // 2]), "tabg")
                full(dve, l, "tabs")
                tabs_b = bank("tabs")
                own(S(sidx[:, :], tabs_b[:, 0:NBLK], 2.0, C("half"), ALU.mult, ALU.add))
                free(dve.tensor_copy(ogidx[:, :], tabs_b[:, 64 + NE:64 + NBLK]), "tabs")
                freed(dve, l, "tabs")
                freed(dve, l, "tabg")
                own.wait()
                dve.sem_inc(idx_ready, 1)

                g3 = bc(gff[:, l, :].unsqueeze(2), [128, KT, 128])

                def tokens(g2, it):
                    for n_, (kind, k0) in enumerate((("x0", 0), ("x1", 4))):
                        b, n = expert_job(kind, g2, it, l)
                        dve.wait_ge(bank_full[b], n + 1)
                        T(xsT[:, g2 % 2, k0:k0 + 4, :], psum[:, b, :].rearrange("p (k s) -> p k s", k=4), g3[:, k0:k0 + 4, :],
                          ALU.mult).then_inc(bank_free[b], 1)

                def hidden(u, it):
                    b, n = expert_job("hT", u, it, l)
                    p = psum[:, b, 0:256].rearrange("p (f j s) -> p f j s", f=2, j=2)
                    dve.wait_ge(th_ready, l * NE + 4 * it + u + 1)
                    STT(tm, th, 1.0, p[:, :, 0, :], ALU.add, ALU.mult).then_inc(tm_ready, 1)
                    dve.wait_ge(tm_ready, l * NE + 4 * it + u + 1)
                    STT(hT[:, u % 2], tm, 0.5, p[:, :, 1, :], ALU.mult, ALU.mult).then_inc(bank_free[b], 1)

                def result(u, it):
                    b, n = expert_job("y", u, it, l)
                    dve.wait_ge(bank_full[b], n + 1)
                    if isinstance(it, int) and it == 0 and u < 2:
                        if l:
                            dve.wait_ge(y_put[u % 2], 16 * (l * NE // 2))
                    else:
                        dve.wait_ge(y_put[u % 2], 16 * (l * NE // 2 + 2 * it + u // 2))
                    dve.tensor_copy(ysb[:, u % 2, :], psum[:, b, :]).then_inc(bank_free[b], 1)

                def experts4(it, first=False, last=False):
                    for u in range(4):
                        if u:
                            result(u - 1, it)
                        elif not first:
                            result(3, it - 1)
                        if u == 1 or (u == 3 and not last):
                            tokens((u + 1) // 2, it)
                        hidden(u, it)

                dve.wait_ge(st_out, 128 * (l + 1))
                tokens(0, 0)
                experts4(0, first=True)
                with dve.Fori(1, GROUPS - 1) as it:
                    experts4(it)
                experts4(GROUPS - 1, last=True)
                result(3, GROUPS - 1)

                o = O[l]
                n = dve.value_load(ovi[0:1, 8:9], min_val=0, max_val=OVER)
                for i in range(2):
                    dve.wait_ge(y_put[i], 16 * (l + 1) * NE // 2)
                with dve.If(n > 0):
                    with dve.Fori(0, n) as j:
                        dve.tensor_copy(ovg[:, :], ogidx[:, bass.ds(j, 1)]).then_inc(o["idx"], 1)
                        dve.tensor_copy(ovs[:, :], sidx[:, bass.ds(j + NE, 1)]).then_inc(o["idx"], 1)
                        dve.wait_ge(o["xT"], j + 1)
                        T(xsT[:, 0, :, 0:SLOTS], psum[:, 0, :].rearrange("p (k s) -> p k s", k=KT), g3[:, :, 0:SLOTS],
                          ALU.mult).then_inc(o["xTe"], 1)
                        p = psum[:, 4, 0:256].rearrange("p (f j s) -> p f j s", f=2, j=2)
                        dve.wait_ge(o["th"], j + 1)
                        STT(tm, th, 1.0, p[:, :, 0, :], ALU.add, ALU.mult).then_inc(o["tm"], 1)
                        dve.wait_ge(o["tm"], j + 1)
                        STT(hT[:, 0], tm, 0.5, p[:, :, 1, :], ALU.mult, ALU.mult).then_inc(o["hTe"], 1)
                        dve.wait_ge(o["y"], j + 1)
                        dve.tensor_copy(ysb[:, 0, :], psum[:, 6, :]).then_inc(o["ye"], 1)
                        dve.wait_ge(o["done"], j + 1)
                with dve.Else():
                    dve.nop()

                for t, (oo, nn) in enumerate(TILES):
                    dve.wait_ge((y_in0, y_in1)[t % 2], 16 * (l * (2 - t % 2) + t // 2 + 1))
                    yb = ybuf[t % 2]
                    do(STT(x[0:nn, t, :], yb[0:nn, 0, :], gate[0:nn, t, 0:1], x[0:nn, t, :], ALU.mult, ALU.add))
                    STT(x[0:nn, t, :], yb[0:nn, 1, :], gate[0:nn, t, 1:2], x[0:nn, t, :], ALU.mult, ALU.add).then_inc(moe_done, 1)
                dve.wait_ge(moe_done, 3 * (l + 1))

            dve.wait_ge(rms_ready, 2 * DEPTH + 1)
            do(dve.reciprocal(rec[:, :], rms[:, :]))
            dve.wait_ge(gfin_in, 16)
            for t, (o, n) in enumerate(TILES):
                STT(x[0:n, t, :], x[0:n, t, :], rec[0:n, t:t + 1], gfin[0:n, :], ALU.mult, ALU.mult).then_inc(rows_ready, 1)

        @block.scalar
        def _(act):
            own = Own(act, own_act)

            def do(i):
                own(i)
                own.wait()

            A = act.activation

            def load_states(l):
                act.dma_start(cb[0:24, 0:256], st_lru_conv[l].rearrange("b k c -> (b k) c")).then_inc(state_in, 16)
                act.dma_start(cb[24:32, 0:256], st_lru_h[l]).then_inc(state_in, 16)
                for h in range(2):
                    act.dma_start(xc[0:120, 256 * h:256 * h + 256],
                                  st_conv[l, 4 * h:4 * h + 4].rearrange("b k c -> (b k) c")).then_inc(state_in, 16)

            def load_gates(l):
                for i, w in enumerate((w_a, w_x)):
                    for h in range(4):
                        r = 64 * (h % 2)
                        act.dma_start(bd[r:r + 64, i, h // 2, r:r + 64], w[l, h]).then_inc(bd_in, 16)

            def load_router(l):
                act.dma_start(wr[:, :, 0:NG], w_grp[l].rearrange("(p k) g -> p k g", k=KT)).then_inc(wr_in, 16)
                act.dma_start(wr[:, :, NG:], w_exp[l].rearrange("(p k) g -> p k g", k=KT)).then_inc(wr_in, 16)

            act.dma_start(gmx[:, :, :], g_mix.rearrange("l (p k) -> p l k", k=KT)).then_inc(g_in, 16)
            act.dma_start(gff[:, :, :], g_ffn.rearrange("l (p k) -> p l k", k=KT)).then_inc(g_in, 16)
            act.dma_start(lbias[0:NG, :], b_grp.rearrange("l g -> g l"), allow_slow_non_contiguous=True).then_inc(g_in, 16)
            act.dma_start(lbias[NG:, :], b_exp.rearrange("l g -> g l"), allow_slow_non_contiguous=True).then_inc(g_in, 16)
            load_states(0)
            for l in range(DEPTH):
                for a, name in params:
                    c, k = PCOL[name], dict(PARAMS)[name]
                    src = a[l].rearrange("(c p) -> c p", p=128) if len(a.shape) == 2 else a[l].rearrange("k (c p) -> (k c) p", p=128)
                    act.dma_start(prow[l][c:c + k, :], src).then_inc(param_in, 16)
            load_router(0)
            act.wait_ge(bd_zero, 1)
            load_gates(0)
            act.dma_start(s_conv[:, :, 0:CONV_B - 1 - DT, :], st_conv[:, :, DT:, :]).then_inc(past_out, 16)

            z, az, u, w = (sp_t[:, 4 * i:4 * i + 4].rearrange("p (l c) -> p l c", l=2) for i in range(4))
            act.wait_ge(prm_ready, 1)
            A(u, az, ACT.Exp, scale=-1.0).then_inc(u_lam, 1)
            act.wait_ge(la_ready, 1)
            A(az, w, ACT.Ln).then_inc(u_lam, 1)

            def mean_square():
                for t, (o, n) in enumerate(TILES):
                    do(A(ttf[0:n, :], x[0:n, t, :], ACT.Square, accum_out=ssq[0:n, t:t + 1]))
                A(rms[:, :], ssq[:, :], ACT.Sqrt, bias=eps[:, :], scale=1.0 / D).then_inc(rms_ready, 1)

            act.wait_ge(setup_done, 1)
            for l in range(DEPTH):
                if l:
                    act.wait_ge(moe_done, 3 * l)
                else:
                    act.wait_ge(x_in, 32)
                mean_square()
                for c in range(2):
                    full(act, l, f"b{c}")
                    free(A(AG[:, NT * c:NT * c + NT], bank(f"b{c}")[:, 0:NT], ACT.Copy), f"b{c}")
                for c in range(2):
                    name = f"b{2 + c}"
                    b = bank(name)
                    full(act, l, name)
                    own(A(axp[:, c, 3:LA], b[:, 0:SEQ], ACT.Copy))
                    free(A(axs[:, c, :, 3:LS], b[:, SEQ:NT].rearrange("p (b t) -> p b t", b=NB), ACT.Copy), name)
                for c in range(2):
                    name = f"b{4 + c}"
                    full(act, l, name)
                    free(A(cb[:, NT * c:NT * c + NT], bank(name)[:, 0:NT], ACT.Copy, scale=0.5), name)
                for c in range(2):
                    name = f"b{6 + c}"
                    full(act, l, name)
                    free(A(xc[:, NT * c:NT * c + NT], bank(name)[:, 0:NT], ACT.Tanh, scale=0.5), name)

                def gate(name, dst, bias, c):
                    full(act, l, name)
                    free(A(dst[:, NT * c:NT * c + NT], bank(name)[:, 0:NT], ACT.Tanh, bias=P_(l, bias, c), scale=0.5), name)

                def turned(name, t):
                    o, n = TILES[t]
                    dst = qT if name[1] == "q" else kT
                    full(act, l, name)
                    free(A(dst[:, :, o:o + n], bank(name)[:, 0:4 * n].rearrange("p (m t) -> p m t", m=4), ACT.Copy), name)

                def values(t):
                    name = f"v{t}"
                    full(act, l, name)
                    free(A(v[:, t, :], bank(name), ACT.Copy), name)

                def gate_tanh(t):
                    full(act, l, f"g{t}")
                    A(sg[:, t, :], bank(f"g{t}"), ACT.Tanh, scale=0.5).then_inc(sg_tanh, 1)

                gate("gr0", RG, "ba", 0)
                turned("tq0", 0)
                gate("gi0", IG, "bx", 0)
                turned("tk0", 0)
                if l == 0:
                    act.wait_ge(tab_init, 16 * DEPTH)
                values(0)
                gate("gr1", RG, "ba", 1)
                turned("tq1", 1)
                gate("gi1", IG, "bx", 1)
                turned("tk1", 1)
                gate_tanh(0)
                if l + 1 < DEPTH:
                    load_gates(l + 1)
                turned("tq2", 2)
                turned("tk2", 2)
                act.wait_ge(la_ready, l + 2)
                A(RG, RG, ACT.Tanh).then_inc(tau_ready, 1)
                act.wait_ge(gelu_arg, l + 1)
                m0 = mixT[:, 0:2, :].rearrange("p c t -> p (c t)")
                A(m0, m0, ACT.Tanh, scale=0.7978845608028654).then_inc(gelu_ready, 1)
                act.wait_ge(tau_ready, l + 1)
                act.wait_ge(ixa_ready, l + 1)
                A(XA, RG, ACT.Sqrt, scale=-1.0).then_inc(sqrt_tau, 1)
                values(1)
                gate_tanh(1)
                full(act, l, "vg2")
                b = bank("vg2")
                own(A(v[0:32, 2, :], b[0:32, :], ACT.Copy))
                A(sg[0:32, 2, :], b[32:64, :], ACT.Tanh, scale=0.5).then_inc(sg_tanh, 1)
                act.wait_ge(mixa_done, l + 1)
                for q in range(2):
                    for m in range(4):
                        act.dma_start(S0[64 * q:64 * q + 64, m, :, :],
                                      st_ret[l, :, 2 * m + q].rearrange("b d e -> d b e")).then_inc(s0_in, 16)
                full(act, l, "st")
                act.wait_ge(conv_ready, l + 1)
                A(so[:, :, :], bank("st")[0:64, :].rearrange("p (c n) -> p c n", c=4), ACT.Copy).then_inc(bank_free[BANK["st"][0]], 1)
                freed(act, l, "st")
                act.dma_start(o_lru_conv[l, 0].rearrange("k (c n) -> k c n", c=2), so[29:32, 0:2, :]).then_inc(conv_out, 16)
                act.dma_start(o_conv[l, 0].rearrange("k (c n) -> k c n", c=2), so[2:32, 2:4, :]).then_inc(conv_out, 16)
                for t in range(DT):
                    s = slice(32 + NB * t, 32 + NB * t + NB)
                    if t:
                        act.dma_start(s_lru_conv[l, :, t - 1].rearrange("b (c n) -> b c n", c=2), so[s, 0:2, :]).then_inc(conv_out, 16)
                    act.dma_start(s_conv[l, :, CONV_B - 1 - DT + t].rearrange("b (c n) -> b c n", c=2), so[s, 2:4, :]).then_inc(conv_out, 16)
                freed(act, l, "lnm")
                A(cb[:, :], xc[:, :], ACT.Square).then_inc(ln_sq, 1)
                full(act, l, "lnv")
                free(A(rs[:, :], bank("lnv")[:, 0:NT], ACT.Sqrt, bias=eps[:, :]), "lnv")

                def group_std(t):
                    H = NH if t < 2 else 2
                    act.wait_ge(var_ready, 3 * l + t + 1)
                    A(st_va[:, 0:H], st_va[:, 0:H], ACT.Sqrt, bias=eps[:, :], scale=1.0 / HD).then_inc(gstd_ready, 1)

                full(act, l, "ht")
                free(A(ho[:, :, :], bank("ht")[0:9, 0:256].rearrange("p (c n) -> p c n", c=2), ACT.Copy), "ht")
                freed(act, l, "ht")
                act.dma_start(o_lru_h[l], ho[0:1, :, :].rearrange("p c n -> p (c n)")).then_inc(conv_out, 16)
                act.dma_start(s_lru_h[l], ho[1:9, :, :].rearrange("p c n -> p (c n)")).then_inc(conv_out, 16)
                group_std(0)
                act.wait_ge(ln_arg, 2 * l + 2)
                A(cb[:, :], xc[:, :], ACT.Tanh).then_inc(ln_tanh, 1)
                group_std(1)
                freed(act, l, "S1")
                for q in range(2):
                    act.dma_start(o_ret[l, 0].rearrange("(m q) d e -> q d m e", q=2)[q], S1[64 * q:64 * q + 64, :, :]).then_inc(ret_out, 16)
                group_std(2)
                act.wait_ge(os_norm, l + 1)
                for m in range(4):
                    i = A(tt[0:32, 0, 128 * m:128 * m + 128], osm[32 * m:32 * m + 32, :, :].rearrange("p q e -> p (q e)"), ACT.Copy)
                    i.then_inc(os_packed, 1) if m == 3 else own(i)
                freed(act, l, "su3")
                for q in range(2):
                    for m in range(4):
                        act.dma_start(s_ret[l, :, 2 * m + q].rearrange("b d e -> d b e"), S0[64 * q:64 * q + 64, m, :, :]).then_inc(st_out, 16)
                if l + 1 < DEPTH:
                    act.wait_ge(mixb_done, l + 1)
                    full(act, l, "w00")
                    load_states(l + 1)

                freed(act, l, "w2")
                mean_square()
                for t, (o, n) in enumerate(TILES):
                    act.wait_ge(rows_ready, 6 * l + 3 + t + 1)
                    act.dma_start(xn_dram[o:o + n, :], rows[0:n, t % 2, :]).then_inc(xn_out[t], 16)
                full(act, l, "lgT")
                free(A(lgT, bank("lgT")[0:NG + NE, 0:NT], ACT.Identity, bias=lbias[:, l:l + 1]), "lgT")
                if l + 1 < DEPTH:
                    load_router(l + 1)
                act.wait_ge(lg_arg, l + 1)
                A(r_ex[:, :, :], r_ex[:, :, :], ACT.Exp).then_inc(lg_exp, 1)
                act.wait_ge(e2_arg, l + 1)
                A(r_e2[:, :], r_e2[:, :], ACT.Exp).then_inc(e2_ready, 1)
                act.wait_ge(tab_put, 96 * (l + 1))
                act.dma_start(vf[0:NBLK // 2, 0:256], tab_dram[l].rearrange("(g s) c -> g (s c)", s=128)).then_inc(tab_in, 16)
                for j in range(2):
                    act.dma_start(vf[0:NBLK, 256 + 128 * j:384 + 128 * j], tab_dram[l].rearrange("(g s) c -> g (s c)", s=SLOTS)).then_inc(tab_in, 16)

                def experts4(it, first=False):
                    for u in range(4):
                        b, n = expert_job("h", u, it, l)
                        act.wait_ge(bank_full[b], n + 1)
                        A(hsb[:, u % 2, :], psum[:, b, 0:256], ACT.Copy).then_inc(bank_free[b], 1)
                        if not (first and u == 0):
                            xfreed(act, "hT", (u - 1) % 4, it if u else it - 1, l)
                        b, n = expert_job("hT", u, it, l)
                        act.wait_ge(bank_full[b], n + 1)
                        A(th, psum[:, b, 0:256].rearrange("p (f j s) -> p f j s", f=2, j=2)[:, :, 0, :], ACT.Tanh, scale=0.5).then_inc(th_ready, 1)

                act.wait_ge(conv_out, 16 * 11 * (l + 1))
                experts4(0, first=True)
                with act.Fori(1, GROUPS) as it:
                    experts4(it)

                o = O[l]
                act.wait_ge(idx_ready, l + 1)
                n = act.value_load(ovi[0:1, 8:9], min_val=0, max_val=OVER)
                xfreed(act, "hT", 3, GROUPS - 1, l)
                with act.If(n > 0):
                    with act.Fori(0, n) as j:
                        act.wait_ge(o["h"], j + 1)
                        A(hsb[:, 0, :], psum[:, 2, 0:256], ACT.Copy).then_inc(o["he"], 1)
                        act.wait_ge(o["hT"], j + 1)
                        A(th, psum[:, 4, 0:256].rearrange("p (f j s) -> p f j s", f=2, j=2)[:, :, 0, :], ACT.Tanh, scale=0.5).then_inc(o["th"], 1)
                        act.wait_ge(o["done"], j + 1)
                with act.Else():
                    act.nop()

                yv = y_dram.rearrange("(t q) c -> t (q c)", q=4)
                act.wait_ge(all_put, l + 1)
                for t, (o_, n_) in enumerate(TILES):
                    if t == 2:
                        act.wait_ge(moe_done, 3 * l + 1)
                    dst = (rows[0:n_, :, :].rearrange("p k d -> p (k d)"), arena[0:n_, 0:2048])[t % 2]
                    act.dma_start(dst, yv[o_:o_ + n_]).then_inc((y_in0, y_in1)[t % 2], 16)

            act.wait_ge(moe_done, 3 * DEPTH)
            mean_square()
            act.wait_ge(conv_out, 16 * 11 * DEPTH)
            act.wait_ge(past_out, 16)
            act.wait_ge(ret_out, 32 * DEPTH)
            act.wait_ge(st_out, 128 * DEPTH)

        @block.gpsimd
        def _(pool):
            own = Own(pool, own_pool)
            pool.memset(bd[:, :, :, :], 0.0).then_inc(bd_zero, 1)
            own(pool.memset(empty, EMPTY))
            own.wait()
            for l in range(DEPTH):
                pool.dma_start(tab_dram[l].rearrange("(p s) c -> p (s c)", p=128), empty).then_inc(tab_init, 16)
            T = pool.tensor_tensor
            for l in range(DEPTH):
                freed(pool, l, "b1")
                m0 = mixT[:, 0:2, :].rearrange("p c t -> p (c t)")
                own(T(m0, AG, AG, ALU.mult))
                own.wait()
                own(pool.tensor_scalar(m0, m0, 0.044715, 1.0, ALU.mult, ALU.add))
                own.wait()
                T(m0, m0, AG, ALU.mult).then_inc(gelu_arg, 1)
                if l:
                    pool.wait_ge(ret_out, 32 * l)
                freed(pool, l, "b3")
                dve_done = 2 * l + 2
                own(pool.tensor_copy(stg[:, 0:2, 0:32], axp[:, :, LA - 32:LA]))
                for c in range(2):
                    own(pool.tensor_copy(stg[:, c, 32:64].rearrange("p (t b) -> p b t", b=NB), axs[:, c, :, 3:LS]))
                pool.wait_ge(glu_ready, dve_done)
                own(pool.tensor_copy(stg[:, 2:4, 0:32], glp[:, :, LB - 32:LB]))
                own(pool.tensor_copy(stg[:, 2, 32:64].rearrange("p (t b) -> p b t", b=NB), gls[:, 0, :, 30:LT]))
                pool.tensor_copy(stg[:, 3, 32:64].rearrange("p (t b) -> p b t", b=NB), gls[:, 1, :, 30:LT]).then_inc(stage_ready, 1)
                pool.wait_ge(sg_tanh, 3 * l + 3)
                full(pool, l, "o0")
                full(pool, l, "o1")
                vm = bc(C("vmask", 32).unsqueeze(2), [32, NB, HD])
                for m in range(4):
                    if m > 1:
                        full(pool, l, f"su{m - 2}")
                    for q in range(2):
                        h = 64 * (2 * m + q)
                        i = T(Vx[:, m % 2, q, :, :], bc(v[0:32, 2, h:h + 64].unsqueeze(1), [32, NB, HD]), vm, ALU.mult)
                        i.then_inc(vx_ready, 1) if q else own(i)

                if l == 0:
                    pool.wait_ge(tab_init, 16 * DEPTH)
                pool.wait_ge(slot_ready, l + 1)
                for t, (o, n) in enumerate(TILES):
                    for k in range(2):
                        a = 4 * t + 2 * k
                        pool.indirect_dma_start(out=tab_dram[l], out_offset=bass.IndirectOffsetOnAxis(ap=slotu[0:n, t, k:k + 1], axis=0),
                                                in_=C("vals", n)[:, a:a + 2], in_offset=None, bounds_check=NSLOT - 1,
                                                oob_is_err=False).then_inc(tab_put, 16)
                pool.wait_ge(idx_ready, l + 1)
                for t in range(3):
                    pool.wait_ge(xn_out[t], 16 * (l + 1))

                def gather(g):
                    if g > 1:
                        xfull(pool, "x1", g % 2, (g - 2) // 2, l)
                    else:
                        full(pool, l, "n2t2a")
                    pool.indirect_dma_start(out=rows[:, g % 2, :], out_offset=None, in_=xn_dram,
                                            in_offset=bass.IndirectOffsetOnAxis(ap=gidx[:, g:g + 1], axis=0),
                                            bounds_check=NT - 1, oob_is_err=False).then_inc(gath[g % 2], 16)

                def put(e):
                    xfreed(pool, "y", e % 4, e // 4, l)
                    pool.indirect_dma_start(out=y_dram, out_offset=bass.IndirectOffsetOnAxis(ap=sidx[:, e:e + 1], axis=0),
                                            in_=ysb[:, e % 2, :], in_offset=None, bounds_check=4 * NT - 1,
                                            oob_is_err=False).then_inc(y_put[e % 2], 16)

                gather(0)
                gather(1)
                for e in range(NE):
                    if e % 2 == 0 and e // 2 + 2 < NE // 2:
                        gather(e // 2 + 2)
                    put(e)
                for i in range(2):
                    pool.wait_ge(y_put[i], 16 * (l + 1) * NE // 2)

                o = O[l]
                n = pool.value_load(ovi[0:1, 8:9], min_val=0, max_val=OVER)
                xfull(pool, "x1", 1, GROUPS - 1, l)
                with pool.If(n > 0):
                    with pool.Fori(0, n) as j:
                        pool.wait_ge(o["idx"], 2 * j + 2)
                        pool.sem_inc(o["seen"], 1)
                        pool.indirect_dma_start(out=rows[0:SLOTS, 0, :], out_offset=None, in_=xn_dram,
                                                in_offset=bass.IndirectOffsetOnAxis(ap=ovg[0:SLOTS, :], axis=0),
                                                bounds_check=NT - 1, oob_is_err=False).then_inc(o["gath"], 16)
                        pool.wait_ge(o["ye"], j + 1)
                        pool.sem_inc(o["seen"], 1)
                        pool.indirect_dma_start(out=y_dram, out_offset=bass.IndirectOffsetOnAxis(ap=ovs[:, :], axis=0),
                                                in_=ysb[:, 0, :], in_offset=None, bounds_check=4 * NT - 1,
                                                oob_is_err=False).then_inc(o["put"], 16)
                        pool.wait_ge(o["put"], 16 * j + 16)
                        pool.sem_inc(o["done"], 1)
                with pool.Else():
                    pool.nop()
                pool.sem_inc(all_put, 1)


_INS = ["x_prompt", "x_sample", "state_lru_h", "state_lru_conv", "state_conv", "state_ret", "norm_mix_g",
        "norm_ffn_g", "final_norm_g", "w_in", "lru_conv_w", "lru_conv_b", "lru_wa", "lru_ba", "lru_wx",
        "lru_bx", "lru_lambda", "cm_dw_w", "cm_dw_b", "cm_ln_g", "cm_ln_b", "ret_norm_g", "w_out",
        "moe_w_group", "moe_b_group", "moe_w_expert", "moe_b_expert", "moe_w1", "moe_w3", "moe_w2"]
_OUTS = [(1, SEQ, D), (NB, DT, D)] + OUTS[2:]


def kernel(**inputs):
    import concourse.bacc as bacc
    from concourse.bass_utils import run_bass_kernel_spmd

    nc = bacc.Bacc("TRN2", target_bir_lowering=False, num_devices=1)
    arrays, ins = {}, []
    for name, a in [(n, np.ascontiguousarray(inputs[n])) for n in _INS] + [("constants", constants())]:
        arrays[f"in_{name}"] = a
        ins.append(nc.dram_tensor(f"in_{name}", a.shape, mybir.dt.from_np(a.dtype), kind="ExternalInput").ap())
    outs = [nc.dram_tensor(f"out_{i}", s, F32, kind="ExternalOutput").ap() for i, s in enumerate(_OUTS)]
    build(nc, ins, outs)
    r = run_bass_kernel_spmd(nc, [arrays], core_ids=[0])
    return tuple(r.results[0][f"out_{i}"] for i in range(len(_OUTS)))
```

```python
from contextlib import ExitStack

import numpy as np

import concourse.bass as bass
from concourse import mybir

F32 = mybir.dt.float32
BF16 = mybir.dt.bfloat16
U32 = mybir.dt.uint32
I32 = mybir.dt.int32
ALU = mybir.AluOpType
ACT = mybir.ActivationFunctionType
AX = mybir.AxisListType.X

DEPTH, D, SEQ, NB, DT = 2, 1024, 256, 8, 4
NT = SEQ + NB * DT
TILES = [(0, 128), (128, 128), (256, 32)]
KT = D // 128
W_A = W_B = 256
CONV_A, CONV_B = 4, 31
NH, HD = 8, 64
NG, EPG = 4, 8
NE = NG * EPG
FE = 256
EPS = 1e-6
PAST = 2048
SLOTS = 64
OVER = 8
NBLK = NE + OVER
OUTSIDE = 2048
NPAIR = NE // 2
BIG = 1.0e30
WAIT_NORM, WAIT_CHOICE, WAIT_MARKS, WAIT_ROWS = (13, 8), 17, 26, 17
LA, LS = 3 + SEQ, 3 + DT
LB, LT = 30 + SEQ, 30 + DT
SCAN = SEQ + NB * (DT + 1)

PARAMS = [("cw", CONV_A * 2), ("cb", 2), ("ba", 2), ("bx", 2), ("lam", 2), ("dw", CONV_B * 2),
          ("db", 2), ("lg", 2), ("lb", 2), ("rg", 4)]
PCOL, _n = {}, 0
for _name, _k in PARAMS:
    PCOL[_name] = _n
    _n += _k
NPRM = _n

CONSTS = [("ident", 128), ("upper", 128), ("dmat", 1024), ("dmats", 256), ("xi", 8), ("zeta", 8),
          ("zetas", 8), ("gch", 4), ("gst", 4), ("cmask", 16), ("vmask", 8), ("cos", 96),
          ("sin", 96), ("iota", 128), ("first", NBLK), ("ovc", 32),
          ("thr", 4), ("iotaj", 8), ("desc", 4), ("vals", 6)]
CCOL, _n = {}, 0
for _name, _k in CONSTS:
    CCOL[_name] = (_n, _k)
    _n += _k
NCONST = _n


def constants():
    c = np.zeros((128, NCONST), np.float32)

    def put(name, a, rows=128):
        o, k = CCOL[name]
        c[:rows, o:o + k] = np.asarray(a, np.float64).reshape(rows, k).astype(np.float32)

    p = np.arange(128)
    g = 1.0 - 2.0 ** (-5.0 - np.arange(NH))
    heads = np.arange(NH).reshape(4, 2).T
    scale = HD ** -0.5
    put("ident", np.eye(128))
    put("upper", p[:, None] < p[None, :])
    diff = p[None, :] - p[:, None]
    put("dmat", scale * np.where(diff[:, None, None, :] >= 0,
                         g[heads][None, :, :, None] ** np.maximum(diff, 0)[:, None, None, :], 0.0))
    s = np.arange(32)
    ds = s[None, :] - s[:, None]
    same = (s[None, :] // DT == s[:, None] // DT) & (ds >= 0)
    put("dmats", scale * np.where(same[:, None, None, :],
                          g[heads][None, :, :, None] ** np.maximum(ds, 0)[:, None, None, :], 0.0), 32)
    put("xi", g[None, :] ** (p[:, None] + 1))
    put("zeta", scale * g[None, :] ** (127 - p[:, None]))
    put("zetas", scale * g[None, :] ** (DT - 1 - s[:, None] % DT), 32)
    par, m4 = (p // 64)[:, None], np.arange(4)[None, :]
    put("gch", g[2 * m4 + par] ** 128)
    put("gst", g[2 * m4 + par] ** DT)
    m, tok = p // 32, p % 32
    cm = np.zeros((128, 2, NB))
    for q in range(2):
        cm[p, q, tok // DT] = g[2 * m + q] ** (tok % DT + 1)
    put("cmask", cm)
    put("vmask", s[:, None] // DT == np.arange(NB)[None, :], 32)
    half = HD // 2
    inv = (np.float32(10000.0) ** (-np.arange(half, dtype=np.float32) / np.float32(half))).astype(np.float32)
    pos = np.zeros((128, 3), np.float32)
    pos[:, 0], pos[:, 1] = p, p + 128
    pos[:32, 2] = PAST + s % DT
    ang = (pos[:, :, None] * inv[None, None, :]).astype(np.float32).astype(np.float64)
    put("cos", np.cos(ang))
    put("sin", np.sin(ang))
    e = np.arange(NE)
    put("iota", np.tile(np.arange(128), (128, 1)))
    put("first", np.tile(SLOTS * np.arange(NBLK), (128, 1)))
    put("ovc", np.tile(SLOTS * (NE - 1 - e), (128, 1)))
    put("thr", np.tile(SLOTS * (1 + np.arange(4)), (128, 1)))
    put("iotaj", np.tile(np.arange(OVER), (128, 1)))
    put("desc", np.tile(NG - np.arange(NG), (128, 1)))
    put("vals", (2 * (p[:, None, None] + 128 * np.arange(3)[None, :, None]) + np.arange(2) - OUTSIDE).reshape(128, 6))
    return c


def bank_plan():
    jobs = [("n1t0a", 0), ("n1t0b", 1), ("n1t1a", 2), ("n1t1b", 3), ("n1t2a", 0)]
    jobs += [(f"b{c}", 4 + c % 4) for c in range(4)] + [("sa", 1), ("sc", 2)]
    jobs += [(f"b{c}", 4 + c % 4) for c in range(4, 8)]
    jobs += [("q0", 0), ("k0", 1), ("s2", 2), ("gr0", 7), ("gi0", 3), ("gr1", 4), ("gi1", 5),
             ("tq0", 6), ("tk0", 7), ("q1", 0), ("tq2", 3), ("tk2", 4), ("st", 5), ("k1", 1),
             ("in0e", 5), ("in0o", 6), ("v0", 7), ("tq1", 3), ("S0", 4), ("tk1", 5), ("inse", 0), ("inso", 6),
             ("v1", 2), ("in1e", 1), ("in1o", 3), ("o0", 7), ("x1e", 4), ("x1o", 5), ("g0", 0), ("o1", 2),
             ("S1", 6), ("lnm", 7), ("xse", 1), ("xso", 3), ("os", 4), ("su0", 0), ("lnv", 2), ("g1", 5), ("ht", 6),
             ("su1", 4), ("to0", 3), ("su2", 6), ("to1", 1)]
    jobs += [("w00", 5), ("su3", 7), ("to2", 2), ("w01", 1), ("w10", 3), ("n2t0a", 0), ("n2t0b", 6), ("w11", 4), ("w2", 7),
             ("n2t1a", 2), ("n2t1b", 0), ("n2t2a", 1)]
    jobs += [("lgT", 3), ("lg", 2), ("cum", 5), ("tab", 6)]
    return jobs


PLACE = (1, 3, 2)
GROUPS = NE // 4
BANK, PER_BANK = {}, [0] * 8
for _name, _b in bank_plan():
    assert _name not in BANK
    BANK[_name] = (_b, PER_BANK[_b])
    PER_BANK[_b] += 1
EXPERT_BASE = list(PER_BANK)
EXPERT_TURN = [2, 2, 4, 4, 2, 2, 6, 4]
PER_BANK = [n + GROUPS * k for n, k in zip(PER_BANK, EXPERT_TURN)]

OUTS = [(SEQ, D), (NB * DT, D), (DEPTH, 1, W_A), (DEPTH, 1, CONV_A - 1, W_A), (DEPTH, 1, CONV_B - 1, W_B),
        (DEPTH, 1, NH, HD, HD), (DEPTH, NB, W_A), (DEPTH, NB, CONV_A - 1, W_A),
        (DEPTH, NB, CONV_B - 1, W_B), (DEPTH, NB, NH, HD, HD)]


class Own:

    def __init__(self, eng, sem):
        self.eng, self.sem, self.n = eng, sem, 0

    def __call__(self, ins):
        ins.then_inc(self.sem, 1)
        self.n += 1
        return self.n

    def wait(self, n=None):
        self.eng.wait_ge(self.sem, self.n if n is None else n)


def build(nc, ins, outs):
    (x_prompt, x_sample, st_lru_h, st_lru_conv, st_conv, st_ret, g_mix, g_ffn, g_fin, w_in, p_cw, p_cb,
     w_a, p_ba, w_x, p_bx, p_lam, p_dw, p_db, p_lg, p_lb, p_rg, w_out, w_grp, b_grp, w_exp, b_exp,
     w1, w3, w2, cst) = ins
    (y_prompt, y_sample, o_lru_h, o_lru_conv, o_conv, o_ret, s_lru_h, s_lru_conv, s_conv, s_ret) = outs
    params = [(p_cw, "cw"), (p_cb, "cb"), (p_ba, "ba"), (p_bx, "bx"), (p_lam, "lam"), (p_dw, "dw"),
              (p_db, "db"), (p_lg, "lg"), (p_lb, "lb"), (p_rg, "rg")]

    xn_dram = nc.dram_tensor("xn_scratch", (NT, D), F32, kind="Internal").ap()

    with ExitStack() as ctx:
        def sb(name, shape, dt=F32):
            return ctx.enter_context(nc.sbuf_tensor(name, shape, dt))

        def sem(name):
            return ctx.enter_context(nc.semaphore(name))

        ring = sb("ring", [128, 12, 2048])
        x = sb("x", [128, 3, D])
        uT = sb("uT", [128, KT * NT])
        mixT = sb("mixT", [128, KT, NT])
        rows = sb("rows", [128, 2, D])
        arena = sb("arena", [128, 4096])
        const = sb("const", [128, NCONST])
        qT = sb("qT", [128, 4, NT])
        kT = sb("kT", [128, 4, NT])
        kr = sb("kr", [128, 3, 512])
        v = sb("v", [128, 3, 512])
        sg = sb("sg", [128, 3, 512])
        axp = sb("axp", [128, 2, LA])
        axs = sb("axs", [128, 2, NB, LS])
        glp = sb("glp", [128, 2, LB])
        gls = sb("gls", [128, 2, NB, LT])
        cb = sb("cb", [128, 2 * NT])
        xc = sb("xc", [128, 2 * NT])
        rs = sb("rs", [128, NT])
        tt = sb("tt", [128, 2, 512])
        S1 = sb("S1", [128, 4, HD])
        bd = sb("bd", [128, 2, 2, 128])
        prm = sb("prm", [128, DEPTH, NPRM])
        wr = sb("wr", [128, KT, NG + NE])
        gmx = sb("gmx", [128, DEPTH, KT])
        gff = sb("gff", [128, DEPTH, KT])
        lbias = sb("lbias", [NG + NE, DEPTH])
        ones = sb("ones", [128, 128])
        onesb = sb("onesb", [128, 128], BF16)
        upb = sb("upb", [128, 128], BF16)
        ssq = sb("ssq", [128, 3])
        rms = sb("rms", [128, 3])
        rec = sb("rec", [128, 3])
        eps = sb("eps", [128, 1])
        root = sb("root", [128, 1])
        st_mu = sb("st_mu", [128, NH])
        st_va = sb("st_va", [128, NH])
        hst = sb("hst", [128, 2, 9])
        osumb = sb("osumb", [128, 3, NE], BF16)

        psum = ctx.enter_context(nc.psum_tensor("psum", [128, 8, 512], F32))

        uTk = uT[:, :].rearrange("p (k t) -> p k t", k=KT)
        
        def C(name, n=128):
            o, k = CCOL[name]
            return const[0:n, o:o + k]

        def P_(l, name, i):
            return prm[:, l, PCOL[name] + i:PCOL[name] + i + 1]

        AG, XA = arena[:, 0:576], arena[:, 576:1152]
        RG, RI = arena[:, 1152:1728], arena[:, 1744:2320]
        IG = arena[:, 2320:2896]
        HS = arena[:, 1152:1744].rearrange("p (c n) -> p c n", c=2)
        As = arena[:, 2896:3488].rearrange("p (c n) -> p c n", c=2)
        Bs = arena[:, 3488:4080].rearrange("p (c n) -> p c n", c=2)
        S0 = arena[:, 0:2048].rearrange("p (m b e) -> p m b e", m=4, b=NB)
        xsT = arena[:, 0:2048].rearrange("p (i k s) -> p i k s", i=2, k=KT)
        hsb = arena[:, 2048:2560].rearrange("p (i n) -> p i n", i=2)
        hT = arena[:, 2560:2816].rearrange("p (i f s) -> p i f s", i=2, f=2)
        th = arena[:, 2816:2944].rearrange("p (f s) -> p f s", f=2)
        tm = arena[:, 2944:3072].rearrange("p (f s) -> p f s", f=2)
        ysb = arena[:, 3072:4096]
        back = kT[:, :, :].rearrange("p m t -> p (m t)")[:, 0:2 * NT].rearrange("p (i t) -> p i t", i=2)
        P = rows[:, :, :].rearrange("p c (q m i) -> p c q m i", q=2, m=4)
        Vx = rows[0:32, :, :].rearrange("p i (q b e) -> p i q b e", q=2, b=NB)
        ttf = tt[:, :, :].rearrange("p a n -> p (a n)")
        krf, vf, sgf = (a[:, :, :].rearrange("p a n -> p (a n)") for a in (kr, v, sg))
        onehot = krf[:, 0:192].rearrange("p (t k e) -> p t k e", t=3, k=2)
        rtmp = krf[:, 192:384].rearrange("p (t k e) -> p t k e", t=3, k=2)
        bsum = krf[:, 384:480].rearrange("p (t e) -> p t e", t=3)
        ge = krf[:, 480:576].rearrange("p (t e) -> p t e", t=3)
        ovcmp = krf[:, 576:832]
        lgT = krf[0:NG + NE, 832:832 + NT]
        masked = krf[:, 1152:1248].rearrange("p (t e) -> p t e", t=3)
        used = 0

        def cut(shape, dt=F32):
            nonlocal used
            n = int(np.prod(shape))
            a = sgf[:, used:used + n]
            used += n
            if dt != F32:
                a = a.bitcast(dt)
            return a.rearrange("p (a b) -> p a b", a=shape[0]) if len(shape) == 2 else a

        r_oh, r_ex = cut((3, NG)), cut((3, NG))
        r_gm, r_pt, r_e2 = cut((3,)), cut((3,)), cut((3,))
        r_top, r_idx, r_if = cut((3, 8)), cut((3, 8), U32), cut((3, 2))
        gate, slot, slotu = cut((3, 2)), cut((3, 2)), cut((3, 2), U32)
        slot_in, slot_blk = cut((3, 2)), cut((3, 2))
        sel, selu, gidx, tok = cut((2, NPAIR + OVER)), cut((NPAIR + OVER,), U32), cut((NPAIR + OVER,), U32), cut((3, NPAIR + OVER))
        ovi, ovg = cut((16,), I32), cut((1,), U32)
        ovt = cut((4,))
        ov = cut((4, NE))
        ps_ = rs[:, 0:256].rearrange("p (q m i) -> p q m i", q=2, m=4)
        normed1 = arena[:, 2432:2944]
        osm = arena[:, 2048:2176].rearrange("p (q e) -> p q e", q=2)
        ho = arena[0:9, 2176:2432].rearrange("p (c n) -> p c n", c=2)
        so = gls[0:64, :, :, :].rearrange("p c b t -> p (c b t)")[:, 0:512].rearrange("p (c n) -> p c n", c=4)
        stg = S1[:, :, :]
        slot_oh = vf[:, 0:768].rearrange("p (t k s) -> p t k s", t=3, k=2)
        blk_oh = vf[:, 768:768 + 12 * NBLK].rearrange("p (t k v b) -> p t k v b", t=3, k=2, v=2)
        spare_w1 = uT[:, 0:2048].rearrange("p (k f) -> p k f", k=KT)
        spare_w3 = mixT[:, :, :].rearrange("p k t -> p (k t)")[:, 0:2048].rearrange("p (k f) -> p k f", k=KT)
        spare_w2 = [a[:, :, :].rearrange("p a n -> p (a n)")[:, 0:D] for a in (qT, kr)]
        gfin = ring[:, 0, 0:D]
        prow = [ring[0:NPRM, 10, 0:128], ring[0:NPRM, 10, 128:256]]
        sp_t = ring[:, 11, 0:16]

        def pr(a):
            return a.rearrange("p (c t) -> p c t", c=2)[:, :, 0:SEQ]

        def sa(a):
            return a.rearrange("p (c t) -> p c t", c=2)[:, :, SEQ:NT].rearrange("p c (b t) -> p c b t", b=NB)

        def spr(a):
            return a[:, :, 0:SEQ]

        def ssa(a):
            return a[:, :, SEQ:SCAN].rearrange("p c (b t) -> p c b t", b=NB)

        def bc(a, shape):
            return a.to_broadcast(shape)

        bank_full = [sem(f"bank_full{b}") for b in range(8)]
        bank_free = [sem(f"bank_free{b}") for b in range(8)]
        granule_in = [sem(f"granule_in{g}") for g in range(12)]
        x_in = [sem(f"x_in{t}") for t in range(3)]
        ident_in, const_in, param_in, state_in, s0_in = (sem(f"{n}_in") for n in ("ident", "const", "param", "state", "s0"))
        bd_in, wr_in, g_in, gfin_in = (sem(f"{n}_in") for n in ("bd", "wr", "g", "gfin"))
        rms_ready, rows_ready = sem("rms_ready"), sem("rows_ready")
        xn_out = [sem(f"xn_out{t}") for t in range(3)]
        setup_done, prm_ready, u_lam, xa_ready, la_ready, tau_ready = (
            sem(n) for n in ("setup_done", "prm_ready", "u_lam", "xa_ready", "la_ready", "tau_ready"))
        sample_conv = sem("sample_conv")
        gelu_arg, gelu_ready, glu_ready, conv_ready, ln_arg, ln_sq = (
            sem(n) for n in ("gelu_arg", "gelu_ready", "glu_ready", "conv_ready", "ln_arg", "ln_sq"))
        var_a, ixa_ready, sqrt_tau, ln_tanh, mixb_done, mixa_done = (
            sem(n) for n in ("var_a", "ixa_ready", "sqrt_tau", "ln_tanh", "mixb_done", "mixa_done"))
        qr_ready, kr_ready, kz_ready, sg_tanh, sg_ready, stage_ready, h_ready, so_ready, ho_ready = (
            sem(n) for n in ("qr_ready", "kr_ready", "kz_ready", "sg_tanh", "sg_ready", "stage_ready",
                             "h_ready", "so_ready", "ho_ready"))
        var_ready, gstd_ready, oc_ready, vx_ready, os_norm, os_packed = (
            sem(n) for n in ("var_ready", "gstd_ready", "oc_ready", "vx_ready", "os_norm", "os_packed"))
        ret_out, st_out, conv_out = (sem(n) for n in ("ret_out", "st_out", "conv_out"))
        lg_arg, lg_exp, osum_ready, mark_ready, idx_ready, back_ready = (
            sem(n) for n in ("lg_arg", "lg_exp", "osum_ready", "mark_ready", "idx_ready", "back_ready"))
        e2_arg, e2_ready = sem("e2_arg"), sem("e2_ready")
        gath = [sem(f"gathered{i}") for i in range(2)]
        th_ready, tm_ready, root_in = sem("th_ready"), sem("tm_ready"), sem("root_in")
        eps_ready, slot_ready, slot_marked = sem("eps_ready"), sem("slot_ready"), sem("slot_marked")
        spare13_in, spare2_in, tok_ready = sem("spare13_in"), sem("spare2_in"), sem("tok_ready")
        bd_zero, count_read = sem("bd_zero"), sem("count_read")
        y_out, past_out = sem("y_out"), sem("past_out")
        O = [{n: sem(f"ov{l}_{n}") for n in ("w", "idx", "gath", "xT", "xTe", "h", "he", "hT", "th", "tm", "hTe",
                                             "y", "ye", "back", "acc", "done", "seen")} for l in range(DEPTH)]
        own_dve, own_act, own_pool = sem("own_dve"), sem("own_act"), sem("own_pool")

        def bank(name):
            return psum[:, BANK[name][0], :]

        def full(eng, l, name):
            b, n = BANK[name]
            eng.wait_ge(bank_full[b], l * PER_BANK[b] + n + 1)

        def freed(eng, l, name):
            b, n = BANK[name]
            eng.wait_ge(bank_free[b], l * PER_BANK[b] + n + 1)

        def free(i, name):
            i.then_inc(bank_free[BANK[name][0]], 1)

        def done(i, name):
            i.then_inc(bank_full[BANK[name][0]], 1)

        def expert_job(kind, u, it, l):
            pair, e = 2 * it + u, 4 * it + u
            b, n = {"x0": (0, pair), "x1": (1, pair), "h": (2, e), "hT": (3, e), "y0": (4, pair), "y1": (5, pair),
                    "back0": (6, 3 * pair), "back1": (7, 2 * pair), "back2": (6, 3 * pair + 1), "back3": (7, 2 * pair + 1),
                    "back4": (6, 3 * pair + 2)}[kind]
            return b, l * PER_BANK[b] + EXPERT_BASE[b] + n

        def xfull(eng, kind, u, it, l):
            b, n = expert_job(kind, u, it, l)
            eng.wait_ge(bank_full[b], n + 1)

        def xfreed(eng, kind, u, it, l):
            b, n = expert_job(kind, u, it, l)
            eng.wait_ge(bank_free[b], n + 1)

        def granule(eng, l, g, use):
            per = 1 + (g >= 8) + GROUPS - (g >= 9)
            k = {"in": 0, "out": 1}[use] if isinstance(use, str) else 1 + (g >= 8) + use[0]
            eng.wait_ge(granule_in[g], 16 * (l * per + k + 1))

        def load_states(eng, l):
            eng.dma_start(cb[0:24, 0:256], st_lru_conv[l].rearrange("b k c -> (b k) c")).then_inc(state_in, 16)
            eng.dma_start(cb[24:32, 0:256], st_lru_h[l]).then_inc(state_in, 16)
            for h in range(2):
                eng.dma_start(xc[0:120, 256 * h:256 * h + 256],
                              st_conv[l, 4 * h:4 * h + 4].rearrange("b k c -> (b k) c")).then_inc(state_in, 16)

        def load_gates(eng, l):
            for i, w in enumerate((w_a, w_x)):
                for h in range(4):
                    r = 64 * (h % 2)
                    eng.dma_start(bd[r:r + 64, i, h // 2, r:r + 64], w[l, h]).then_inc(bd_in, 16)

        def load_router(eng, l):
            eng.dma_start(wr[:, :, 0:NG], w_grp[l].rearrange("(p k) g -> p k g", k=KT)).then_inc(wr_in, 16)
            eng.dma_start(wr[:, :, NG:], w_exp[l].rearrange("(p k) g -> p k g", k=KT)).then_inc(wr_in, 16)

        block = ctx.enter_context(nc.Block())

        @block.sync
        def _(sp):
            for t, (o, n) in enumerate(TILES):
                src = x_prompt[0, o:o + n] if t < 2 else x_sample.rearrange("b t d -> (b t) d")
                sp.dma_start(x[0:n, t, :], src).then_inc(x_in[t], 16)
                if t == 0:
                    sp.dma_start(const[:, 0:256], cst[:, 0:256]).then_inc(ident_in, 16)

            def small_loads(g):
                if g == 1:
                    for a, name in params:
                        c, k = PCOL[name], dict(PARAMS)[name]
                        src = a.rearrange("l (c p) -> c l p", p=128) if len(a.shape) == 2 else a.rearrange("l k (c p) -> (k c) l p", p=128)
                        sp.dma_start(ring[c:c + k, 10, 0:128 * DEPTH].rearrange("p (l n) -> p l n", l=DEPTH), src).then_inc(param_in, 16)
                elif g == 2:
                    load_states(sp, 0)
                elif g == 3:
                    sp.dma_start(const[:, 256:], cst[:, 256:]).then_inc(const_in, 16)
                elif g == 4:
                    sp.wait_ge(bd_zero, 1)
                    load_gates(sp, 0)
                elif g == 5:
                    load_router(sp, 0)

            def expert(l, it, u):
                e = 4 * it + u
                sp.dma_start(ring[:, 3 * u, :], w1[l, e].rearrange("(p k) f -> p (k f)", p=128)).then_inc(granule_in[3 * u], 16)
                sp.dma_start(ring[:, 3 * u + 1, :], w3[l, e].rearrange("(p k) f -> p (k f)", p=128)).then_inc(granule_in[3 * u + 1], 16)

            def expert2(l, it, u):
                e = 4 * it + u
                sp.dma_start(ring[:, 3 * u + 2, :].rearrange("p (f d) -> p f d", f=2),
                             w2[l, e].rearrange("(f p) d -> p f d", p=128)).then_inc(granule_in[3 * u + 2], 16)

            for l in range(DEPTH):
                for g in range(12):
                    if l:
                        last_turn = GROUPS - 1 - (g >= 9)
                        if g % 3 == 2:
                            xfull(sp, "y1", g // 6, last_turn, l - 1)
                        else:
                            xfull(sp, "h", g // 3, last_turn, l - 1)
                    elif g == 10:
                        sp.wait_ge(prm_ready, 2)
                    sp.dma_start(ring[:, g, :].rearrange("p (k c) -> p k c", k=KT),
                                 w_in[l].rearrange("(p k) c -> p k c", k=KT)[:, :, 256 * g:256 * g + 256]).then_inc(granule_in[g], 16)
                    if l == 0:
                        small_loads(g)
                full(sp, l, "b5")
                expert(l, 0, 0)
                expert2(l, 0, 0)
                full(sp, l, "k1")
                expert(l, 0, 1)
                expert2(l, 0, 1)
                sp.dma_start(ring[:, 6, :], w1[l, 2].rearrange("(p k) f -> p (k f)", p=128)).then_inc(granule_in[6], 16)
                sp.dma_start(ring[:, 7, :], w3[l, 2].rearrange("(p k) f -> p (k f)", p=128)).then_inc(granule_in[7], 16)
                for q in range(4):
                    full(sp, l, "v1" if q < 2 else "g1")
                    sp.dma_start(ring[:, 8 + q, :].rearrange("p (k c) -> p k c", k=KT),
                                 w_out[l].rearrange("(k p) c -> p k c", p=128)[:, :, 256 * q:256 * q + 256]).then_inc(granule_in[8 + q], 16)
                full(sp, l, "w2")
                expert2(l, 0, 2)
                expert(l, 0, 3)
                expert2(l, 0, 3)
                full(sp, l, "lgT")
                for w_, dst in ((w1, spare_w1), (w3, spare_w3)):
                    sp.dma_start(dst.rearrange("p k f -> p (k f)"), w_[l, NE - 1].rearrange("(p k) f -> p (k f)", p=128)).then_inc(spare13_in, 16)
                for i in range(2):
                    sp.wait_ge(gath[i], 16 * (l * GROUPS + 1))
                for f in range(2):
                    sp.dma_start(spare_w2[f], w2[l, NE - 1, 128 * f:128 * f + 128, :]).then_inc(spare2_in, 16)
                for it in range(1, GROUPS):
                    for pair in range(2):
                        experts = [u for u in (2 * pair, 2 * pair + 1) if 4 * it + u < NE - 1]
                        for u in experts:
                            xfull(sp, "h", u, it - 1, l)
                            expert(l, it, u)
                        xfull(sp, "y1", pair, it - 1, l)
                        for u in experts:
                            expert2(l, it, u)
                sp.wait_ge(idx_ready, l + 1)
                n = sp.value_load(ovi[0:1, 8:9], min_val=0, max_val=OVER)
                xfull(sp, "y1", 0, GROUPS - 1, l)
                with sp.If(n > 0):
                    with sp.Fori(0, n) as j:
                        e = sp.value_load(ovi[0:1, bass.ds(j, 1)], min_val=0, max_val=NE - 1)
                        sp.dma_start(ring[:, 0, :], w1[l, bass.ds(e, 1)].rearrange("o (p k) f -> p (o k f)", p=128)).then_inc(O[l]["w"], 16)
                        sp.dma_start(ring[:, 1, :], w3[l, bass.ds(e, 1)].rearrange("o (p k) f -> p (o k f)", p=128)).then_inc(O[l]["w"], 16)
                        sp.dma_start(ring[:, 2, :].rearrange("p (f d) -> p f d", f=2),
                                     w2[l, bass.ds(e, 1)].rearrange("o (f p) d -> p (o f) d", p=128)).then_inc(O[l]["w"], 16)
                        sp.wait_ge(O[l]["done"], j + 1)
                        sp.sem_inc(O[l]["seen"], 1)
                with sp.Else():
                    sp.nop()
            xfull(sp, "h", 0, GROUPS - 1, DEPTH - 1)
            sp.dma_start(gfin, g_fin.partition_broadcast(128)).then_inc(gfin_in, 16)
            for t, (o, n) in enumerate(TILES):
                sp.wait_ge(rows_ready, 6 * DEPTH + t + 1)
                dst = y_prompt[0, o:o + n] if t < 2 else y_sample.rearrange("b t d -> (b t) d")
                sp.dma_start(dst, x[0:n, t, :]).then_inc(y_out, 16)
            sp.wait_ge(y_out, 48)

        @block.tensor
        def _(pe):
            def start(l, name):
                b, n = BANK[name]
                if l * PER_BANK[b] + n:
                    pe.wait_ge(bank_free[b], l * PER_BANK[b] + n)
                return bank(name)

            ident = C("ident")
            pe.wait_ge(ident_in, 16)

            def transpose(out, in_, n):
                return pe.transpose(out, in_, ident[0:n, 0:n])

            def keep_clock(b, n):
                for _ in range(n):
                    pe.matmul(b[:, 0:128], ident, ident)

            def norm(l, s, t):
                n = TILES[t][1]
                if (s, t) == (0, 0):
                    keep_clock(psum[:, 3, :], WAIT_NORM[min(l, 1)])
                pe.wait_ge(rows_ready, 6 * l + 3 * s + t + 1)
                r = rows[0:n, t % 2, :].rearrange("p (m k) -> p m k", k=KT)
                halves = (("a", 0, 4), ("b", 4, 8)) if t < 2 else (("a", 0, 8),)
                for h, k0, k1 in halves:
                    name = f"n{s + 1}t{t}{h}"
                    b = start(l, name)[:, 0:(k1 - k0) * n].rearrange("p (k t) -> p k t", t=n)
                    for k in range(k0, k1):
                        i = transpose(b[:, k - k0, :], r[:, :, k], n)
                    done(i, name)

            def states(l):
                pe.wait_ge(state_in, 64 * (l + 1))
                b = start(l, "sa")
                for c in range(2):
                    i = transpose(b[:, 32 * c:32 * c + 32], cb[0:32, 128 * c:128 * c + 128], 32)
                done(i, "sa")
                b = start(l, "sc")
                for c in range(2):
                    for h in range(2):
                        i = transpose(b[:, 240 * c + 120 * h:240 * c + 120 * h + 120], xc[0:120, 256 * h + 128 * c:256 * h + 128 * c + 128], 120)
                done(i, "sc")

            for l in range(DEPTH):
                for t in range(3):
                    norm(l, 0, t)

                freed(pe, l, "n1t2a")
                for c in range(8):
                    granule(pe, l, c // 2, "in")
                    b = start(l, f"b{c}")[:, 0:NT]
                    w = ring[:, c // 2, :].rearrange("p (k c) -> p k c", k=KT)
                    for k in range(KT):
                        i = pe.matmul(b, w[:, k, 128 * (c % 2):128 * (c % 2) + 128], uTk[:, k, :], start=k == 0, stop=k == KT - 1)
                    done(i, f"b{c}")
                    if l == 0 and c == 1:
                        pe.wait_ge(param_in, 16 * len(params))
                        for m in range(DEPTH):
                            i = transpose(psum[:, 3, 128 * m:128 * m + NPRM], prow[m], NPRM)
                        i.then_inc(u_lam, 1)
                    if c == 3:
                        states(l)

                def project(name, g, t):
                    for h in range(2):
                        granule(pe, l, g + h, "in")
                    b = start(l, name)
                    if l == 0 and name == "k1":
                        pe.wait_ge(prm_ready, 1)
                    w = ring[:, g:g + 2, :].rearrange("p g (k c) -> p g k c", k=KT)
                    for k in range(KT):
                        i = pe.matmul(b, uTk[:, k, 128 * t:128 * t + 128], w[:, :, k, :], start=k == 0, stop=k == KT - 1)
                    done(i, name)

                def project_samples():
                    for g in range(8, 12):
                        granule(pe, l, g, "in")
                    b = start(l, "s2")
                    for k in range(KT):
                        for h in range(4):
                            w = ring[:, 4 + 2 * h:6 + 2 * h, :].rearrange("p g (k c) -> p g k c", k=KT)
                            i = pe.matmul(b[32 * h:32 * h + 32, :], uTk[:, k, SEQ:NT], w[:, :, k, :], start=k == 0, stop=k == KT - 1,
                                          skip_group_check=True)
                    done(i, "s2")

                def gates(name, which, c):
                    if name == "gr0":
                        pe.wait_ge(bd_in, 16 * 8 * (l + 1))
                        pe.wait_ge(xa_ready, l + 1)
                    b = start(l, name)
                    done(pe.matmul(b[:, 0:NT], bd[:, which, c, :], XA[:, NT * c:NT * c + NT], start=True, stop=True), name)

                def turn(name, t):
                    o, n = TILES[t]
                    src, s, k = (tt[:, 0, :], qr_ready, 3 * l + PLACE[t]) if name[1] == "q" else (kr[:, t, :], kr_ready, 3 * l + PLACE[t])
                    pe.wait_ge(s, k)
                    b = start(l, name)[:, 0:4 * n].rearrange("p (m t) -> p m t", m=4)
                    for m in range(4):
                        i = transpose(b[:, m, :], src[0:n, 128 * m:128 * m + 128], n)
                    done(i, name)

                def inner(c):
                    o, n = TILES[c]
                    freed(pe, l, f"tk{c}")
                    nm = [f"in{c}e", f"in{c}o"] if c < 2 else ["inse", "inso"]
                    b = [start(l, z)[0:n, 0:4 * n].rearrange("p (m t) -> p m t", m=4) for z in nm]
                    for m in range(4):
                        for q in range(2):
                            h = slice(64 * q, 64 * q + 64)
                            i = pe.matmul(b[q][:, m, :], kT[h, m, o:o + n], qT[h, m, o:o + n], start=True, stop=True)
                            if m == 3:
                                done(i, nm[q])

                def state(c):
                    freed(pe, l, f"v{c}")
                    pe.wait_ge(kz_ready, 3 * l + PLACE[c])
                    b = start(l, f"S{c}")[:, 0:256].rearrange("p (m e) -> p m e", m=4)
                    for m in range(4):
                        for q in range(2):
                            h = 64 * (2 * m + q)
                            i = pe.matmul(b[64 * q:64 * q + 64, m, :], kr[:, c, h:h + 64], v[:, c, h:h + 64], start=True, stop=True,
                                          skip_group_check=True)
                    done(i, f"S{c}")

                def inside(c):
                    freed(pe, l, f"in{c}e")
                    freed(pe, l, f"in{c}o")
                    freed(pe, l, f"v{c}")
                    b = start(l, f"o{c}")
                    for m in range(4):
                        for q in range(2):
                            h = 64 * (2 * m + q)
                            i = pe.matmul(b[:, h:h + 64], P[:, c, q, m, :], v[:, c, h:h + 64], start=True, stop=True)
                    done(i, f"o{c}")

                def mean(name):
                    b = start(l, name)
                    for c in range(2):
                        i = pe.matmul(b[:, 0:NT], ones[:, :], cb[:, NT * c:NT * c + NT], start=c == 0, stop=c == 1)
                    done(i, name)

                def turn_out(t):
                    o, n = TILES[t]
                    pe.wait_ge(oc_ready, 3 * l + t + 1)
                    b = start(l, f"to{t}")[:, 0:4 * n].rearrange("p (m t) -> p m t", m=4)
                    for m in range(4):
                        i = transpose(b[:, m, :], sg[0:n, t, 128 * m:128 * m + 128], n)
                    done(i, f"to{t}")

                def new_states(m):
                    pe.wait_ge(vx_ready, 4 * l + m + 1)
                    b = start(l, f"su{m}")
                    for q in range(2):
                        h = 64 * (2 * m + q)
                        i = pe.matmul(b[64 * q:64 * q + 64, :], kr[0:32, 2, h:h + 64], Vx[:, m % 2, q, :, :], start=True, stop=True,
                                      skip_group_check=True)
                    done(i, f"su{m}")

                project("q0", 4, 0)
                project("k0", 6, 0)
                project_samples()
                gates("gr0", 0, 0)
                gates("gi0", 1, 0)
                gates("gr1", 0, 1)
                gates("gi1", 1, 1)
                turn("tq0", 0)
                turn("tk0", 0)
                project("q1", 4, 1)
                turn("tq2", 2)
                turn("tk2", 2)
                pe.wait_ge(stage_ready, l + 1)
                b = start(l, "st")
                for c in range(4):
                    i = transpose(b[0:64, 128 * c:128 * c + 128], stg[:, c, :], 128)
                done(i, "st")
                project("k1", 6, 1)
                inner(0)
                project("v0", 8, 0)
                turn("tq1", 1)
                state(0)
                turn("tk1", 1)
                inner(2)
                project("v1", 8, 1)
                inner(1)
                inside(0)
                freed(pe, l, "S0")
                b = [start(l, z)[:, 0:256].rearrange("p (m e) -> p m e", m=4) for z in ("x1e", "x1o")]
                for m in range(4):
                    for q in range(2):
                        h = slice(64 * q, 64 * q + 64)
                        i = pe.matmul(b[q][:, m, :], qT[h, m, 128:256], S1[h, m, :], start=True, stop=True)
                        if m == 3:
                            done(i, ("x1e", "x1o")[q])
                project("g0", 10, 0)
                inside(1)
                state(1)
                pe.wait_ge(conv_ready, l + 1)
                mean("lnm")
                pe.wait_ge(s0_in, 128 * (l + 1))
                b = [start(l, z) for z in ("xse", "xso")]
                for m in range(4):
                    for q in range(2):
                        h = slice(64 * q, 64 * q + 64)
                        i = pe.matmul(b[q][32 * m:32 * m + 32, :], qT[h, m, SEQ:NT], S0[h, m, :, :], start=True, stop=True,
                                      skip_group_check=True)
                        if m == 3:
                            done(i, ("xse", "xso")[q])
                freed(pe, l, "inse")
                freed(pe, l, "inso")
                freed(pe, l, "s2")
                b = start(l, "os")[:, 0:128].rearrange("p (q e) -> p q e", q=2)
                for m in range(4):
                    for q in range(2):
                        h = 64 * (2 * m + q)
                        i = pe.matmul(b[32 * m:32 * m + 32, q, :], ps_[0:32, q, m, :], v[0:32, 2, h:h + 64], start=True, stop=True,
                                      skip_group_check=True)
                done(i, "os")
                pe.wait_ge(kz_ready, 3 * l + PLACE[2])
                new_states(0)
                pe.wait_ge(ln_sq, l + 1)
                mean("lnv")
                project("g1", 10, 1)
                pe.wait_ge(h_ready, l + 1)
                b = start(l, "ht")
                for c in range(2):
                    i = transpose(b[0:9, 128 * c:128 * c + 128], hst[:, c, :], 128)
                done(i, "ht")
                new_states(1)
                turn_out(0)
                new_states(2)
                turn_out(1)

                pe.wait_ge(mixa_done, l + 1)
                for t in range(2):
                    freed(pe, l, f"to{t}")
                    for h in range(2):
                        if (t, h) == (0, 1):
                            new_states(3)
                            turn_out(2)
                        if (t, h) == (1, 1):
                            norm(l, 1, 0)
                        for g in (8 + 2 * h, 9 + 2 * h):
                            granule(pe, l, g, "out")
                        w = ring[:, 8 + 2 * h:10 + 2 * h, :].rearrange("p g (k c) -> p g k c", k=KT)
                        b = start(l, f"w{t}{h}")
                        for n_, k in enumerate((0, 1, 4, 5, 6, 7, 2, 3)):
                            if (t, h, k) == (0, 0, 2):
                                pe.wait_ge(mixb_done, l + 1)
                            i = pe.matmul(b, mixT[:, k, 128 * t:128 * t + 128], w[:, :, k, :], start=n_ == 0, stop=n_ == KT - 1)
                        done(i, f"w{t}{h}")
                freed(pe, l, "to2")
                b = start(l, "w2")
                for k in range(KT):
                    for q in range(4):
                        w = ring[:, 8 + q, :].rearrange("p (k c) -> p k c", k=KT)
                        i = pe.matmul(b[32 * q:32 * q + 32, 0:256], mixT[:, k, SEQ:NT], w[:, k, :], start=k == 0,
                                      stop=k == KT - 1, skip_group_check=True)
                done(i, "w2")
                norm(l, 1, 1)

                def logits(o, n):
                    for k in range(KT):
                        i = pe.matmul(bank("lgT")[0:NG + NE, o:o + n], wr[:, k, :], uTk[:, k, o:o + n], start=k == 0, stop=k == KT - 1)
                    return i

                pe.wait_ge(wr_in, 32 * (l + 1))
                freed(pe, l, "n2t0b")
                start(l, "lgT")
                logits(0, 128)
                norm(l, 1, 2)
                freed(pe, l, "n2t2a")
                done(logits(128, NT - 128), "lgT")
                freed(pe, l, "lgT")
                b = start(l, "lg")[:, 0:3 * (NG + NE)].rearrange("p (t e) -> p t e", t=3)
                for t, (o, n) in enumerate(TILES):
                    i = transpose(b[0:n, t, :], lgT[:, o:o + n], NG + NE)
                done(i, "lg")
                b = start(l, "cum")
                keep_clock(b, WAIT_CHOICE)
                pe.wait_ge(osum_ready, l + 1)
                b = b[:, 0:128].rearrange("p (t e) -> p t e", t=4)
                for t in range(4):
                    for s in range(min(t, 2) + 1):
                        n = TILES[s][1]
                        i = pe.matmul(b[:, t, :], (upb if s == t else onesb)[0:n, :], osumb[0:n, s, :], start=s == 0,
                                      stop=s == min(t, 2))
                done(i, "cum")
                b = start(l, "tab")
                keep_clock(b, WAIT_MARKS)
                b = b[:, 0:2 * NBLK]
                for t, (o, n) in enumerate(TILES):
                    pe.wait_ge(mark_ready, 3 * l + t + 1)
                    pe.wait_ge(slot_marked, 3 * l + t + 1)
                    for k in range(2):
                        i = pe.matmul(b, slot_oh[0:n, t, k, :], blk_oh[0:n, t, k, :, :], start=(t, k) == (0, 0), stop=(t, k) == (2, 1))
                done(i, "tab")

                def begin(kind, u, it):
                    b, n = expert_job(kind, u, it, l)
                    pe.wait_ge(bank_free[b], n)
                    return psum[:, b, :]

                def finish(i, kind, u):
                    i.then_inc(bank_full[expert_job(kind, u, 0, l)[0]], 1)

                def tokens(g2, it):
                    par = g2 % 2
                    pe.wait_ge(gath[par], 16 * (l * GROUPS + it + g2 // 2 + 1))
                    for kind, k0 in (("x0", 0), ("x1", 4)):
                        b = begin(kind, g2, it).rearrange("p (k s) -> p k s", k=4)
                        r = rows[:, par, :].rearrange("p (m k) -> p m k", k=KT)
                        for k in range(4):
                            i = transpose(b[:, k, :], r[:, :, k0 + k], 128)
                        finish(i, kind, g2)

                def up(u, it, spare=False):
                    if spare:
                        pe.wait_ge(spare13_in, 32 * (l + 1))
                    else:
                        granule(pe, l, 3 * u, (it,))
                        granule(pe, l, 3 * u + 1, (it,))
                    if u % 2 == 0:
                        xfreed(pe, "x1", u // 2, it, l)
                    b = begin("h", u, it)
                    w = [(spare_w1, spare_w3)[j] if spare else ring[:, 3 * u + j, :].rearrange("p (k f) -> p k f", k=KT) for j in range(2)]
                    s = slice(SLOTS * (u % 2), SLOTS * (u % 2) + SLOTS)
                    for k in range(KT):
                        for j in range(2):
                            i = pe.matmul(b[64 * j:64 * j + 64, 0:FE], xsT[:, u // 2, k, s], w[j][:, k, :], start=k == 0,
                                          stop=k == KT - 1, skip_group_check=True)
                    finish(i, "h", u)

                def turn_h(u, it):
                    xfreed(pe, "h", u, it, l)
                    b = begin("hT", u, it)
                    for f in range(2):
                        i = transpose(b[:, 128 * f:128 * f + 128], hsb[:, u % 2, 128 * f:128 * f + 128], 128)
                    finish(i, "hT", u)

                def down(pair, it, spare=False):
                    for u in (2 * pair, 2 * pair + 1):
                        if spare and u == 3:
                            pe.wait_ge(spare2_in, 32 * (l + 1))
                        else:
                            granule(pe, l, 3 * u + 2, (it,))
                    xfreed(pe, "hT", 2 * pair + 1, it, l)
                    for j in range(2):
                        b = begin(f"y{j}", pair, it)
                        for f in range(2):
                            for q in range(2):
                                w = ring[:, 6 * pair + 3 * q + 2, 1024 * f:1024 * f + 1024]
                                if spare and q:
                                    w = spare_w2[f]
                                i = pe.matmul(b[64 * q:64 * q + 64, :], hT[:, q, f, :], w[:, 512 * j:512 * j + 512], start=f == 0,
                                              stop=f == 1, skip_group_check=True)
                        finish(i, f"y{j}", pair)

                def give_back(pair, it, parts):
                    if 0 in parts:
                        pe.wait_ge(back_ready, l * NPAIR + 2 * it + pair + 1)
                    for a in parts:
                        if a < 2:
                            xfreed(pe, f"y{a % 2}", pair, it, l)
                        b = begin(f"back{a}", pair, it)
                        if a < 4:
                            i = pe.matmul(b, back[:, pair, 128 * (a // 2):128 * (a // 2) + 128], ysb[:, 512 * (a % 2):512 * (a % 2) + 512],
                                          start=True, stop=True)
                        else:
                            for j in range(2):
                                i = pe.matmul(b[32 * j:32 * j + 32, :], back[:, pair, SEQ:NT], ysb[:, 512 * j:512 * j + 512],
                                              start=True, stop=True, skip_group_check=True)
                        finish(i, f"back{a}", pair)

                def experts4(it, first=False, last=False):
                    for pair in range(2):
                        before = (0, it) if pair else (1, it - 1)
                        up(2 * pair, it)
                        if pair or not first:
                            give_back(*before, (0, 1))
                        turn_h(2 * pair, it)
                        up(2 * pair + 1, it, spare=last and pair == 1)
                        if pair or not first:
                            give_back(*before, (2, 3))
                        turn_h(2 * pair + 1, it)
                        if pair or not first:
                            give_back(*before, (4,))
                        if not (pair and last):
                            tokens(pair + 1, it)
                        down(pair, it, spare=last and pair == 1)

                keep_clock(begin("x0", 0, 0), WAIT_ROWS)
                tokens(0, 0)
                experts4(0, first=True)
                with pe.Fori(1, GROUPS - 1) as it:
                    experts4(it)
                experts4(GROUPS - 1, last=True)
                give_back(1, GROUPS - 1, (0, 1, 2, 3, 4))

                o = O[l]
                pe.wait_ge(idx_ready, l + 1)
                n = pe.value_load(ovi[0:1, 8:9], min_val=0, max_val=OVER)
                for kind, u in (("x0", 1), ("x1", 1), ("h", 3), ("hT", 3), ("y0", 1), ("y1", 1), ("back3", 1), ("back4", 1)):
                    xfreed(pe, kind, u, GROUPS - 1, l)
                with pe.If(n > 0):
                    with pe.Fori(0, n) as j:
                        pe.wait_ge(o["gath"], 16 * j + 16)
                        pe.sem_inc(o["seen"], 1)
                        r = rows[0:SLOTS, 0, :].rearrange("p (m k) -> p m k", k=KT)
                        for k in range(KT):
                            i = transpose(psum[:, 0, SLOTS * k:SLOTS * k + SLOTS], r[:, :, k], SLOTS)
                        i.then_inc(o["xT"], 1)
                        pe.wait_ge(o["xTe"], j + 1)
                        pe.wait_ge(o["w"], 48 * j + 48)
                        for k in range(KT):
                            for q in range(2):
                                w = ring[:, q, :].rearrange("p (k f) -> p k f", k=KT)
                                i = pe.matmul(psum[64 * q:64 * q + 64, 2, 0:FE], xsT[:, 0, k, 0:SLOTS], w[:, k, :], start=k == 0,
                                              stop=k == KT - 1, skip_group_check=True)
                        i.then_inc(o["h"], 1)
                        pe.wait_ge(o["he"], j + 1)
                        for f in range(2):
                            i = transpose(psum[:, 3, 128 * f:128 * f + 128], hsb[:, 0, 128 * f:128 * f + 128], 128)
                        i.then_inc(o["hT"], 1)
                        pe.wait_ge(o["hTe"], j + 1)
                        w = ring[:, 2, :].rearrange("p (f d) -> p f d", f=2)
                        for q in range(2):
                            for f in range(2):
                                i = pe.matmul(psum[0:SLOTS, 4 + q, :], hT[:, 0, f, :], w[:, f, 512 * q:512 * q + 512],
                                              start=f == 0, stop=f == 1)
                        i.then_inc(o["y"], 1)
                        pe.wait_ge(o["ye"], j + 1)
                        pe.wait_ge(o["back"], j + 1)
                        for t, (o_, n_) in enumerate(TILES):
                            for q in range(2):
                                b = psum[:, 6 + q, :] if t == 0 else psum[:, q, :] if t == 1 else psum[:, 2 + q, :]
                                i = pe.matmul(b[0:n_, :], back[0:SLOTS, 0, o_:o_ + n_], ysb[0:SLOTS, 512 * q:512 * q + 512], start=True, stop=True)
                        i.then_inc(o["acc"], 1)
                        pe.wait_ge(o["done"], j + 1)
                with pe.Else():
                    pe.nop()

        @block.vector
        def _(dve):
            own = Own(dve, own_dve)

            def do(i):
                own(i)
                own.wait()

            T = dve.tensor_tensor
            S = dve.tensor_scalar
            STT = dve.scalar_tensor_tensor

            dve.memset(eps[:, :], EPS).then_inc(eps_ready, 1)
            own(dve.memset(ones[:, :], 1.0 / W_B))
            own(dve.memset(onesb[:, :], 1.0))
            own(dve.memset(axp[:, :, 0:3], 0.0))
            own(dve.memset(glp[:, :, 0:30], 0.0))
            own.wait()
            dve.wait_ge(ident_in, 16)
            dve.tensor_copy(upb[:, :], C("upper")).then_inc(setup_done, 1)

            def parameters():
                dve.wait_ge(u_lam, 1)
                do(dve.tensor_copy(prm[:, :, :], psum[:, 3, 0:256].rearrange("p (l n) -> p l n", l=2)[:, :, 0:NPRM]))
                own(S(prm[:, :, PCOL["ba"]:PCOL["ba"] + 4], prm[:, :, PCOL["ba"]:PCOL["ba"] + 4], 0.5, None, ALU.mult))
                own(S(prm[:, :, PCOL["lg"]:PCOL["lg"] + 8], prm[:, :, PCOL["lg"]:PCOL["lg"] + 8], 0.5, None, ALU.mult))
                lam = prm[:, :, PCOL["lam"]:PCOL["lam"] + 2]
                z, az, u, w = (sp_t[:, 4 * i:4 * i + 4].rearrange("p (l c) -> p l c", l=2) for i in range(4))
                do(S(z, lam, -1.0, None, ALU.mult))
                T(az, lam, z, ALU.max).then_inc(prm_ready, 1)
                dve.wait_ge(u_lam, 2)
                do(S(w, u, 1.0, None, ALU.add))
                S(lam, w, -1.0, None, ALU.add).then_inc(la_ready, 1)
                dve.wait_ge(u_lam, 3)
                dve.wait_ge(la_ready, 1)
                do(T(az, az, u, ALU.mult))
                do(S(w, lam, 0.0, None, ALU.is_equal))
                do(T(u, u, w, ALU.mult))
                do(S(lam, lam, 1.0e-30, None, ALU.max))
                do(dve.reciprocal(w, lam))
                do(T(az, az, w, ALU.mult))
                do(T(az, az, u, ALU.add))
                do(S(z, z, 0.0, None, ALU.max))
                do(T(az, az, z, ALU.add))
                S(lam, az, -2.0, None, ALU.mult).then_inc(prm_ready, 1)
                dve.wait_ge(prm_ready, 2)

            def scaled(l, s, t):
                n = TILES[t][1]
                dve.wait_ge(rms_ready, 6 * l + 3 * s + t + 1)
                do(dve.reciprocal(rec[0:n, t:t + 1], rms[0:n, t:t + 1]))
                if t == 2:
                    full(dve, l, f"n{s + 1}t0b")
                    if s:
                        dve.wait_ge(xn_out[0], 16 * (l + 1))
                S(rows[0:n, t % 2, :], x[0:n, t, :], rec[0:n, t:t + 1], None, ALU.mult).then_inc(rows_ready, 1)

            def turned(l, s, t):
                g = (gmx, gff)[s]
                o, n = TILES[t]
                for h, k0, k1 in (("a", 0, 4), ("b", 4, 8)) if t < 2 else (("a", 0, 8),):
                    name = f"n{s + 1}t{t}{h}"
                    full(dve, l, name)
                    free(T(uTk[:, k0:k1, o:o + n], bank(name)[:, 0:(k1 - k0) * n].rearrange("p (k t) -> p k t", t=n),
                           bc(g[:, l, k0:k1].unsqueeze(2), [128, k1 - k0, n]), ALU.mult), name)

            for l in range(DEPTH):
                if l == 0:
                    dve.wait_ge(g_in, 16 * 4)
                scaled(l, 0, 0)
                scaled(l, 0, 1)
                turned(l, 0, 0)
                scaled(l, 0, 2)
                turned(l, 0, 1)
                turned(l, 0, 2)
                if l == 0:
                    parameters()
                    dve.wait_ge(const_in, 16)

                full(dve, l, "sa")
                sa_b = bank("sa")[:, 0:64].rearrange("p (c n) -> p c n", c=2)
                own(dve.tensor_copy(axs[:, :, :, 0:3], sa_b[:, :, 0:24].rearrange("p c (b k) -> p c b k", b=NB)))
                own(dve.memset(ssa(As)[:, :, :, 0], 0.0))
                free(dve.tensor_copy(ssa(Bs)[:, :, :, 0], sa_b[:, :, 24:32]), "sa")
                full(dve, l, "sc")
                if l:
                    dve.wait_ge(conv_out, 16 * 11 * l)
                free(dve.tensor_copy(gls[:, :, :, 0:30], bank("sc")[:, 0:480].rearrange("p (c b k) -> p c b k", c=2, b=NB)), "sc")

                freed(dve, l, "b3")
                freed(dve, l, "sa")
                last = [None] * 4
                for k in range(CONV_A):
                    for c in range(2):
                        w = P_(l, "cw", 2 * k + c)
                        for i, (src, dst) in enumerate((
                                (axp[:, c, k:k + SEQ], pr(XA)[:, c, :]),
                                (axs[:, c, :, k:k + DT], sa(XA)[:, c, :, :]))):
                            if k == 0:
                                ins_ = S(dst, src, w, P_(l, "cb", c), ALU.mult, ALU.add)
                            else:
                                own.wait(last[2 * c + i])
                                ins_ = STT(dst, src, w, dst, ALU.mult, ALU.add)
                            if k < CONV_A - 1:
                                last[2 * c + i] = own(ins_)
                            elif (c, i) == (1, 1):
                                ins_.then_inc(xa_ready, 1)
                            else:
                                own(ins_)

                freed(dve, l, "b7")
                freed(dve, l, "sc")
                STT(glp[:, :, 30:LB], pr(xc[:, :]), 1.0, pr(cb[:, :]), ALU.add, ALU.mult).then_inc(glu_ready, 1)
                dve.wait_ge(glu_ready, 2 * l + 1)
                for c in range(2):
                    i = STT(gls[:, c, :, 30:LT], sa(xc[:, :])[:, c], 1.0, sa(cb[:, :])[:, c], ALU.add, ALU.mult)
                    if c:
                        i.then_inc(glu_ready, 1)
                    else:
                        own(i)
                dve.wait_ge(glu_ready, 2 * l + 2)

                chain = [None, None]

                def taps(k0, k1):
                    for k in range(k0, k1):
                        for c in range(2):
                            w = P_(l, "dw", 2 * k + c)
                            dst = pr(cb[:, :])[:, c, :]
                            if k == 0:
                                chain[c] = own(S(dst, glp[:, c, k:k + SEQ], w, P_(l, "db", c), ALU.mult, ALU.add))
                            else:
                                own.wait(chain[c])
                                chain[c] = own(STT(dst, glp[:, c, k:k + SEQ], w, dst, ALU.mult, ALU.add))

                def taps_samples(c):
                    pw = ttf[:, 0:NB * DT * CONV_B].rearrange("p (b t k) -> p b t k", b=NB, t=DT)
                    a = PCOL["dw"] + c
                    w = prm[:, l, a:a + 2 * CONV_B - 1:2]
                    for t in range(DT):
                        own(T(pw[:, :, t, :], gls[:, c, :, t:t + CONV_B], bc(w.unsqueeze(1), [128, NB, CONV_B]), ALU.mult))
                    own.wait()
                    do(dve.tensor_reduce(sa(cb[:, :])[:, c], pw, AX, ALU.add))
                    own(S(sa(cb[:, :])[:, c], sa(cb[:, :])[:, c], P_(l, "db", c), None, ALU.add))

                taps_samples(0)
                taps_samples(1)
                own.wait()
                dve.sem_inc(sample_conv, 1)

                def rotate(name, t, out, lo, cos, sin, n, last_sem):
                    b = bank(name)[lo:lo + n, :].rearrange("p (h s i) -> p h s i", h=NH, s=2)
                    c3 = C(cos, n)[:, 32 * t:32 * t + 32].unsqueeze(1)
                    s3 = C(sin, n)[:, 32 * t:32 * t + 32].unsqueeze(1)
                    o4 = out.rearrange("p (h s i) -> p h s i", h=NH, s=2)
                    x4 = tt[0:n, 1, :].rearrange("p (h s i) -> p h s i", h=NH, s=2)
                    full(dve, l, name)
                    own(T(o4, b, bc(c3.unsqueeze(1), [n, NH, 2, 32]), ALU.mult))
                    own(T(x4[:, :, 0, :], b[:, :, 1, :], bc(s3, [n, NH, 32]), ALU.mult))
                    i = T(x4[:, :, 1, :], b[:, :, 0, :], bc(s3, [n, NH, 32]), ALU.mult)
                    if name != "s2":
                        free(i, name)
                        freed(dve, l, name)
                    else:
                        own(i)
                    own.wait()
                    own(T(o4[:, :, 0, :], o4[:, :, 0, :], x4[:, :, 0, :], ALU.subtract))
                    T(o4[:, :, 1, :], o4[:, :, 1, :], x4[:, :, 1, :], ALU.add).then_inc(last_sem, 1)
                    own.wait()

                def rotate_q(t, name="", lo=0):
                    if t:
                        full(dve, l, ("", "tq2", "tq0")[t])
                    rotate(name or f"q{t}", t, tt[0:TILES[t][1], 0, :], lo, "cos", "sin", TILES[t][1], qr_ready)
                    dve.wait_ge(qr_ready, 3 * l + PLACE[t])

                def rotate_k(t, name="", lo=0):
                    rotate(name or f"k{t}", t, kr[0:TILES[t][1], t, :], lo, "cos", "sin", TILES[t][1], kr_ready)
                    dve.wait_ge(kr_ready, 3 * l + PLACE[t])

                def gate_v(t):
                    n = TILES[t][1]
                    name = f"g{t}" if t < 2 else "s2"
                    lo = 0 if t < 2 else 96
                    dve.wait_ge(sg_tanh, 3 * l + (2, 3, 1)[t])
                    free(STT(sg[0:n, t, :], sg[0:n, t, :], 1.0, bank(name)[lo:lo + n, :], ALU.add, ALU.mult), name)

                def mask_scores(c):
                    for q in range(2):
                        name = f"in{c if c < 2 else 's'}{'eo'[q]}"
                        full(dve, l, name)
                        if c < 2:
                            i = T(P[:, c, q].rearrange("p m i -> p (m i)"), bank(name), C("dmat")[:, 512 * q:512 * q + 512], ALU.mult)
                        else:
                            i = T(ps_[0:32, q].rearrange("p m i -> p (m i)"), bank(name)[0:32, 0:128],
                                  C("dmats", 32)[:, 128 * q:128 * q + 128], ALU.mult)
                        free(i, name)

                def group_norm(src, n, H, t, dst=None):
                    mu, va = st_mu[0:n, 0:H], st_va[0:n, 0:H]
                    sq = tt[0:n, 1, 0:H * HD].rearrange("p (h e) -> p h e", h=H)
                    do(dve.tensor_reduce(mu, src, AX, ALU.add))
                    do(S(mu, mu, 1.0 / HD, None, ALU.mult))
                    do(T(src, src, bc(mu.unsqueeze(2), [n, H, HD]), ALU.subtract))
                    do(T(sq, src, src, ALU.mult))
                    dve.tensor_reduce(va, sq, AX, ALU.add).then_inc(var_ready, 1)
                    dve.wait_ge(gstd_ready, 3 * l + t + 1)
                    do(dve.reciprocal(va, va))
                    do(T(src if dst is None else dst, src, bc(va.unsqueeze(2), [n, H, HD]), ALU.mult))

                def gated(t, src):
                    n = TILES[t][1]
                    freed(dve, l, f"g{t}" if t < 2 else "s2")
                    T(sg[0:n, t, :], sg[0:n, t, :], src, ALU.mult).then_inc(oc_ready, 1)
                    dve.wait_ge(oc_ready, 3 * l + t + 1)

                rotate_q(0)
                rotate_k(0)
                taps(0, 9)
                rotate_q(2, "s2", 0)
                rotate_k(2, "s2", 32)
                gate_v(2)
                freed(dve, l, "gr0")
                own(S(RG[:, 0:NT], RG[:, 0:NT], 1.0, P_(l, "lam", 0), ALU.add, ALU.mult))
                freed(dve, l, "gr1")
                freed(dve, l, "gi0")
                freed(dve, l, "gi1")
                S(RG[:, NT:], RG[:, NT:], 1.0, P_(l, "lam", 1), ALU.add, ALU.mult).then_inc(la_ready, 1)
                STT(IG, IG, 1.0, XA, ALU.add, ALU.mult).then_inc(ixa_ready, 1)
                taps(9, 12)
                rotate_q(1)
                dve.wait_ge(tau_ready, l + 1)
                STT(RI, RI, 1.0, RG, ALU.add, ALU.mult).then_inc(var_a, 1)
                rotate_k(1)
                mask_scores(0)
                dve.wait_ge(sqrt_tau, l + 1)
                dve.wait_ge(ixa_ready, l + 1)
                own(T(spr(Bs), pr(IG), pr(XA), ALU.mult))
                for c in range(2):
                    own(T(ssa(Bs)[:, c, :, 1:5], sa(IG)[:, c], sa(XA)[:, c], ALU.mult))
                own.wait()
                for c in range(2):
                    own(dve.tensor_tensor_scan(HS[:, c, :], As[:, c, :], Bs[:, c, :], 0.0, ALU.mult, ALU.add))
                dve.wait_ge(gelu_ready, l + 1)
                m0 = mixT[:, 0:2, :].rearrange("p c t -> p (c t)")
                do(STT(m0, m0, 1.0, AG, ALU.add, ALU.mult))
                own(STT(spr(mixT[:, 0:2, :]), spr(mixT[:, 0:2, :]), 0.5, spr(HS), ALU.mult, ALU.mult))
                for c in range(2):
                    ms = mixT[:, c, SEQ:NT].rearrange("p (b t) -> p b t", b=NB)
                    own(STT(ms, ms, 0.5, ssa(HS)[:, c, :, 1:5], ALU.mult, ALU.mult))
                own(dve.tensor_copy(hst[:, :, 0:1], HS[:, :, SEQ - 1:SEQ]))
                own.wait()
                dve.tensor_copy(hst[:, :, 1:9], ssa(HS)[:, :, :, 4]).then_inc(h_ready, 1)
                dve.wait_ge(h_ready, l + 1)
                own.wait()
                dve.sem_inc(mixa_done, 1)
                taps(12, 15)
                full(dve, l, "S0")
                if l:
                    dve.wait_ge(ret_out, 32 * l)
                free(dve.tensor_copy(S1[:, :, :], bank("S0")[:, 0:256].rearrange("p (m e) -> p m e", m=4)), "S0")
                mask_scores(2)
                taps(15, 24)
                mask_scores(1)
                full(dve, l, "tq1")
                full(dve, l, "o0")
                free(dve.tensor_copy(tt[:, 0, :], bank("o0")), "o0")
                freed(dve, l, "o0")
                group_norm(tt[:, 0, :].rearrange("p (h e) -> p h e", h=NH), 128, NH, 0)
                taps(24, CONV_B)
                own.wait()
                dve.sem_inc(conv_ready, 1)
                gate_v(0)
                gated(0, tt[:, 0, :])

                t3 = tt[:, 0, :].rearrange("p (m q e) -> p m q e", m=4, q=2)
                for q in range(2):
                    name = ("x1e", "x1o")[q]
                    full(dve, l, name)
                    xi = C("xi").rearrange("p (m q) -> p m q", q=2)[:, :, q]
                    free(T(t3[:, :, q, :], bank(name)[:, 0:256].rearrange("p (m e) -> p m e", m=4),
                           bc(xi.unsqueeze(2), [128, 4, HD]), ALU.mult), name)
                    freed(dve, l, name)
                full(dve, l, "o1")
                free(T(tt[:, 0, :], tt[:, 0, :], bank("o1"), ALU.add), "o1")
                freed(dve, l, "o1")
                full(dve, l, "lnm")
                for c in range(2):
                    i = T(xc[:, NT * c:NT * c + NT], cb[:, NT * c:NT * c + NT], bank("lnm")[:, 0:NT], ALU.subtract)
                    free(i, "lnm") if c else own(i)
                group_norm(tt[:, 0, :].rearrange("p (h e) -> p h e", h=NH), 128, NH, 1, normed1.rearrange("p (h e) -> p h e", h=NH))
                do(T(S1[:, :, :], S1[:, :, :], bc(C("gch").unsqueeze(2), [128, 4, HD]), ALU.mult))
                full(dve, l, "S1")
                free(T(S1[:, :, :], S1[:, :, :], bank("S1")[:, 0:256].rearrange("p (m e) -> p m e", m=4), ALU.add), "S1")
                for q in range(2):
                    name = ("xse", "xso")[q]
                    full(dve, l, name)
                    free(T(tt[:, q, :].rearrange("p (b e) -> p b e", b=NB), bank(name).rearrange("p (b e) -> p b e", b=NB),
                           bc(C("cmask")[:, 8 * q:8 * q + 8].unsqueeze(2), [128, NB, HD]), ALU.mult), name)
                    freed(dve, l, name)
                for q in range(2):
                    own(dve.tensor_reduce(osm[:, q, :], tt[:, q, :].rearrange("p (b e) -> p e b", b=NB), AX, ALU.add))
                own.wait()
                full(dve, l, "os")
                free(T(osm[:, :, :], osm[:, :, :], bank("os")[:, 0:128].rearrange("p (q e) -> p q e", q=2), ALU.add), "os")
                freed(dve, l, "os")
                def turned_out(t):
                    o, n = TILES[t]
                    name = f"to{t}"
                    full(dve, l, name)
                    free(T(mixT[:, 4:8, o:o + n], bank(name)[:, 0:4 * n].rearrange("p (m t) -> p m t", m=4),
                           bc(prm[:, l, PCOL["rg"]:PCOL["rg"] + 4].unsqueeze(2), [128, 4, n]), ALU.mult), name)

                group_norm(osm[:, :, :], 128, 2, 2)
                dve.sem_inc(os_norm, 1)
                gate_v(1)
                gated(1, normed1)
                turned_out(0)
                freed(dve, l, "lnv")
                do(dve.reciprocal(rs[:, :], rs[:, :]))
                do(T(xc[:, :].rearrange("p (c t) -> p c t", c=2), xc[:, :].rearrange("p (c t) -> p c t", c=2),
                     bc(rs[:, :].unsqueeze(1), [128, 2, NT]), ALU.mult))
                for c in range(2):
                    S(xc[:, NT * c:NT * c + NT], xc[:, NT * c:NT * c + NT], P_(l, "lg", c), P_(l, "lb", c), ALU.mult, ALU.add).then_inc(ln_arg, 1)

                turned_out(1)
                dve.wait_ge(os_packed, l + 1)
                gated(2, tt[0:32, 0, :])
                dve.wait_ge(ln_tanh, l + 1)
                STT(mixT[:, 2:4, :].rearrange("p c t -> p (c t)"), cb[:, :], 1.0, xc[:, :], ALU.add, ALU.mult).then_inc(mixb_done, 1)
                for m in range(4):
                    name = f"su{m}"
                    full(dve, l, name)
                    s = S0[:, m, :, :].rearrange("p b e -> p (b e)")
                    free(STT(s, s, C("gst")[:, m:m + 1], bank(name), ALU.mult, ALU.add), name)
                turned_out(2)

                for t in range(2):
                    for h in range(2):
                        name = f"w{t}{h}"
                        full(dve, l, name)
                        s = x[:, t, 512 * h:512 * h + 512]
                        free(T(s, s, bank(name), ALU.add), name)
                        if (t, h) == (0, 1):
                            scaled(l, 1, 0)
                        if (t, h) == (1, 0):
                            turned(l, 1, 0)
                scaled(l, 1, 1)
                full(dve, l, "w2")
                for q in range(4):
                    s = x[0:32, 2, 256 * q:256 * q + 256]
                    i = T(s, s, bank("w2")[32 * q:32 * q + 32, 0:256], ALU.add)
                    free(i, "w2") if q == 3 else own(i)
                turned(l, 1, 1)
                scaled(l, 1, 2)
                turned(l, 1, 2)

                full(dve, l, "lg")
                lg = bank("lg")[:, 0:3 * (NG + NE)].rearrange("p (t e) -> p t e", t=3)
                G = lg[:, :, 0:NG]
                do(dve.tensor_reduce(r_gm[:, :], G, AX, ALU.max))
                gm3 = bc(r_gm[:, :].unsqueeze(2), [128, 3, NG])
                T(r_ex[:, :, :], G, gm3, ALU.subtract).then_inc(lg_arg, 1)
                do(T(r_oh[:, :, :], G, gm3, ALU.is_equal))
                do(T(r_oh[:, :, :], r_oh[:, :, :], bc(C("desc").unsqueeze(1), [128, 3, NG]), ALU.mult))
                do(dve.tensor_reduce(r_gm[:, :], r_oh[:, :, :], AX, ALU.max))
                do(T(r_oh[:, :, :], r_oh[:, :, :], gm3, ALU.is_equal))
                E3 = lg[:, :, NG:].rearrange("p t (g e) -> p t g e", g=NG)
                M3 = masked.rearrange("p t (g e) -> p t g e", g=NG)
                do(S(r_oh[:, :, :], r_oh[:, :, :], -1.0, BIG, ALU.add, ALU.mult))
                free(T(M3, E3, bc(r_oh[:, :, :].unsqueeze(3), [128, 3, NG, EPG]), ALU.add), "lg")
                freed(dve, l, "lg")
                for t in range(3):
                    own(dve.max(r_top[:, t, :], masked[:, t, :]))
                own.wait()
                T(r_e2[:, :], r_top[:, :, 1], r_top[:, :, 0], ALU.subtract).then_inc(e2_arg, 1)
                for t in range(3):
                    own(dve.max_index(r_idx[:, t, :], r_top[:, t, :], masked[:, t, :]))
                own.wait()
                do(dve.tensor_copy(r_if[:, :, :], r_idx[:, :, 0:2]))
                for k in range(2):
                    own(T(onehot[:, :, k, :], bc(C("iota")[:, 0:NE].unsqueeze(1), [128, 3, NE]), bc(r_if[:, :, k].unsqueeze(2), [128, 3, NE]), ALU.is_equal))
                own.wait()
                T(osumb[:, :, :], onehot[:, :, 0, :], onehot[:, :, 1, :], ALU.add).then_inc(osum_ready, 1)
                dve.wait_ge(lg_exp, l + 1)
                do(dve.tensor_reduce(r_pt[:, :], r_ex[:, :, :], AX, ALU.add))
                do(dve.reciprocal(r_pt[:, :], r_pt[:, :]))
                dve.wait_ge(e2_ready, l + 1)
                do(S(r_gm[:, :], r_e2[:, :], 1.0, None, ALU.add))
                do(dve.reciprocal(r_gm[:, :], r_gm[:, :]))
                do(T(gate[:, :, 0], r_gm[:, :], r_pt[:, :], ALU.mult))
                own(T(gate[:, :, 1], gate[:, :, 0], r_e2[:, :], ALU.mult))
                full(dve, l, "cum")
                cum = bank("cum")[:, 0:128].rearrange("p (t e) -> p t e", t=4)
                cmp_ = ovcmp[:, 0:128].rearrange("p (e j) -> p e j", j=4)
                own(dve.memset(ov[:, 3, :], 0.0))
                do(T(cmp_, bc(cum[:, 3, :].unsqueeze(2), [128, NE, 4]), bc(C("thr").unsqueeze(1), [128, NE, 4]), ALU.is_gt))
                do(dve.tensor_reduce(ov[:, 0, :], cmp_, AX, ALU.add))
                do(dve.tensor_tensor_scan(ov[:, 1, :], ov[:, 0, :], ov[:, 3, :], 0.0, ALU.add, ALU.add))
                do(T(ov[:, 2, :], ov[:, 1, :], ov[:, 0, :], ALU.subtract))
                do(STT(ov[:, 2, :], ov[:, 2, :], float(SLOTS), C("ovc"), ALU.mult, ALU.add))
                do(S(ge, cum[:, 0:3, :], float(SLOTS), None, ALU.is_ge))
                do(T(ge, ge, bc(ov[:, 2:3, :], [128, 3, NE]), ALU.mult))
                free(T(bsum, cum[:, 0:3, :], bc(C("first")[:, 0:NE].unsqueeze(1), [128, 3, NE]), ALU.add), "cum")
                freed(dve, l, "cum")
                do(T(bsum, bsum, ge, ALU.add))
                for k in range(2):
                    own(T(rtmp[:, :, k, :], onehot[:, :, k, :], bsum, ALU.mult))
                own.wait()
                do(dve.tensor_reduce(slot[:, :, :], rtmp, AX, ALU.add))
                do(dve.tensor_copy(slotu[:, :, :], slot[:, :, :]))
                do(S(slotu[:, :, :], slotu[:, :, :], SLOTS - 1, None, ALU.bitwise_and))
                do(dve.tensor_copy(slot_in[:, :, :], slotu[:, :, :]))
                dve.sem_inc(slot_ready, 1)
                do(T(slot_blk[:, :, :], slot[:, :, :], slot_in[:, :, :], ALU.subtract))
                for t, (o, n) in enumerate(TILES):
                    for k in range(2):
                        for v_, what in enumerate((C("vals", n)[:, 2 * t + k:2 * t + k + 1], gate[0:n, t, k:k + 1])):
                            i = S(blk_oh[0:n, t, k, v_, :], C("first", n), slot_blk[0:n, t, k:k + 1], what, ALU.is_equal, ALU.mult)
                            if not (k and v_):
                                own(i)
                    i.then_inc(mark_ready, 1)
                cmp8 = ovcmp.rearrange("p (j e) -> p j e", j=OVER)
                do(T(cmp8, bc(ov[:, 1:2, :], [128, OVER, NE]), bc(C("iotaj").unsqueeze(2), [128, OVER, NE]), ALU.is_le))
                do(dve.tensor_reduce(ov[:, 0, 0:OVER], cmp8, AX, ALU.add))
                own(S(ovi[:, 0:OVER], ov[:, 0, 0:OVER], float(NE - 1), None, ALU.min))
                own(dve.tensor_copy(ovi[:, 8:9], ov[:, 1, NE - 1:NE]))
                full(dve, l, "tab")
                tab = bank("tab")[:, 0:2 * NBLK].rearrange("p (v b) -> p v b", v=2)
                by_pair = tab[:, :, 0:NE].rearrange("p v (g i) -> p v g i", i=2)
                for i in range(2):
                    h = slice(64 * i, 64 * i + 64)
                    own(dve.tensor_copy(sel[h, :, 0:NPAIR], by_pair[h, :, :, i]))
                free(dve.tensor_copy(sel[:, :, NPAIR:], tab[:, :, NE:NBLK]), "tab")
                freed(dve, l, "tab")
                own.wait()
                do(S(selu[:, :], sel[:, 0, :], float(OUTSIDE), None, ALU.add))
                S(gidx[:, :], selu[:, :], 1, None, ALU.logical_shift_right).then_inc(idx_ready, 1)
                dve.wait_ge(idx_ready, l + 1)
                do(dve.tensor_copy(tok[:, 0, :], gidx[:, :]))
                for t in (1, 2):
                    own(S(tok[:, t, :], tok[:, 0, :], float(-128 * t), None, ALU.add))
                own.wait()
                dve.sem_inc(tok_ready, 1)

                g3 = bc(gff[:, l, :].unsqueeze(2), [128, KT, 128])

                def tokens(g2, it):
                    for n_, (kind, k0) in enumerate((("x0", 0), ("x1", 4))):
                        b, n = expert_job(kind, g2, it, l)
                        dve.wait_ge(bank_full[b], n + 1)
                        T(xsT[:, g2 % 2, k0:k0 + 4, :], psum[:, b, :].rearrange("p (k s) -> p k s", k=4), g3[:, k0:k0 + 4, :],
                          ALU.mult).then_inc(bank_free[b], 1)

                def hidden(u, it):
                    b, n = expert_job("hT", u, it, l)
                    p = psum[:, b, 0:256].rearrange("p (f j s) -> p f j s", f=2, j=2)
                    dve.wait_ge(th_ready, l * NE + 4 * it + u + 1)
                    STT(tm, th, 1.0, p[:, :, 0, :], ALU.add, ALU.mult).then_inc(tm_ready, 1)
                    dve.wait_ge(tm_ready, l * NE + 4 * it + u + 1)
                    STT(hT[:, u % 2], tm, 0.5, p[:, :, 1, :], ALU.mult, ALU.mult).then_inc(bank_free[b], 1)

                def given_back(pair, it, parts):
                    for a in parts:
                        b, n = expert_job(f"back{a}", pair, it, l)
                        dve.wait_ge(bank_full[b], n + 1)
                        if a < 4:
                            s = x[:, a // 2, 512 * (a % 2):512 * (a % 2) + 512]
                            i = T(s, s, psum[:, b, :], ALU.add)
                        else:
                            for j in range(2):
                                s = x[0:32, 2, 512 * j:512 * j + 512]
                                i = T(s, s, psum[32 * j:32 * j + 32, b, :], ALU.add)
                        i.then_inc(bank_free[b], 1)

                def experts4(it, first=False, last=False):
                    for pair in range(2):
                        before = (0, it) if pair else (1, it - 1)
                        if pair or not first:
                            given_back(*before, (0, 1))
                        hidden(2 * pair, it)
                        if pair or not first:
                            given_back(*before, (2, 3))
                        hidden(2 * pair + 1, it)
                        if pair or not first:
                            given_back(*before, (4,))
                        if not (pair and last):
                            tokens(pair + 1, it)

                dve.wait_ge(st_out, 128 * (l + 1))
                tokens(0, 0)
                experts4(0, first=True)
                with dve.Fori(1, GROUPS - 1) as it:
                    experts4(it)
                experts4(GROUPS - 1, last=True)
                given_back(1, GROUPS - 1, (0, 1, 2, 3, 4))

                o = O[l]
                n = dve.value_load(ovi[0:1, 8:9], min_val=0, max_val=OVER)
                for a in range(3, 5):
                    xfreed(dve, f"back{a}", 1, GROUPS - 1, l)
                with dve.If(n > 0):
                    with dve.Fori(0, n) as j:
                        dve.tensor_copy(ovg[:, :], gidx[:, bass.ds(j + NPAIR, 1)]).then_inc(o["idx"], 1)
                        for t in range(3):
                            dve.tensor_copy(ovt[:, t:t + 1], tok[:, t, bass.ds(j + NPAIR, 1)]).then_inc(o["idx"], 1)
                        dve.tensor_copy(ovt[:, 3:4], sel[:, 1, bass.ds(j + NPAIR, 1)]).then_inc(o["idx"], 1)
                        dve.wait_ge(o["idx"], 5 * j + 5)
                        for t, (o_, n_) in enumerate(TILES):
                            i = S(back[:, 0, o_:o_ + n_], C("iota")[:, 0:n_], ovt[:, t:t + 1], ovt[:, 3:4], ALU.is_equal, ALU.mult)
                        i.then_inc(o["back"], 1)
                        dve.wait_ge(o["xT"], j + 1)
                        T(xsT[:, 0, :, 0:SLOTS], psum[:, 0, :].rearrange("p (k s) -> p k s", k=KT), g3[:, :, 0:SLOTS],
                          ALU.mult).then_inc(o["xTe"], 1)
                        p = psum[:, 3, 0:256].rearrange("p (f j s) -> p f j s", f=2, j=2)
                        dve.wait_ge(o["th"], j + 1)
                        STT(tm, th, 1.0, p[:, :, 0, :], ALU.add, ALU.mult).then_inc(o["tm"], 1)
                        dve.wait_ge(o["tm"], j + 1)
                        STT(hT[:, 0], tm, 0.5, p[:, :, 1, :], ALU.mult, ALU.mult).then_inc(o["hTe"], 1)
                        dve.wait_ge(o["y"], j + 1)
                        dve.tensor_copy(ysb[0:SLOTS, :].rearrange("p (q n) -> p q n", q=2), psum[0:SLOTS, 4:6, :]).then_inc(o["ye"], 1)
                        dve.wait_ge(o["acc"], j + 1)
                        for t, (o_, n_) in enumerate(TILES):
                            b = (6, 0, 2)[t]
                            s = x[0:n_, t, :].rearrange("p (q n) -> p q n", q=2)
                            i = T(s, s, psum[0:n_, b:b + 2, :], ALU.add)
                        i.then_inc(o["done"], 1)
                        dve.wait_ge(o["done"], j + 1)
                with dve.Else():
                    dve.nop()

            dve.wait_ge(gfin_in, 16)
            for t, (o, n) in enumerate(TILES):
                dve.wait_ge(rms_ready, 6 * DEPTH + t + 1)
                do(dve.reciprocal(rec[0:n, t:t + 1], rms[0:n, t:t + 1]))
                STT(x[0:n, t, :], x[0:n, t, :], rec[0:n, t:t + 1], gfin[0:n, :], ALU.mult, ALU.mult).then_inc(rows_ready, 1)

        @block.scalar
        def _(act):
            own = Own(act, own_act)

            def do(i):
                own(i)
                own.wait()

            A = act.activation

            act.dma_start(gmx[:, :, :], g_mix.rearrange("l (p k) -> p l k", k=KT)).then_inc(g_in, 16)
            act.dma_start(gff[:, :, :], g_ffn.rearrange("l (p k) -> p l k", k=KT)).then_inc(g_in, 16)
            act.dma_start(lbias[0:NG, :], b_grp.rearrange("l g -> g l"), allow_slow_non_contiguous=True).then_inc(g_in, 16)
            act.dma_start(lbias[NG:, :], b_exp.rearrange("l g -> g l"), allow_slow_non_contiguous=True).then_inc(g_in, 16)

            def mean_square(t):
                n = TILES[t][1]
                do(A(ttf[0:n, :], x[0:n, t, :], ACT.Square, accum_out=ssq[0:n, t:t + 1]))
                A(rms[0:n, t:t + 1], ssq[0:n, t:t + 1], ACT.Sqrt, bias=eps[0:n, :], scale=1.0 / D).then_inc(rms_ready, 1)

            def load_root(n):
                A(root[:, :], eps[:, :], ACT.Sqrt).then_inc(root_in, 1)
                act.wait_ge(root_in, n)

            def experts_done(l, t):
                for a in ((0, 1), (2, 3), (4,))[t]:
                    xfreed(act, f"back{a}", 1, GROUPS - 1, l)

            act.wait_ge(eps_ready, 1)
            load_root(1)
            for l in range(DEPTH):
                for t in range(3):
                    if l:
                        experts_done(l - 1, t)
                    else:
                        act.wait_ge(x_in[t], 16)
                    mean_square(t)
                for c in range(2):
                    full(act, l, f"b{c}")
                    free(A(AG[:, NT * c:NT * c + NT], bank(f"b{c}")[:, 0:NT], ACT.Copy), f"b{c}")
                for c in range(2):
                    name = f"b{2 + c}"
                    b = bank(name)
                    full(act, l, name)
                    own(A(axp[:, c, 3:LA], b[:, 0:SEQ], ACT.Copy))
                    free(A(axs[:, c, :, 3:LS], b[:, SEQ:NT].rearrange("p (b t) -> p b t", b=NB), ACT.Copy), name)
                if l == 0:
                    act.dma_start(s_conv[:, :, 0:CONV_B - 1 - DT, :], st_conv[:, :, DT:, :]).then_inc(past_out, 16)
                    z, az, u, w = (sp_t[:, 4 * i:4 * i + 4].rearrange("p (l c) -> p l c", l=2) for i in range(4))
                    act.wait_ge(prm_ready, 1)
                    A(u, az, ACT.Exp, scale=-1.0).then_inc(u_lam, 1)
                    act.wait_ge(la_ready, 1)
                    A(az, w, ACT.Ln).then_inc(u_lam, 1)
                for c in range(2):
                    name = f"b{4 + c}"
                    full(act, l, name)
                    free(A(cb[:, NT * c:NT * c + NT], bank(name)[:, 0:NT], ACT.Copy, scale=0.5), name)
                for c in range(2):
                    name = f"b{6 + c}"
                    full(act, l, name)
                    free(A(xc[:, NT * c:NT * c + NT], bank(name)[:, 0:NT], ACT.Tanh, scale=0.5), name)

                def gate(name, dst, bias, c):
                    full(act, l, name)
                    free(A(dst[:, NT * c:NT * c + NT], bank(name)[:, 0:NT], ACT.Tanh, bias=P_(l, bias, c), scale=0.5), name)

                def turned(name, t):
                    o, n = TILES[t]
                    dst = qT if name[1] == "q" else kT
                    full(act, l, name)
                    free(A(dst[:, :, o:o + n], bank(name)[:, 0:4 * n].rearrange("p (m t) -> p m t", m=4), ACT.Copy), name)

                def values(t):
                    name = f"v{t}"
                    full(act, l, name)
                    free(A(v[:, t, :], bank(name), ACT.Copy), name)

                def gate_tanh(t):
                    full(act, l, f"g{t}")
                    A(sg[:, t, :], bank(f"g{t}"), ACT.Tanh, scale=0.5).then_inc(sg_tanh, 1)

                if l:
                    act.wait_ge(count_read, l)
                full(act, l, "s2")
                b = bank("s2")
                own(A(v[0:32, 2, :], b[64:96, :], ACT.Copy))
                A(sg[0:32, 2, :], b[96:128, :], ACT.Tanh, scale=0.5).then_inc(sg_tanh, 1)
                gate("gr0", RG, "ba", 0)
                gate("gi0", IG, "bx", 0)
                gate("gr1", RG, "ba", 1)
                gate("gi1", IG, "bx", 1)
                turned("tq0", 0)
                turned("tk0", 0)
                if l + 1 < DEPTH:
                    load_gates(act, l + 1)
                act.wait_ge(gelu_arg, l + 1)
                m0 = mixT[:, 0:2, :].rearrange("p c t -> p (c t)")
                A(m0, m0, ACT.Tanh, scale=0.7978845608028654).then_inc(gelu_ready, 1)
                turned("tq2", 2)
                turned("tk2", 2)
                act.wait_ge(la_ready, l + 2)
                own(A(spr(As), pr(RG), ACT.Exp, scale=2.0))
                for c in range(2):
                    own(A(ssa(As)[:, c, :, 1:5], sa(RG)[:, c], ACT.Exp, scale=2.0))
                own(A(RI, RG, ACT.Exp, scale=4.0))
                own.wait()
                A(RG, RG, ACT.Tanh, scale=2.0).then_inc(tau_ready, 1)
                full(act, l, "st")
                act.wait_ge(sample_conv, l + 1)
                A(so[:, :, :], bank("st")[0:64, :].rearrange("p (c n) -> p c n", c=4), ACT.Copy).then_inc(bank_free[BANK["st"][0]], 1)
                act.wait_ge(var_a, l + 1)
                act.wait_ge(ixa_ready, l + 1)
                A(XA, RI, ACT.Sqrt, scale=-0.25).then_inc(sqrt_tau, 1)
                values(0)
                turned("tq1", 1)
                turned("tk1", 1)
                freed(act, l, "st")
                act.dma_start(o_lru_conv[l, 0].rearrange("k (c n) -> k c n", c=2), so[29:32, 0:2, :]).then_inc(conv_out, 16)
                act.dma_start(o_conv[l, 0].rearrange("k (c n) -> k c n", c=2), so[2:32, 2:4, :]).then_inc(conv_out, 16)
                for t in range(DT):
                    s = slice(32 + NB * t, 32 + NB * t + NB)
                    if t:
                        act.dma_start(s_lru_conv[l, :, t - 1].rearrange("b (c n) -> b c n", c=2), so[s, 0:2, :]).then_inc(conv_out, 16)
                    act.dma_start(s_conv[l, :, CONV_B - 1 - DT + t].rearrange("b (c n) -> b c n", c=2), so[s, 2:4, :]).then_inc(conv_out, 16)
                values(1)
                act.wait_ge(mixa_done, l + 1)
                for q in range(2):
                    for m in range(4):
                        act.dma_start(S0[64 * q:64 * q + 64, m, :, :],
                                      st_ret[l, :, 2 * m + q].rearrange("b d e -> d b e")).then_inc(s0_in, 16)

                def group_std(t):
                    H = NH if t < 2 else 2
                    act.wait_ge(var_ready, 3 * l + t + 1)
                    A(st_va[:, 0:H], st_va[:, 0:H], ACT.Sqrt, bias=eps[:, :], scale=1.0 / HD).then_inc(gstd_ready, 1)

                group_std(0)
                gate_tanh(0)
                freed(act, l, "lnm")
                A(cb[:, :], xc[:, :], ACT.Square).then_inc(ln_sq, 1)
                group_std(1)
                full(act, l, "lnv")
                free(A(rs[:, :], bank("lnv")[:, 0:NT], ACT.Sqrt, bias=eps[:, :]), "lnv")
                group_std(2)
                gate_tanh(1)
                full(act, l, "ht")
                free(A(ho[:, :, :], bank("ht")[0:9, 0:256].rearrange("p (c n) -> p c n", c=2), ACT.Copy), "ht")
                freed(act, l, "ht")
                act.dma_start(o_lru_h[l], ho[0:1, :, :].rearrange("p c n -> p (c n)")).then_inc(conv_out, 16)
                act.dma_start(s_lru_h[l], ho[1:9, :, :].rearrange("p c n -> p (c n)")).then_inc(conv_out, 16)
                act.wait_ge(ln_arg, 2 * l + 2)
                A(cb[:, :], xc[:, :], ACT.Tanh).then_inc(ln_tanh, 1)
                freed(act, l, "S1")
                for q in range(2):
                    act.dma_start(o_ret[l, 0].rearrange("(m q) d e -> q d m e", q=2)[q], S1[64 * q:64 * q + 64, :, :]).then_inc(ret_out, 16)
                act.wait_ge(os_norm, l + 1)
                for m in range(4):
                    i = A(tt[0:32, 0, 128 * m:128 * m + 128], osm[32 * m:32 * m + 32, :, :].rearrange("p q e -> p (q e)"), ACT.Copy)
                    i.then_inc(os_packed, 1) if m == 3 else own(i)
                freed(act, l, "su3")
                for q in range(2):
                    for m in range(4):
                        act.dma_start(s_ret[l, :, 2 * m + q].rearrange("b d e -> d b e"), S0[64 * q:64 * q + 64, m, :, :]).then_inc(st_out, 16)
                if l + 1 < DEPTH:
                    act.wait_ge(mixb_done, l + 1)
                    full(act, l, "w00")
                    load_states(act, l + 1)

                def store_rows(t):
                    o, n = TILES[t]
                    act.wait_ge(rows_ready, 6 * l + 3 + t + 1)
                    act.dma_start(xn_dram[o:o + n, :], rows[0:n, t % 2, :]).then_inc(xn_out[t], 16)

                for t in range(3):
                    for name in (("w00", "w01"), ("w10", "w11"), ("w2",))[t]:
                        freed(act, l, name)
                    mean_square(t)
                    if t:
                        store_rows(t - 1)
                store_rows(2)
                full(act, l, "lgT")
                free(A(lgT, bank("lgT")[0:NG + NE, 0:NT], ACT.Identity, bias=lbias[:, l:l + 1]), "lgT")
                if l + 1 < DEPTH:
                    load_router(act, l + 1)
                act.wait_ge(lg_arg, l + 1)
                A(r_ex[:, :, :], r_ex[:, :, :], ACT.Exp).then_inc(lg_exp, 1)
                act.wait_ge(e2_arg, l + 1)
                A(r_e2[:, :], r_e2[:, :], ACT.Exp).then_inc(e2_ready, 1)
                def results(pair, it):
                    for j in range(2):
                        b, n = expert_job(f"y{j}", pair, it, l)
                        act.wait_ge(bank_full[b], n + 1)
                        A(ysb[:, 512 * j:512 * j + 512], psum[:, b, :], ACT.Copy).then_inc(bank_free[b], 1)

                def experts4(it, first=False):
                    for pair in range(2):
                        for u in (2 * pair, 2 * pair + 1):
                            b, n = expert_job("h", u, it, l)
                            act.wait_ge(bank_full[b], n + 1)
                            A(hsb[:, u % 2, :], psum[:, b, 0:256], ACT.Copy).then_inc(bank_free[b], 1)
                            if not (first and u == 0):
                                xfreed(act, "hT", (u - 1) % 4, it if u else it - 1, l)
                            b, n = expert_job("hT", u, it, l)
                            act.wait_ge(bank_full[b], n + 1)
                            A(th, psum[:, b, 0:256].rearrange("p (f j s) -> p f j s", f=2, j=2)[:, :, 0, :], ACT.Tanh, scale=0.5).then_inc(th_ready, 1)
                        if pair or not first:
                            xfull(act, "back4", 1 - pair, it if pair else it - 1, l)
                        results(pair, it)

                act.wait_ge(conv_out, 16 * 11 * (l + 1))
                experts4(0, first=True)
                with act.Fori(1, GROUPS) as it:
                    experts4(it)

                o = O[l]
                act.wait_ge(idx_ready, l + 1)
                n = act.value_load(ovi[0:1, 8:9], min_val=0, max_val=OVER)
                xfreed(act, "hT", 3, GROUPS - 1, l)
                with act.If(n > 0):
                    with act.Fori(0, n) as j:
                        act.wait_ge(o["h"], j + 1)
                        A(hsb[:, 0, :], psum[:, 2, 0:256], ACT.Copy).then_inc(o["he"], 1)
                        act.wait_ge(o["hT"], j + 1)
                        A(th, psum[:, 3, 0:256].rearrange("p (f j s) -> p f j s", f=2, j=2)[:, :, 0, :], ACT.Tanh, scale=0.5).then_inc(o["th"], 1)
                        act.wait_ge(o["done"], j + 1)
                with act.Else():
                    act.nop()
                load_root(l + 2)

            for t in range(3):
                experts_done(DEPTH - 1, t)
                mean_square(t)
            act.wait_ge(conv_out, 16 * 11 * DEPTH)
            act.wait_ge(past_out, 16)
            act.wait_ge(ret_out, 32 * DEPTH)
            act.wait_ge(st_out, 128 * DEPTH)

        @block.gpsimd
        def _(pool):
            own = Own(pool, own_pool)
            pool.memset(bd[:, :, :, :], 0.0).then_inc(bd_zero, 1)
            T = pool.tensor_tensor
            for l in range(DEPTH):
                freed(pool, l, "b1")
                m0 = mixT[:, 0:2, :].rearrange("p c t -> p (c t)")
                own(T(m0, AG, AG, ALU.mult))
                own.wait()
                own(pool.tensor_scalar(m0, m0, 0.044715, 1.0, ALU.mult, ALU.add))
                own.wait()
                T(m0, m0, AG, ALU.mult).then_inc(gelu_arg, 1)
                if l:
                    pool.wait_ge(ret_out, 32 * l)
                freed(pool, l, "b3")
                dve_done = 2 * l + 2
                own(pool.tensor_copy(stg[:, 0:2, 0:32], axp[:, :, LA - 32:LA]))
                for c in range(2):
                    own(pool.tensor_copy(stg[:, c, 32:64].rearrange("p (t b) -> p b t", b=NB), axs[:, c, :, 3:LS]))
                pool.wait_ge(glu_ready, dve_done)
                own(pool.tensor_copy(stg[:, 2:4, 0:32], glp[:, :, LB - 32:LB]))
                own(pool.tensor_copy(stg[:, 2, 32:64].rearrange("p (t b) -> p b t", b=NB), gls[:, 0, :, 30:LT]))
                pool.tensor_copy(stg[:, 3, 32:64].rearrange("p (t b) -> p b t", b=NB), gls[:, 1, :, 30:LT]).then_inc(stage_ready, 1)
                for t in (0, 2, 1):
                    n = TILES[t][1]
                    full(pool, l, f"tk{t}")
                    k3 = kr[0:n, t, :].rearrange("p (h e) -> p h e", h=NH)
                    T(k3, k3, bc(C("zeta" if t < 2 else "zetas", n).unsqueeze(2), [n, NH, HD]), ALU.mult).then_inc(kz_ready, 1)
                full(pool, l, "o0")
                full(pool, l, "o1")
                vm = bc(C("vmask", 32).unsqueeze(2), [32, NB, HD])
                for m in range(4):
                    if m > 1:
                        full(pool, l, f"su{m - 2}")
                    for q in range(2):
                        h = 64 * (2 * m + q)
                        i = T(Vx[:, m % 2, q, :, :], bc(v[0:32, 2, h:h + 64].unsqueeze(1), [32, NB, HD]), vm, ALU.mult)
                        i.then_inc(vx_ready, 1) if q else own(i)

                pool.wait_ge(slot_ready, l + 1)
                for t, (o, n) in enumerate(TILES):
                    for k in range(2):
                        i = pool.tensor_scalar(slot_oh[0:n, t, k, :].rearrange("p (i s) -> p i s", i=2), bc(C("iota", n)[:, 0:SLOTS].unsqueeze(1), [n, 2, SLOTS]),
                              slot_in[0:n, t, k:k + 1], None, ALU.is_equal)
                        i.then_inc(slot_marked, 1) if k else own(i)
                pool.wait_ge(idx_ready, l + 1)
                for t in range(3):
                    pool.wait_ge(xn_out[t], 16 * (l + 1))

                def gather(g):
                    if g > 1:
                        xfull(pool, "x1", g % 2, (g - 2) // 2, l)
                    else:
                        full(pool, l, "n2t2a")
                    pool.indirect_dma_start(out=rows[:, g % 2, :], out_offset=None, in_=xn_dram,
                                            in_offset=bass.IndirectOffsetOnAxis(ap=gidx[:, g:g + 1], axis=0),
                                            bounds_check=NT - 1, oob_is_err=False).then_inc(gath[g % 2], 16)

                def way_back(g):
                    if g > 1:
                        xfull(pool, "back4", g % 2, (g - 2) // 2, l)
                    for t, (o, n) in enumerate(TILES):
                        i = pool.tensor_scalar(back[:, g % 2, o:o + n], C("iota")[:, 0:n], tok[:, t, g:g + 1], sel[:, 1, g:g + 1], ALU.is_equal, ALU.mult)
                        i.then_inc(back_ready, 1) if t == 2 else own(i)

                gather(0)
                for g in range(NPAIR):
                    if g + 1 < NPAIR:
                        gather(g + 1)
                    if g == 0:
                        pool.wait_ge(tok_ready, l + 1)
                    way_back(g)

                o = O[l]
                n = pool.value_load(ovi[0:1, 8:9], min_val=0, max_val=OVER)
                xfull(pool, "x1", 1, GROUPS - 1, l)
                with pool.If(n > 0):
                    with pool.Fori(0, n) as j:
                        pool.wait_ge(o["idx"], 5 * j + 5)
                        pool.sem_inc(o["seen"], 1)
                        pool.indirect_dma_start(out=rows[0:SLOTS, 0, :], out_offset=None, in_=xn_dram,
                                                in_offset=bass.IndirectOffsetOnAxis(ap=ovg[0:SLOTS, :], axis=0),
                                                bounds_check=NT - 1, oob_is_err=False).then_inc(o["gath"], 16)
                with pool.Else():
                    pool.nop()
                pool.sem_inc(count_read, 1)


_INS = ["x_prompt", "x_sample", "state_lru_h", "state_lru_conv", "state_conv", "state_ret", "norm_mix_g",
        "norm_ffn_g", "final_norm_g", "w_in", "lru_conv_w", "lru_conv_b", "lru_wa", "lru_ba", "lru_wx",
        "lru_bx", "lru_lambda", "cm_dw_w", "cm_dw_b", "cm_ln_g", "cm_ln_b", "ret_norm_g", "w_out",
        "moe_w_group", "moe_b_group", "moe_w_expert", "moe_b_expert", "moe_w1", "moe_w3", "moe_w2"]
_OUTS = [(1, SEQ, D), (NB, DT, D)] + OUTS[2:]


def kernel(**inputs):
    import concourse.bacc as bacc
    from concourse.bass_utils import run_bass_kernel_spmd

    nc = bacc.Bacc("TRN2", target_bir_lowering=False, num_devices=1)
    arrays, ins = {}, []
    for name, a in [(n, np.ascontiguousarray(inputs[n])) for n in _INS] + [("constants", constants())]:
        arrays[f"in_{name}"] = a
        ins.append(nc.dram_tensor(f"in_{name}", a.shape, mybir.dt.from_np(a.dtype), kind="ExternalInput").ap())
    outs = [nc.dram_tensor(f"out_{i}", s, F32, kind="ExternalOutput").ap() for i, s in enumerate(_OUTS)]
    build(nc, ins, outs)
    r = run_bass_kernel_spmd(nc, [arrays], core_ids=[0])
    return tuple(r.results[0][f"out_{i}"] for i in range(len(_OUTS)))
```
